# Optimizing a Trainium2 kernel written in Bass

```python
import math
import jax, jax.numpy as jnp
from jax import lax
import numpy as np

D_MODEL = 1024
BATCH = 1
SEQ = 256
DEPTH = 2

N_HEADS = 8
HEAD_DIM = 64
V_HEAD_DIM = 2 * HEAD_DIM
ATTN_QK_W = N_HEADS * 2 * HEAD_DIM
ATTN_V_W = N_HEADS * V_HEAD_DIM
Q_BLOCK = 128
CONV_W = 1024
CONV_K = 3
NUM_BUCKETS = 32
MAX_DISTANCE = 128
FF_DENSE = 2816
N_EXPERTS = 8
TOP_K = 2
FF_EXPERT = 3584
RMS_EPS = 1e-6
IN_W = 2 * ATTN_QK_W + ATTN_V_W + 3 * CONV_W + 2 * D_MODEL
N_DENSE_LAYERS = (DEPTH + 1) // 2
N_MOE_LAYERS = DEPTH // 2

kernel_name = "hybrid_diffattn_shortconv_moe_trunk"

def lambda_init_fn(layer_idx):
    return 0.8 - 0.6 * math.exp(-0.3 * layer_idx)

def rmsnorm(x, g):
    xf = x.astype(jnp.float32)
    y = xf * lax.rsqrt(jnp.mean(xf * xf, axis=-1, keepdims=True) + RMS_EPS)
    return (y * g.astype(jnp.float32)).astype(x.dtype)

def t5_causal_bucket(dist):
    max_exact = NUM_BUCKETS // 2
    is_small = dist < max_exact
    d = jnp.maximum(dist, 1).astype(jnp.float32)
    large = max_exact + (jnp.log(d / max_exact) / math.log(MAX_DISTANCE / max_exact)
                         * (NUM_BUCKETS - max_exact)).astype(jnp.int32)
    large = jnp.minimum(large, NUM_BUCKETS - 1)
    return jnp.where(is_small, dist, large)

def diff_attention(q, k, v, bias_dist, lam, lam_init, subln_g):
    B, S = q.shape[0], q.shape[1]
    nblk = S // Q_BLOCK
    scale = HEAD_DIM ** -0.5
    qb = q.reshape(B, nblk, Q_BLOCK, N_HEADS, 2, HEAD_DIM).swapaxes(0, 1)
    kf = k.astype(jnp.float32)
    vf = v.astype(jnp.float32)
    kpos = jnp.arange(S, dtype=jnp.int32)
    g = subln_g.astype(jnp.float32) * (1.0 - lam_init)

    def one_block(args):
        blk, qblk = args
        qpos = blk * Q_BLOCK + jnp.arange(Q_BLOCK, dtype=jnp.int32)
        dist = qpos[:, None] - kpos[None, :]
        bias = bias_dist[:, jnp.maximum(dist, 0)]
        s = jnp.einsum('bqhmd,bkhmd->bhmqk', qblk.astype(jnp.float32) * scale, kf)
        s = s + bias[None, :, None]
        s = jnp.where(dist >= 0, s, -jnp.inf)
        p = jax.nn.softmax(s, axis=-1)
        w = p[:, :, 0] - lam * p[:, :, 1]
        o = jnp.einsum('bhqk,bkhe->bqhe', w, vf)
        o = o * lax.rsqrt(jnp.mean(o * o, axis=-1, keepdims=True) + RMS_EPS) * g
        return o

    out = lax.map(one_block, (jnp.arange(nblk, dtype=jnp.int32), qb))
    return out.swapaxes(0, 1).reshape(B, S, ATTN_V_W).astype(q.dtype)

def short_gated_conv(h, gate_b, gate_c, conv_w):
    u = gate_c * h
    up = jnp.pad(u, ((0, 0), (CONV_K - 1, 0), (0, 0)))
    S = h.shape[1]
    y = conv_w[0] * up[:, 0:S] + conv_w[1] * up[:, 1:S + 1] + conv_w[2] * up[:, 2:S + 2]
    return gate_b * y

def swiglu(h, w_gu, w_down):
    gu = h @ w_gu
    g, u = jnp.split(gu, 2, axis=-1)
    return (jax.nn.silu(g) * u) @ w_down

def moe_swiglu(h, router_w, w_gu, w_down):
    B, S, D = h.shape
    xf = h.reshape(B * S, D)
    logits = (xf @ router_w).astype(jnp.float32)
    top_v, top_i = lax.top_k(logits, TOP_K)
    gates = jax.nn.softmax(top_v, axis=-1)
    cw = jnp.sum(jax.nn.one_hot(top_i, N_EXPERTS, dtype=jnp.float32) * gates[..., None], axis=1)
    cw = cw.astype(h.dtype)
    out = jnp.zeros_like(xf)
    for e in range(N_EXPERTS):
        out = out + cw[:, e:e + 1] * swiglu(xf, w_gu[e], w_down[e])
    return out.reshape(B, S, D)

def setup_inputs(seed: int = 0) -> dict:
    key = jax.random.key(seed)
    ks = jax.random.split(key, 17)
    f32 = jnp.float32
    nrm = lambda k, shape, s: (jax.random.normal(k, shape, f32) * s)
    x = jax.random.normal(ks[0], (BATCH, SEQ, D_MODEL), f32)
    rel_bias = nrm(ks[1], (NUM_BUCKETS, N_HEADS), 0.5)
    mix_norm_g = 1.0 + nrm(ks[2], (DEPTH, D_MODEL), 0.02)
    w_in = nrm(ks[3], (DEPTH, D_MODEL, IN_W), D_MODEL ** -0.5)
    lam_qk = nrm(ks[4], (DEPTH, 4, HEAD_DIM), 0.1)
    subln_g = 1.0 + nrm(ks[5], (DEPTH, V_HEAD_DIM), 0.02)
    conv_w = nrm(ks[6], (DEPTH, CONV_K, CONV_W), CONV_K ** -0.5)
    w_o_attn = nrm(ks[7], (DEPTH, ATTN_V_W, D_MODEL), ATTN_V_W ** -0.5)
    w_o_conv = nrm(ks[8], (DEPTH, CONV_W, D_MODEL), CONV_W ** -0.5)
    w_o = nrm(ks[9], (DEPTH, D_MODEL, D_MODEL), D_MODEL ** -0.5)
    ffn_norm_g = 1.0 + nrm(ks[10], (DEPTH, D_MODEL), 0.02)
    dense_w_gate_up = nrm(ks[11], (N_DENSE_LAYERS, D_MODEL, 2 * FF_DENSE), D_MODEL ** -0.5)
    dense_w_down = nrm(ks[12], (N_DENSE_LAYERS, FF_DENSE, D_MODEL), FF_DENSE ** -0.5)
    router_w = nrm(ks[13], (N_MOE_LAYERS, D_MODEL, N_EXPERTS), D_MODEL ** -0.5)
    expert_w_gate_up = nrm(ks[14], (N_MOE_LAYERS, N_EXPERTS, D_MODEL, 2 * FF_EXPERT), D_MODEL ** -0.5)
    expert_w_down = nrm(ks[15], (N_MOE_LAYERS, N_EXPERTS, FF_EXPERT, D_MODEL), FF_EXPERT ** -0.5)
    final_norm_g = 1.0 + nrm(ks[16], (D_MODEL,), 0.02)
    return {"x": x, "rel_bias": rel_bias, "mix_norm_g": mix_norm_g, "w_in": w_in,
            "lam_qk": lam_qk, "subln_g": subln_g, "conv_w": conv_w,
            "w_o_attn": w_o_attn, "w_o_conv": w_o_conv, "w_o": w_o,
            "ffn_norm_g": ffn_norm_g, "dense_w_gate_up": dense_w_gate_up,
            "dense_w_down": dense_w_down, "router_w": router_w,
            "expert_w_gate_up": expert_w_gate_up, "expert_w_down": expert_w_down,
            "final_norm_g": final_norm_g}

def reference(x, rel_bias, mix_norm_g, w_in, lam_qk, subln_g, conv_w, w_o_attn, w_o_conv, w_o,
              ffn_norm_g, dense_w_gate_up, dense_w_down, router_w, expert_w_gate_up,
              expert_w_down, final_norm_g):
    B, S, D = x.shape
    dists = jnp.arange(S, dtype=jnp.int32)
    bias_dist = rel_bias.astype(jnp.float32)[t5_causal_bucket(dists)].T
    offs = np.cumsum([ATTN_QK_W, ATTN_QK_W, ATTN_V_W, CONV_W, CONV_W, CONV_W, D_MODEL]).tolist()

    for l in range(DEPTH):
        h = rmsnorm(x, mix_norm_g[l])
        z = h @ w_in[l]
        q, k, v, ch, cb, cc, ga, gc = jnp.split(z, offs, axis=-1)
        q = q.reshape(B, S, N_HEADS, 2, HEAD_DIM)
        k = k.reshape(B, S, N_HEADS, 2, HEAD_DIM)
        v = v.reshape(B, S, N_HEADS, V_HEAD_DIM)
        lq = lam_qk[l].astype(jnp.float32)
        lam_init = lambda_init_fn(l)
        lam = jnp.exp(jnp.sum(lq[0] * lq[1])) - jnp.exp(jnp.sum(lq[2] * lq[3])) + lam_init
        a = diff_attention(q, k, v, bias_dist, lam, lam_init, subln_g[l])
        c = short_gated_conv(ch, cb, cc, conv_w[l])
        merged = jax.nn.sigmoid(ga) * (a @ w_o_attn[l]) + jax.nn.sigmoid(gc) * (c @ w_o_conv[l])
        x = x + merged @ w_o[l]
        h = rmsnorm(x, ffn_norm_g[l])
        if l % 2 == 0:
            f = swiglu(h, dense_w_gate_up[l // 2], dense_w_down[l // 2])
        else:
            f = moe_swiglu(h, router_w[l // 2], expert_w_gate_up[l // 2], expert_w_down[l // 2])
        x = x + f

    return rmsnorm(x, final_norm_g)


_drawn_inputs = setup_inputs


def setup_inputs(seed=0):
    import zlib

    import numpy as np

    out = dict(_drawn_inputs(seed))
    spreads = {}
    factors = {}
    for name, (base, spread) in spreads.items():
        noise = np.random.default_rng([zlib.crc32(name.encode()), seed]).standard_normal(out[name].shape)
        drawn = base * np.exp(spread * noise) if base else spread * noise
        out[name] = __import__('jax').numpy.asarray(drawn.astype(out[name].dtype))
    for name, factor in factors.items():
        out[name] = (out[name] * factor).astype(out[name].dtype)
    return out
```

```python
import math
from contextlib import ExitStack

import concourse.bass as bass
from concourse import mybir

P = 128
F32 = mybir.dt.float32
F32R = mybir.dt.float32r
I32 = mybir.dt.int32
ALU = mybir.AluOpType
ACT = mybir.ActivationFunctionType
AX = mybir.AxisListType.X

D = 1024
SEQ = 256
TT = SEQ // P
KC = D // P
HEADS = 8
HD = 64
NBUCKETS = 32
EPS = 1e-6
DEPTH = 2
FF = 2816
FE = 3584
EXPERTS = 8
CHUNK = 512
HALF = 2048
RAW = 6
SPLIT = 3
FFW = 256
FSTEPS = FF // FFW
MSTEPS = FE // CHUNK
SLOTS = 3
COLS = EXPERTS + SLOTS + 1
LINE = 384
BIG = 1e30

MIX_HALVES = 44
DENSE_HALVES = 3 * FSTEPS
BLOCK_HALVES = 6 * MSTEPS
CYCLES = BLOCK_HALVES // RAW
MIX0 = (0, MIX_HALVES + DENSE_HALVES)
DENSE0 = MIX_HALVES
MOE0 = 2 * MIX_HALVES + DENSE_HALVES

W_IN_COLS = [0, 512, 1024, 1536, 2048, 2560, 3072, 5120, 4096, 3584, 5632, 4608, 6144, 6656, 7168, 7680]
U_Q, U_V, U_GATE, U_OUT, U_WO = 0, 4, 12, 16, 20
UNITS = 22


def unit_of(s):
    return (s // 2, s % 2) if s < 40 else (20 + s % 2, (s - 40) // 2)


def last_half(u):
    return 2 * u + 1 if u < 20 else 42 + (u - 20)


def mixer_jobs():
    jobs = {s: [] for s in range(MIX_HALVES + 1)}
    for h in range(HEADS):
        a = 12 + (3 * h) // 2
        jobs[a].append(("scores", h))
        jobs[a + 1].append(("turn_w", h))
        jobs[a + 2].append(("values", h))
        jobs[a + 3].append(("turn_a", h))
    for s in jobs:
        jobs[s].sort(key=lambda j: ["scores", "turn_w", "values", "turn_a"].index(j[0]))
    for s, job in {2: ("turn_qk", 0), 4: ("turn_qk", 1), 6: ("turn_qk", 2), 8: ("turn_qk", 3),
                   16: ("turn_u", 0), 18: ("turn_b", 0), 22: ("turn_u", 1), 24: ("turn_b", 1),
                   36: ("turn_m", 0), 40: ("turn_m", 1)}.items():
        jobs[s].append(job)
    return jobs


JOBS = mixer_jobs()
JOB_BANKS = {"scores": (4, 5), "turn_w": (6,), "values": (7,), "turn_a": (6,),
             "turn_qk": (6, 7), "turn_u": (6, 7), "turn_b": (6, 7), "turn_m": (6, 7)}
TURNS_OF_ROWS = ("turn_qk", "turn_u", "turn_b")


def count_bank_uses():
    uses, last, at, before_it = {b: 0 for b in (4, 5, 6, 7)}, {}, {}, {}
    for s in range(MIX_HALVES):
        for job in JOBS[s]:
            for b in JOB_BANKS[job[0]]:
                uses[b] += 1
                at[job, b] = uses[b]
                before_it[job, b] = last.get(b)
                last[b] = job
    return at, before_it, uses, last


BANK_AT, JOB_BEFORE, BANK_USES, LAST_JOB = count_bank_uses()
ACT_ROWS = {(layer, u): 2 * (6 * layer + i + 1) for layer in range(DEPTH) for i, u in enumerate((0, 1, 2, 3, 8, 11))}
X_ADDS = {1: 4, 2: 8, 3: 12}


def lambda_init(layer):
    return 0.8 - 0.6 * math.exp(-0.3 * layer)


def build(nc, x, rel_bias, mix_norm_g, w_in, lam_qk, subln_g, conv_w, w_o_attn, w_o_conv, w_o,
          ffn_norm_g, dense_gu, dense_down, router_w, expert_gu, expert_down, final_norm_g,
          bucket_of, out):
    lines = nc.dram_tensor("bias_lines", (HEADS, P, LINE), F32, kind="Internal").ap()
    with ExitStack() as ctx:
        def sb(name, shape, dt=F32):
            return ctx.enter_context(nc.sbuf_tensor(name, shape, dt))

        def sem(name):
            return ctx.enter_context(nc.semaphore(name))

        w_raw = sb("w_raw", [P, RAW, HALF])
        w_hi = sb("w_hi", [P, SPLIT, HALF], F32R)
        w_lo = sb("w_lo", [P, SPLIT, HALF], F32R)
        X = sb("X", [P, TT, D])
        hT_hi = sb("hT_hi", [P, KC * SEQ], F32R)
        hT_lo = sb("hT_lo", [P, KC * SEQ], F32R)
        q_buf = sb("q_buf", [P, KC * SEQ])
        k_buf = sb("k_buf", [P, KC * SEQ])
        v_buf = sb("v_buf", [P, KC * SEQ])
        aT_hi = sb("aT_hi", [P, KC * SEQ], F32R)
        aT_lo = sb("aT_lo", [P, KC * SEQ], F32R)
        cT_hi = sb("cT_hi", [P, KC * SEQ], F32R)
        cT_lo = sb("cT_lo", [P, KC * SEQ], F32R)
        rows = sb("rows", [P, TT * CHUNK])
        part = sb("part", [P, TT * CHUNK])
        uT = sb("uT", [P, 4, SEQ + 2])
        yT = sb("yT", [P, KC * P])
        prob = sb("prob", [P, 2, LINE])
        wgt = sb("wgt", [P, LINE])
        wgtT = sb("wgtT", [P, LINE])
        arow = sb("arow", [P, TT, P])
        squares = sb("squares", [P, TT, P])
        bias = sb("bias", [P, HEADS, LINE])
        ident = sb("ident", [P, P])
        before = sb("before", [P, P])
        ones = sb("ones", [P, P])
        iota_j = sb("iota_j", [P, P])
        iota_e = sb("iota_e", [P, EXPERTS])
        zero_r = sb("zero_r", [P, CHUNK], F32R)
        relb = sb("relb", [64, HEADS])
        relb_bc = sb("relb_bc", [64, P])
        gsub = sb("gsub", [P, DEPTH, P])
        conv_rows = sb("conv_rows", [DEPTH * 3 * KC, P])
        convT = sb("convT", [P, DEPTH, 3, KC])
        lam4 = sb("lam4", [P, 2, DEPTH])
        neg_lam = sb("neg_lam", [P, DEPTH])
        nmax = sb("nmax", [P, 4])
        psum_row = sb("psum_row", [P, 4])
        recip = sb("recip", [P, 4])
        ssq = sb("ssq", [P, 2])
        nw = [sb(f"nw{i}", [P, 2]) for i in range(3)]
        nwi = sb("nwi", [P, 2], I32)
        rtr = sb("rtr", [P, KC * EXPERTS])
        rtr_hi = sb("rtr_hi", [P, KC * EXPERTS], F32R)
        rtr_lo = sb("rtr_lo", [P, KC * EXPERTS], F32R)
        rt = sb("rt", [P, 16, TT, EXPERTS])
        rs = sb("rs", [P, 12, TT])
        posb = sb("posb", [P, TT, COLS])
        cwb = sb("cwb", [P, TT, COLS])
        ctl = sb("ctl", [P, 4])
        ctl_i = sb("ctl_i", [P, 4], I32)
        pcol = sb("pcol", [P, TT])
        gcol = sb("gcol", [P, TT])
        gate = sb("gate", [P, 1])

        bank = [ctx.enter_context(nc.psum_tensor(f"bank{b}", [P, CHUNK], F32)) for b in range(8)]

        def k_tok(buf):
            return buf[:, :].rearrange("p (k t) -> p k t", t=SEQ)

        def tok_d(buf):
            return buf[:, :].rearrange("p (t d) -> p t d", t=TT)

        def tok_c(buf):
            return buf[:, :].rearrange("p (t c) -> p t c", t=TT)

        def quad(ap):
            return ap.rearrange("p (c n) -> p c n", n=P)

        hrow, merged = tok_d(q_buf), tok_d(q_buf)
        qT, kT = k_tok(q_buf), k_tok(k_buf)
        v_rows, sig_attn, sig_conv = tok_d(v_buf), tok_d(k_buf), tok_d(v_buf)
        gain = yT[:, :]
        yTv = yT[:, :].rearrange("p (c t) -> p c t", t=SEQ)
        lamq = rows[:, 0:DEPTH * 4 * HD].rearrange("p (l i d) -> p l i d", l=DEPTH, i=4)
        ffT_hi, ffT_lo = cT_hi[:, 0:CHUNK], cT_lo[:, 0:CHUNK]
        y_hi, y_lo = cT_hi[:, CHUNK:CHUNK + D], cT_lo[:, CHUNK:CHUNK + D]
        pick_r = cT_hi[:, 1536:1792].rearrange("p (t j) -> p t j", t=TT)
        spread_r = cT_hi[:, 1792:2048].rearrange("p (t j) -> p t j", t=TT)
        pick = prob[:, 0, 0:256].rearrange("p (t j) -> p t j", t=TT)
        xg_hi, xg_lo = hT_hi[:, 0:D], hT_lo[:, 0:D]
        hr_hi, hr_lo = tok_d(aT_hi), tok_d(aT_lo)

        x_in, relb_in, bucket_in, lam_in, sub_in, conv_in, rtr_in, gain_in = (
            sem(n) for n in ("x_in", "relb_in", "bucket_in", "lam_in", "sub_in", "conv_in", "rtr_in", "gain_in"))
        line_out, bias_in, out_sent = sem("line_out"), sem("bias_in"), sem("out_sent")
        landed = [sem(f"landed{i}") for i in range(RAW)]
        hi_ready, lo_ready, half_used = sem("hi_ready"), sem("lo_ready"), sem("half_used")
        bank_full = {b: sem(f"bank_full{b}") for b in (4, 5, 6, 7)}
        const_ready = sem("const_ready")
        conv_ps = sem("conv_ps")
        line_ps, line_sb, relb_ready = sem("line_ps"), sem("line_sb"), sem("relb_ready")
        lam_sums, lam_exp = sem("lam_sums"), sem("lam_exp")
        dve_step = sem("dve_step")
        pool_step = sem("pool_step")
        x_new = sem("x_new")
        ss_ready, hrow_ready, norm_ps = sem("ss_ready"), sem("hrow_ready"), sem("norm_ps")
        hT_hi_ready, hT_lo_ready = sem("hT_hi_ready"), sem("hT_lo_ready")
        act_rows, dve_rows = sem("act_rows"), sem("dve_rows")
        qk_ready, v_ready, ch_ready = sem("qk_ready"), sem("v_ready"), sem("ch_ready")
        biased, exp_ready, wgt_ready, wgtT_ready = sem("biased"), sem("exp_ready"), sem("wgt_ready"), sem("wgtT_ready")
        o_ss, arow_ready, aT_hi_ready, aT_lo_ready = sem("o_ss"), sem("arow_ready"), sem("aT_hi_ready"), sem("aT_lo_ready")
        merged_attn, merged_conv, merged_ready = sem("merged_attn"), sem("merged_conv"), sem("merged_ready")
        uT_ready, yT_ready, c_ready = sem("uT_ready"), sem("yT_ready"), sem("c_ready")
        cT_hi_ready, cT_lo_ready = sem("cT_hi_ready"), sem("cT_lo_ready")
        sig_ready, mT_hi_ready, mT_lo_ready = sem("sig_ready"), sem("mT_hi_ready"), sem("mT_lo_ready")
        d_silu, d_rows, d_turn, d_hi, d_lo = sem("d_silu"), sem("d_rows"), sem("d_turn"), sem("d_hi"), sem("d_lo")
        rtr_hi_ready, rtr_lo_ready, hr_hi_ready, hr_lo_ready = (
            sem("rtr_hi_ready"), sem("rtr_lo_ready"), sem("hr_hi_ready"), sem("hr_lo_ready"))
        logits_ps, gap_ready, gap_exp, mask_ready, place_ps = (
            sem("logits_ps"), sem("gap_ready"), sem("gap_exp"), sem("mask_ready"), sem("place_ps"))
        route_ready, moe_init = sem("route_ready"), sem("moe_init")
        e_silu, e_rows, e_turn, e_hi, e_lo = sem("e_silu"), sem("e_rows"), sem("e_turn"), sem("e_hi"), sem("e_lo")
        y_hi_ready, y_lo_ready, scatter_ps, x_add = sem("y_hi_ready"), sem("y_lo_ready"), sem("scatter_ps"), sem("x_add")
        pick_ready, spread_ps, spread_ready = sem("pick_ready"), sem("spread_ps"), sem("spread_ready")
        gather_ps, xg_act, xg_dve = sem("gather_ps"), sem("xg_act"), sem("xg_dve")
        col_ready, moe_step = sem("col_ready"), sem("moe_step")

        def load_half(sp, n, src, cyc=0):
            if n >= RAW:
                sp.wait_ge(lo_ready, n - RAW + 1 + RAW * cyc)
            dst = w_raw[:, n % RAW, :]
            sp.dma_start(dst.rearrange("p (a b) -> p a b", a=src.shape[1]), src).then_inc(landed[n % RAW], 16)

        def split_hi(act, n, cyc=0):
            act.wait_ge(landed[n % RAW], 16 * (n // RAW + 1) + 16 * cyc)
            if n >= SPLIT:
                act.wait_ge(half_used, n - SPLIT + 1 + RAW * cyc)
            act.activation(w_hi[:, n % SPLIT, :], w_raw[:, n % RAW, :], ACT.Copy).then_inc(hi_ready, 1)

        def split_lo(dve, n, cyc=0):
            dve.wait_ge(hi_ready, n + 1 + RAW * cyc)
            dve.tensor_tensor(w_lo[:, n % SPLIT, :], w_raw[:, n % RAW, :], w_hi[:, n % SPLIT, :],
                              ALU.subtract).then_inc(lo_ready, 1)

        def product(pe, dst, hi, lo, whi, wlo, first, last):
            pe.matmul(dst, hi, whi, start=first, stop=False, skip_group_check=True)
            pe.matmul(dst, hi, wlo, start=False, stop=False, skip_group_check=True)
            return pe.matmul(dst, lo, whi, start=False, stop=last, skip_group_check=True)

        def half_parts(n, rows_, c):
            a = w_hi[:, n % SPLIT, :].rearrange("p (k c) -> p k c", k=rows_)[:, c]
            b = w_lo[:, n % SPLIT, :].rearrange("p (k c) -> p k c", k=rows_)[:, c]
            return a, b

        def unit_out(eng, layer, u):
            if (layer, u) in ACT_ROWS:
                eng.wait_ge(act_rows, ACT_ROWS[layer, u])
            elif u < U_V + 2:
                eng.wait_ge(v_ready, 4 * layer + 2 * (u - U_V) + 2)
            elif u in (6, 9):
                eng.wait_ge(ch_ready, 4 * layer + (2 if u == 6 else 4))
            elif u in (7, 10):
                eng.wait_ge(dve_rows, 4 * layer + (2 if u == 7 else 4))
            elif u < U_OUT:
                eng.wait_ge(sig_ready, 8 * layer + 2 * (u - U_GATE) + 2)
            elif u < U_WO:
                eng.wait_ge(merged_conv if u % 2 else merged_attn, 4 * layer + 2 * ((u - U_OUT) // 2) + 2)
            else:
                eng.wait_ge(x_new, 8 * layer + 2 * (u - U_WO) + 2)

        def job_out(eng, layer, job):
            kind, i = job
            head, both = HEADS * layer + i, 2 * layer + i
            if kind == "scores":
                eng.wait_ge(biased, head + 1)
            elif kind == "turn_w":
                eng.wait_ge(wgtT_ready, head + 1)
            elif kind == "values":
                eng.wait_ge(arow_ready, 2 * head + 2)
            elif kind == "turn_a":
                eng.wait_ge(aT_lo_ready, head + 1)
            elif kind == "turn_qk":
                eng.wait_ge(qk_ready, 2 * (4 * layer + i) + 2)
            elif kind == "turn_u":
                eng.wait_ge(uT_ready, 2 * both + 2)
            elif kind == "turn_b":
                eng.wait_ge(c_ready, 2 * both + 2)
            else:
                eng.wait_ge(mT_lo_ready, 2 * both + 2)

        def job_in_bank(eng, layer, job, b):
            eng.wait_ge(bank_full[b], BANK_USES[b] * layer + BANK_AT[job, b])

        def rows_turned(eng, layer, s):
            past = [j for t in range(s) for j in JOBS[t] if j[0] in TURNS_OF_ROWS]
            if past:
                job_in_bank(eng, layer, past[-1], 7)

        def cols_of(w, c0, hf):
            return w.rearrange("(k p) n -> p k n", p=P)[:, 4 * hf:4 * hf + 4, c0:c0 + CHUNK]

        def mixer_source(layer, s):
            u, hf = unit_of(s)
            if u < U_OUT:
                return cols_of(w_in[layer], W_IN_COLS[u], hf)
            if u < U_WO:
                w = w_o_conv if u % 2 else w_o_attn
                return cols_of(w[layer], CHUNK * ((u - U_OUT) // 2), hf)
            return cols_of(w_o[layer], CHUNK * (u - U_WO), hf)

        gu_view = dense_gu[0].rearrange("(k p) (two n) -> p k two n", p=P, two=2)
        down_view = dense_down[0].rearrange("(j p) n -> p j n", p=P)

        def bank_quads(b):
            return bank[b][:, :].rearrange("p (c n) -> p c n", n=P)

        block = ctx.enter_context(nc.Block())

        @block.sync
        def _(sp):
            sp.dma_start(X[:, :, :],
                         x.rearrange("a (t p) d -> p (a t) d", p=P)).then_inc(x_in, 16)
            sp.dma_start(gain, mix_norm_g[0].partition_broadcast(P)).then_inc(gain_in, 16)
            load_half(sp, 0, mixer_source(0, 0))
            load_half(sp, 1, mixer_source(0, 1))
            sp.dma_start(relb[0:NBUCKETS, :], rel_bias).then_inc(relb_in, 16)
            sp.dma_start(w_raw[0:NBUCKETS + 1, RAW - 1, 0:LINE], bucket_of).then_inc(bucket_in, 16)
            sp.dma_start(rows[:, 0:DEPTH * 4 * HD],
                         lam_qk.rearrange("l i d -> (l i d)").partition_broadcast(P)).then_inc(lam_in, 16)
            sp.dma_start(gsub[:, :, :].rearrange("p l e -> p (l e)"),
                         subln_g.rearrange("l e -> (l e)").partition_broadcast(P)).then_inc(sub_in, 16)
            sp.dma_start(conv_rows[:, :], conv_w.rearrange("l w (c p) -> (l w c) p", p=P)).then_inc(conv_in, 16)
            for s in range(2, RAW - 1):
                load_half(sp, s, mixer_source(0, s))
            for h in range(HEADS):
                sp.wait_ge(line_sb, h + 1)
                sp.dma_start(lines[h], bias[:, h, :]).then_inc(line_out, 16)
            sp.wait_ge(line_out, 16 * HEADS)
            for h in range(HEADS):
                for c0, j0, n in ((0, 255, P), (P, 127, 2 * P)):
                    sp.dma_start(bias[:, h, c0:c0 + n],
                                 bass.AP(tensor=lines.tensor, offset=h * P * LINE + j0,
                                         ap=[[LINE - 1, P], [1, n]])).then_inc(bias_in, 16)
            sp.wait_ge(line_ps, HEADS)
            for s in range(RAW - 1, MIX_HALVES):
                load_half(sp, s, mixer_source(0, s))
            n = DENSE0
            for hf in range(2):
                load_half(sp, n + hf, gu_view[:, :, hf, 0:FFW])
            with sp.Fori(0, (FSTEPS - 1) // 2) as it:
                for i in range(2):
                    m = 2 * it + 1 + i
                    for hf in range(2):
                        load_half(sp, n + 2 + 3 * i + hf, gu_view[:, :, hf, bass.ds(FFW * m, FFW)], it)
                    load_half(sp, n + 4 + 3 * i, down_view[:, bass.ds(2 * (m - 1), 2), :], it)
            load_half(sp, n + DENSE_HALVES - 1, down_view[:, 2 * (FSTEPS - 1):2 * FSTEPS, :])
            for s in range(MIX_HALVES):
                load_half(sp, MIX0[1] + s, mixer_source(1, s))

            def stream_expert(e, b):
                gu = expert_gu[0, e].rearrange("(k p) (two n) -> p k two n", p=P, two=2)
                down = expert_down[0, e].rearrange("(j p) n -> p j n", p=P)
                for i in range(4):
                    load_half(sp, MOE0 + i, gu[:, 4 * (i % 2):4 * (i % 2) + 4, i // 2, 0:CHUNK], CYCLES * b)
                with sp.Fori(1, MSTEPS) as m:
                    cyc = CYCLES * b + m - 1
                    for i in range(4):
                        load_half(sp, MOE0 + 4 + i,
                                  gu[:, 4 * (i % 2):4 * (i % 2) + 4, i // 2, bass.ds(CHUNK * m, CHUNK)], cyc)
                    for i in range(2):
                        load_half(sp, MOE0 + 8 + i, down[:, bass.ds(4 * (m - 1) + 2 * i, 2), :], cyc)
                for i in range(2):
                    j = 4 * (MSTEPS - 1) + 2 * i
                    load_half(sp, MOE0 + BLOCK_HALVES - 2 + i, down[:, j:j + 2, :], CYCLES * b)

            with sp.Fori(0, EXPERTS) as b:
                stream_expert(b, b)
            sp.wait_ge(route_ready, 1)
            blocks = sp.value_load(ctl_i[0:1, 0:1], min_val=EXPERTS, max_val=EXPERTS + SLOTS)
            with sp.If(blocks > EXPERTS):
                with sp.Fori(EXPERTS, blocks) as b:
                    e = sp.value_load(ctl_i[0:1, bass.ds(b - (EXPERTS - 1), 1)], min_val=0, max_val=EXPERTS - 1)
                    stream_expert(e, b)
            sp.wait_ge(hrow_ready, 2 * 5)
            sp.dma_start(out.rearrange("a (t p) d -> p (a t) d", p=P), hrow).then_inc(out_sent, 16)
            sp.wait_ge(out_sent, 16)

        @block.gpsimd
        def _(pool):
            pool.memset(ident[:, :], 0.0).then_inc(pool_step, 1)
            pool.memset(ones[:, :], 1.0).then_inc(pool_step, 1)
            pool.memset(uT[:, :, :], 0.0).then_inc(pool_step, 1)
            pool.wait_ge(pool_step, 3)
            pool.affine_select(out=ident[:, :], in_=ident[:, :], compare_op=ALU.not_equal, fill=1.0, base=0,
                               pattern=[[-1, P]], channel_multiplier=1).then_inc(const_ready, 1)
            pool.affine_select(out=before[:, :], in_=ones[:, :], compare_op=ALU.is_gt, fill=0.0, base=0,
                               pattern=[[1, P]], channel_multiplier=-1).then_inc(const_ready, 1)
            pool.iota(iota_j[:, :], pattern=[[1, P]], base=0, channel_multiplier=0,
                      allow_small_or_imprecise_dtypes=True).then_inc(const_ready, 1)
            pool.iota(iota_e[:, :], pattern=[[1, EXPERTS]], base=0, channel_multiplier=0,
                      allow_small_or_imprecise_dtypes=True).then_inc(const_ready, 1)

        @block.scalar
        def _(act):
            for h in range(HEADS):
                act.wait_ge(line_ps, h + 1)
                act.activation(bias[:, h, :], bank[4 + h % 4][:, 0:LINE], ACT.Copy).then_inc(line_sb, 1)
            act.wait_ge(lam_sums, 1)
            act.activation(lam4[:, :, :], lam4[:, :, :], ACT.Exp).then_inc(lam_exp, 1)

            def norm_sums(q):
                if q == 0:
                    act.wait_ge(x_in, 16)
                else:
                    act.wait_ge(x_new, X_ADDS[q])
                    act.wait_ge(hrow_ready, 2 * q)
                for t in range(TT):
                    act.activation(part[:, :], X[:, t, :], ACT.Square,
                                   accum_out=ssq[:, t:t + 1]).then_inc(ss_ready, 1)
                    act.wait_ge(ss_ready, 2 * q + t + 1)

            def norm_hi(q):
                for t in range(TT):
                    for g in range(2):
                        act.wait_ge(norm_ps, 4 * q + 2 * t + g + 1)
                        act.activation(k_tok(hT_hi)[:, 4 * g:4 * g + 4, P * t:P * t + P],
                                       bank_quads(2 * t + g), ACT.Copy).then_inc(hT_hi_ready, 1)

            def next_gain(q, source):
                act.wait_ge(hrow_ready, 2 * q)
                act.wait_ge(cT_lo_ready, q + 1)
                act.dma_start(gain, source.partition_broadcast(P)).then_inc(gain_in, 16)

            def mixer(layer):
                n0 = MIX0[layer]
                for s in range(MIX_HALVES + 1):
                    if s < MIX_HALVES and (layer == 0 or s + 2 < MIX_HALVES):
                        split_hi(act, n0 + s + 2)
                    if s == 30 and layer == 0:
                        next_gain(1, ffn_norm_g[0])
                    if s == 30 and layer == 1:
                        next_gain(3, ffn_norm_g[1])
                        act.dma_start(rtr[:, :].rearrange("p (k e) -> p k e", e=EXPERTS),
                                      router_w[0].rearrange("(k p) e -> p k e", p=P)).then_inc(rtr_in, 16)
                    for u in range(UNITS):
                        if last_half(u) != s - 1:
                            continue
                        banks = [bank[2 * (u % 2) + t] for t in range(TT)]
                        if u < U_V:
                            act.wait_ge(half_used, n0 + s)
                            rows_turned(act, layer, s)
                            for t in range(TT):
                                i = act.activation(tok_c(rows)[:, t], banks[t][:, :], ACT.Copy,
                                                   scale=HD ** -0.5 if u < 2 else 1.0)
                                i.then_inc(act_rows, 1)
                        elif u < U_V + 2:
                            act.wait_ge(half_used, n0 + s)
                            for t in range(TT):
                                act.activation(v_rows[:, t, CHUNK * (u - U_V):CHUNK * (u - U_V + 1)],
                                               banks[t][:, :], ACT.Copy).then_inc(v_ready, 1)
                        elif u in (6, 9):
                            act.wait_ge(half_used, n0 + s)
                            for t in range(TT):
                                act.activation(tok_c(part)[:, t], banks[t][:, :], ACT.Copy).then_inc(ch_ready, 1)
                        elif u in (8, 11):
                            act.wait_ge(half_used, n0 + s)
                            rows_turned(act, layer, s)
                            for t in range(TT):
                                act.activation(tok_c(rows)[:, t], banks[t][:, :], ACT.Copy).then_inc(act_rows, 1)
                        elif U_GATE <= u < U_OUT:
                            act.wait_ge(half_used, n0 + s)
                            g = u - U_GATE
                            dst = sig_attn if g < 2 else sig_conv
                            for t in range(TT):
                                act.activation(dst[:, t, CHUNK * (g % 2):CHUNK * (g % 2 + 1)], banks[t][:, :],
                                               ACT.Sigmoid).then_inc(sig_ready, 1)
                    for kind, i in JOBS[s - 1] if s else []:
                        def full(b):
                            job_in_bank(act, layer, (kind, i), b)
                        if kind == "scores":
                            act.wait_ge(biased, HEADS * layer + i + 1)
                            for t, c0, c1 in ((0, 0, P), (1, P, LINE)):
                                for m in range(2):
                                    act.activation(prob[:, m, c0:c1], prob[:, m, c0:c1], ACT.Exp,
                                                   bias=nmax[:, 2 * t + m:2 * t + m + 1],
                                                   accum_out=psum_row[:, 2 * t + m:2 * t + m + 1]).then_inc(exp_ready, 1)
                        if kind == "turn_w":
                            full(6)
                            if i or layer:
                                pl, ph = (layer, i - 1) if i else (layer - 1, HEADS - 1)
                                job_in_bank(act, pl, ("values", ph), 7)
                            act.activation(wgtT[:, :], bank[6][:, 0:LINE], ACT.Copy).then_inc(wgtT_ready, 1)
                        if kind == "values":
                            full(7)
                            if i or layer:
                                act.wait_ge(arow_ready, 2 * (HEADS * layer + i))
                            for t in range(TT):
                                act.activation(squares[:, t, :], bank[7][:, P * t:P * t + P], ACT.Square,
                                               accum_out=ssq[:, t:t + 1]).then_inc(o_ss, 1)
                        if kind == "turn_a":
                            full(6)
                            act.activation(k_tok(aT_hi)[:, i, :], bank[6][:, 0:SEQ], ACT.Copy).then_inc(aT_hi_ready, 1)
                        if kind == "turn_u":
                            if i or layer:
                                act.wait_ge(yT_ready, 4 * (2 * layer + i))
                            for t in range(TT):
                                full(6 + t)
                                act.activation(uT[:, :, 2 + P * t:2 + P * t + P], bank_quads(6 + t),
                                               ACT.Copy).then_inc(uT_ready, 1)
                        if kind == "turn_b":
                            act.wait_ge(c_ready, 2 * (2 * layer + i) + 2)
                            act.activation(k_tok(cT_hi)[:, 4 * i:4 * i + 4, :], yTv, ACT.Copy).then_inc(cT_hi_ready, 1)
                        if kind == "turn_m":
                            for t in range(TT):
                                full(6 + t)
                                act.activation(k_tok(hT_hi)[:, 4 * i:4 * i + 4, P * t:P * t + P], bank_quads(6 + t),
                                               ACT.Copy).then_inc(mT_hi_ready, 1)

            def dense():
                def silu(m):
                    for t in range(TT):
                        act.wait_ge(d_rows, 2 * m + 1)
                        act.activation(tok_c(part)[:, t, 0:FFW], bank[t][:, 0:FFW], ACT.Silu).then_inc(d_silu, 1)

                def turn_hi(m):
                    act.wait_ge(d_turn, m + 1)
                    act.activation(ffT_hi, bank[2][:, :], ACT.Copy).then_inc(d_hi, 1)

                n0 = DENSE0
                split_hi(act, n0 + 2)
                split_hi(act, n0 + 3)
                act.wait_ge(half_used, n0 + 2)
                silu(0)
                with act.Fori(0, (FSTEPS - 1) // 2) as it:
                    for i in range(2):
                        m = 2 * it + 1 + i
                        n = n0 + 2 + 3 * i
                        split_hi(act, n + 2, it)
                        turn_hi(m - 1)
                        split_hi(act, n + 3, it)
                        split_hi(act, n + 4, it)
                        act.wait_ge(half_used, n + 2 + RAW * it)
                        silu(m)
                turn_hi(FSTEPS - 1)
                split_hi(act, n0 + DENSE_HALVES + 1)

            def experts():
                act.wait_ge(rtr_in, 16)
                act.activation(rtr_hi[:, :], rtr[:, :], ACT.Copy).then_inc(rtr_hi_ready, 1)
                act.wait_ge(hrow_ready, 8)
                for t in range(TT):
                    act.activation(hr_hi[:, t, :], hrow[:, t, :], ACT.Copy).then_inc(hr_hi_ready, 1)
                act.wait_ge(gap_ready, 1)
                act.activation(rs[:, 4, :], rs[:, 3, :], ACT.Exp).then_inc(gap_exp, 1)
                act.wait_ge(route_ready, 1)
                blocks = act.value_load(ctl_i[0:1, 0:1], min_val=EXPERTS, max_val=EXPERTS + SLOTS)

                def gathered(g):
                    for i, b, dst in ((0, 6, xg_hi[:, 0:CHUNK]), (2, 3, xg_lo[:, 0:CHUNK])):
                        act.wait_ge(gather_ps, 4 * g + i + 1)
                        act.activation(dst, bank[b][:, :], ACT.Copy).then_inc(xg_act, 1)

                def take_y(b):
                    act.wait_ge(half_used, MOE0 + BLOCK_HALVES * b)
                    act.wait_ge(scatter_ps, 4 * b + 1)
                    act.wait_ge(spread_ready, 2 * b + 1)
                    for hf in range(2):
                        act.activation(y_hi[:, CHUNK * hf:CHUNK * (hf + 1)], bank[4 + hf][:, :], ACT.Copy,
                                       scale=gate[:, 0:1]).then_inc(y_hi_ready, 1)

                def silu(b, m):
                    act.wait_ge(e_rows, MSTEPS * b + m + 1)
                    act.activation(part[:, 0:CHUNK], bank[0][:, :], ACT.Silu).then_inc(e_silu, 1)

                def turn_hi(b, m):
                    act.wait_ge(e_turn, MSTEPS * b + m + 1)
                    act.activation(ffT_hi, bank[2][:, :], ACT.Copy).then_inc(e_hi, 1)

                act.wait_ge(moe_init, 1)
                gathered(0)
                with act.Fori(0, blocks) as b:
                    c = CYCLES * b
                    split_hi(act, MOE0, c)
                    split_hi(act, MOE0 + 1, c)
                    take_y(b)
                    for i in range(2, 6):
                        split_hi(act, MOE0 + i, c)
                    act.wait_ge(half_used, MOE0 + 4 + BLOCK_HALVES * b)
                    silu(b, 0)
                    act.wait_ge(spread_ps, b + 1)
                    act.activation(spread_r, bank[7][:, 0:SEQ].rearrange("p (t j) -> p t j", t=TT),
                                   ACT.Copy).then_inc(spread_ready, 1)
                    act.activation(gate[:, :], bank[7][:, SEQ:SEQ + 1], ACT.Copy).then_inc(spread_ready, 1)
                    with act.Fori(1, MSTEPS) as m:
                        cm = c + m - 1
                        split_hi(act, MOE0 + 6, cm)
                        turn_hi(b, m - 1)
                        for i in range(7, 11):
                            split_hi(act, MOE0 + i, cm)
                        act.wait_ge(half_used, MOE0 + 8 + RAW * cm)
                        silu(b, m)
                        split_hi(act, MOE0 + 11, cm)
                    turn_hi(b, MSTEPS - 1)
                    gathered(b + 1)
                take_y(blocks)

            norm_sums(0)
            split_hi(act, 0)
            split_hi(act, 1)
            norm_hi(0)
            mixer(0)
            norm_sums(1)
            norm_hi(1)
            act.wait_ge(hrow_ready, 4)
            act.dma_start(gain, mix_norm_g[1].partition_broadcast(P)).then_inc(gain_in, 16)
            dense()
            norm_sums(2)
            norm_hi(2)
            mixer(1)
            norm_sums(3)
            norm_hi(3)
            act.wait_ge(hrow_ready, 8)
            act.dma_start(gain, final_norm_g.partition_broadcast(P)).then_inc(gain_in, 16)
            experts()
            blocks = act.value_load(ctl_i[0:1, 0:1], min_val=EXPERTS, max_val=EXPERTS + SLOTS)
            act.wait_ge(x_add, 4 * blocks + 4)
            act.wait_ge(e_rows, MSTEPS * EXPERTS)
            for t in range(TT):
                act.activation(part[:, :], X[:, t, :], ACT.Square, accum_out=ssq[:, t:t + 1]).then_inc(ss_ready, 1)
                act.wait_ge(ss_ready, 8 + t + 1)

        @block.vector
        def _(dve):
            count = [0]

            def chain(ins):
                count[0] += 1
                ins.then_inc(dve_step, 1)
                dve.wait_ge(dve_step, count[0])

            def rsqrt_of(sums, scale, n):
                v, t, y = nw[0][:, 0:n], nw[1][:, 0:n], nwi[:, 0:n].bitcast(F32)
                chain(dve.tensor_scalar(v, sums, scale, EPS, ALU.mult, ALU.add))
                chain(dve.tensor_scalar(nwi[:, 0:n], v.bitcast(I32), 1, None, ALU.logical_shift_right))
                chain(dve.tensor_scalar(nwi[:, 0:n], nwi[:, 0:n], -1.0, float(0x5F3759DF), ALU.mult, ALU.add))
                chain(dve.tensor_scalar(v, v, -0.5, None, ALU.mult))
                for _ in range(3):
                    chain(dve.tensor_tensor(t, y, y, ALU.mult))
                    chain(dve.tensor_tensor(t, t, v, ALU.mult))
                    chain(dve.scalar_tensor_tensor(out=y, in0=t, scalar=1.5, in1=y, op0=ALU.add, op1=ALU.mult))
                chain(dve.tensor_copy(nw[2][:, 0:n], y))

            def norm_rows(q):
                dve.wait_ge(ss_ready, 2 * q + 2)
                rsqrt_of(ssq[:, 0:TT], 1.0 / D, TT)
                dve.wait_ge(gain_in, 16 * (q + 1))
                for t in range(TT):
                    dve.scalar_tensor_tensor(out=hrow[:, t, :], in0=X[:, t, :], scalar=nw[2][:, t:t + 1], in1=gain,
                                             op0=ALU.mult, op1=ALU.mult).then_inc(hrow_ready, 1)

            def norm_lo(q):
                for t in range(TT):
                    for g in range(2):
                        dve.wait_ge(hT_hi_ready, 4 * q + 2 * t + g + 1)
                        dve.tensor_tensor(k_tok(hT_lo)[:, 4 * g:4 * g + 4, P * t:P * t + P], bank_quads(2 * t + g),
                                          k_tok(hT_hi)[:, 4 * g:4 * g + 4, P * t:P * t + P],
                                          ALU.subtract).then_inc(hT_lo_ready, 1)

            def mixer(layer):
                n0 = MIX0[layer]

                for s in range(MIX_HALVES + 1):
                    def full(b):
                        job_in_bank(dve, layer, (kind, i), b)
                    jobs = JOBS[s - 1] if s else []
                    for kind, i in jobs:
                        if kind == "scores":
                            for m in range(2):
                                full(4 + m)
                                if s == 13 and m == 0 and layer == 0:
                                    dve.wait_ge(bias_in, 16 * 2 * HEADS)
                                chain(dve.tensor_tensor(prob[:, m, :], bank[4 + m][:, 0:LINE], bias[:, i, :],
                                                        ALU.add))
                            chain(dve.tensor_reduce(nmax[:, 0:2], prob[:, :, 0:P], AX, ALU.max, negate=True))
                            dve.tensor_reduce(nmax[:, 2:4], prob[:, :, P:LINE], AX, ALU.max,
                                              negate=True).then_inc(biased, 1)
                    if s < MIX_HALVES and (layer == 0 or s + 2 < MIX_HALVES):
                        split_lo(dve, n0 + s + 2)
                    for u in range(UNITS):
                        if last_half(u) != s - 1:
                            continue
                        banks = [bank[2 * (u % 2) + t] for t in range(TT)]
                        if u in (7, 10):
                            dve.wait_ge(half_used, n0 + s)
                            dve.wait_ge(ch_ready, 4 * layer + (2 if u == 7 else 4))
                            rows_turned(dve, layer, s)
                            for t in range(TT):
                                dve.tensor_tensor(tok_c(rows)[:, t], banks[t][:, :], tok_c(part)[:, t],
                                                  ALU.mult).then_inc(dve_rows, 1)
                        elif U_OUT <= u < U_WO:
                            half_u = (u - U_OUT) // 2
                            cols = slice(CHUNK * half_u, CHUNK * (half_u + 1))
                            dve.wait_ge(half_used, n0 + s)
                            dve.wait_ge(sig_ready, 8 * (layer + 1))
                            if u % 2 == 0:
                                for t in range(TT):
                                    dve.tensor_tensor(merged[:, t, cols], banks[t][:, :], sig_attn[:, t, cols],
                                                      ALU.mult).then_inc(merged_attn, 1)
                            else:
                                for t in range(TT):
                                    dve.tensor_tensor(sig_conv[:, t, cols], banks[t][:, :], sig_conv[:, t, cols],
                                                      ALU.mult).then_inc(merged_conv, 1)
                                dve.wait_ge(merged_attn, 4 * layer + 2 * half_u + 2)
                                dve.wait_ge(merged_conv, 4 * layer + 2 * half_u + 2)
                                for t in range(TT):
                                    dve.tensor_tensor(merged[:, t, cols], merged[:, t, cols], sig_conv[:, t, cols],
                                                      ALU.add).then_inc(merged_ready, 1)
                        elif u >= U_WO:
                            cols = slice(CHUNK * (u - U_WO), CHUNK * (u - U_WO + 1))
                            dve.wait_ge(half_used, n0 + s)
                            for t in range(TT):
                                dve.tensor_tensor(X[:, t, cols], X[:, t, cols], banks[t][:, :],
                                                  ALU.add).then_inc(x_new, 1)
                    for kind, i in jobs:
                        head = HEADS * layer + i
                        if kind == "turn_qk":
                            buf = qT if i < 2 else kT
                            h0 = 4 * (i % 2)
                            for t in range(TT):
                                full(6 + t)
                                dve.tensor_copy(buf[:, h0:h0 + 4, P * t:P * t + P],
                                                bank_quads(6 + t)).then_inc(qk_ready, 1)
                        if kind == "scores":
                            dve.wait_ge(exp_ready, 4 * head + 4)
                            chain(dve.reciprocal(recip[:, :], psum_row[:, :]))
                            chain(dve.tensor_scalar(recip[:, 1:4:2], recip[:, 1:4:2], neg_lam[:, layer:layer + 1],
                                                    None, ALU.mult))
                            if head:
                                pl, ph = (layer, i - 1) if i else (layer - 1, HEADS - 1)
                                job_in_bank(dve, pl, ("turn_w", ph), 6)
                            for t, c0, c1 in ((0, 0, P), (1, P, LINE)):
                                dve.tensor_scalar(wgt[:, c0:c1], prob[:, 0, c0:c1], recip[:, 2 * t:2 * t + 1], None,
                                                  ALU.mult).then_inc(dve_step, 1)
                            count[0] += 2
                            dve.wait_ge(dve_step, count[0])
                            for t, c0, c1 in ((0, 0, P), (1, P, LINE)):
                                dve.scalar_tensor_tensor(out=wgt[:, c0:c1], in0=prob[:, 1, c0:c1],
                                                         scalar=recip[:, 2 * t + 1:2 * t + 2], in1=wgt[:, c0:c1],
                                                         op0=ALU.mult, op1=ALU.add).then_inc(wgt_ready, 1)
                            dve.wait_ge(wgt_ready, 2 * head + 2)
                        if kind == "values":
                            dve.wait_ge(o_ss, 2 * head + 2)
                            rsqrt_of(ssq[:, 0:TT], 1.0 / P, TT)
                            if head:
                                pl, ph = (layer, i - 1) if i else (layer - 1, HEADS - 1)
                                job_in_bank(dve, pl, ("turn_a", ph), 6)
                            for t in range(TT):
                                dve.scalar_tensor_tensor(out=arow[:, t, :], in0=bank[7][:, P * t:P * t + P],
                                                         scalar=nw[2][:, t:t + 1], in1=gsub[:, layer, :],
                                                         op0=ALU.mult, op1=ALU.mult).then_inc(arow_ready, 1)
                        if kind == "turn_a":
                            dve.wait_ge(aT_hi_ready, head + 1)
                            dve.tensor_tensor(k_tok(aT_lo)[:, i, :], bank[6][:, 0:SEQ], k_tok(aT_hi)[:, i, :],
                                              ALU.subtract).then_inc(aT_lo_ready, 1)
                        if kind == "turn_u":
                            dve.wait_ge(uT_ready, 2 * (2 * layer + i) + 2)
                            for tap in (2, 1, 0):
                                for c in range(4):
                                    w = convT[:, layer, tap, 4 * i + c:4 * i + c + 1]
                                    src = uT[:, c, tap:tap + SEQ]
                                    if tap == 2:
                                        ins = dve.tensor_scalar(yTv[:, c, :], src, w, None, ALU.mult)
                                    else:
                                        ins = dve.scalar_tensor_tensor(out=yTv[:, c, :], in0=src, scalar=w,
                                                                       in1=yTv[:, c, :], op0=ALU.mult, op1=ALU.add)
                                    ins.then_inc(dve_step if tap else yT_ready, 1)
                                if tap:
                                    count[0] += 4
                                    dve.wait_ge(dve_step, count[0])
                        if kind == "turn_b":
                            for t in range(TT):
                                full(6 + t)
                                dve.wait_ge(yT_ready, 4 * (2 * layer + i) + 4)
                                dve.tensor_tensor(yTv[:, :, P * t:P * t + P], bank_quads(6 + t),
                                                  yTv[:, :, P * t:P * t + P], ALU.mult).then_inc(c_ready, 1)
                            dve.wait_ge(cT_hi_ready, 2 * layer + i + 1)
                            dve.tensor_tensor(k_tok(cT_lo)[:, 4 * i:4 * i + 4, :], yTv,
                                              k_tok(cT_hi)[:, 4 * i:4 * i + 4, :],
                                              ALU.subtract).then_inc(cT_lo_ready, 1)
                        if kind == "turn_m":
                            for t in range(TT):
                                dve.wait_ge(mT_hi_ready, 2 * (2 * layer + i) + t + 1)
                                dve.tensor_tensor(k_tok(hT_lo)[:, 4 * i:4 * i + 4, P * t:P * t + P], bank_quads(6 + t),
                                                  k_tok(hT_hi)[:, 4 * i:4 * i + 4, P * t:P * t + P],
                                                  ALU.subtract).then_inc(mT_lo_ready, 1)

            def dense():
                def gated(m):
                    for t in range(TT):
                        dve.wait_ge(d_silu, 2 * m + t + 1)
                        if t == 0:
                            dve.wait_ge(d_lo, m + 1)
                        dve.tensor_tensor(tok_c(rows)[:, t, 0:FFW], bank[t][:, FFW:2 * FFW], tok_c(part)[:, t, 0:FFW],
                                          ALU.mult).then_inc(d_rows, 1)

                def turn_lo(m):
                    dve.wait_ge(d_hi, m + 1)
                    dve.tensor_tensor(ffT_lo, bank[2][:, :], ffT_hi, ALU.subtract).then_inc(d_lo, 1)

                n0 = DENSE0
                split_lo(dve, n0 + 2)
                split_lo(dve, n0 + 3)
                gated(0)
                with dve.Fori(0, (FSTEPS - 1) // 2) as it:
                    for i in range(2):
                        m = 2 * it + 1 + i
                        n = n0 + 2 + 3 * i
                        split_lo(dve, n + 2, it)
                        turn_lo(m - 1)
                        split_lo(dve, n + 3, it)
                        split_lo(dve, n + 4, it)
                        gated(m)
                turn_lo(FSTEPS - 1)
                split_lo(dve, n0 + DENSE_HALVES + 1)
                dve.wait_ge(half_used, n0 + DENSE_HALVES)
                for t in range(TT):
                    for hf in range(2):
                        dve.tensor_tensor(X[:, t, CHUNK * hf:CHUNK * (hf + 1)], X[:, t, CHUNK * hf:CHUNK * (hf + 1)],
                                          bank[4 + 2 * t + hf][:, :], ALU.add).then_inc(x_new, 1)

            def route():
                def col(i, t):
                    return rs[:, i, t:t + 1]

                def first_max(src, i_max, i_eq, i_one):
                    chain(dve.tensor_reduce(rs[:, i_max, :], src, AX, ALU.max))
                    for t in range(TT):
                        chain(dve.tensor_scalar(rt[:, i_eq, t, :], src[:, t, :], col(i_max, t), None, ALU.is_equal))
                        chain(dve.tensor_tensor(rt[:, i_eq, t, :], rt[:, i_eq, t, :], rt[:, 15, 0, :], ALU.mult))
                    chain(dve.tensor_reduce(rs[:, 10, :], rt[:, i_eq, :, :], AX, ALU.min))
                    for t in range(TT):
                        chain(dve.tensor_scalar(rt[:, i_one, t, :], rt[:, 15, 0, :], col(10, t), None, ALU.is_equal))

                dve.wait_ge(const_ready, 4)
                chain(dve.tensor_scalar(rt[:, 15, 0, :], iota_e[:, :], 99.0, None, ALU.subtract))
                dve.wait_ge(logits_ps, 1)
                chain(dve.tensor_copy(rt[:, 0, :, :], bank[4][:, 0:TT * EXPERTS].rearrange("p (t e) -> p t e", t=TT)))
                first_max(rt[:, 0, :, :], 0, 1, 2)
                chain(dve.scalar_tensor_tensor(out=rt[:, 3, :, :], in0=rt[:, 2, :, :], scalar=-BIG, in1=rt[:, 0, :, :],
                                               op0=ALU.mult, op1=ALU.add))
                first_max(rt[:, 3, :, :], 1, 4, 5)
                dve.tensor_tensor(rs[:, 3, :], rs[:, 1, :], rs[:, 0, :], ALU.subtract).then_inc(gap_ready, 1)
                dve.tensor_tensor(rt[:, 6, :, :], rt[:, 2, :, :], rt[:, 5, :, :], ALU.add).then_inc(mask_ready, 1)
                dve.wait_ge(gap_exp, 1)
                chain(dve.tensor_scalar(rs[:, 5, :], rs[:, 4, :], 1.0, None, ALU.add))
                chain(dve.reciprocal(rs[:, 6, :], rs[:, 5, :]))
                chain(dve.tensor_tensor(rs[:, 7, :], rs[:, 4, :], rs[:, 6, :], ALU.mult))
                for t in range(TT):
                    chain(dve.tensor_scalar(rt[:, 7, t, :], rt[:, 2, t, :], col(6, t), None, ALU.mult))
                    chain(dve.scalar_tensor_tensor(out=rt[:, 7, t, :], in0=rt[:, 5, t, :], scalar=col(7, t),
                                                   in1=rt[:, 7, t, :], op0=ALU.mult, op1=ALU.add))
                dve.wait_ge(place_ps, 1)
                chain(dve.tensor_copy(rt[:, 8, :, :], bank[5][:, 0:16].rearrange("p (t e) -> p t e", t=TT)))
                chain(dve.tensor_copy(rt[:, 9, 0, :], bank[5][:, 16:24]))
                chain(dve.memset(posb[:, :, :], -1.0))
                chain(dve.memset(cwb[:, :, :], 0.0))
                chain(dve.scalar_tensor_tensor(out=rt[:, 10, :, :], in0=rt[:, 8, :, :], scalar=float(P), in1=rt[:, 6, :, :],
                                               op0=ALU.is_lt, op1=ALU.mult))
                chain(dve.scalar_tensor_tensor(out=rt[:, 11, :, :], in0=rt[:, 8, :, :], scalar=1.0, in1=rt[:, 10, :, :],
                                               op0=ALU.add, op1=ALU.mult))
                chain(dve.tensor_scalar(posb[:, :, 0:EXPERTS], rt[:, 11, :, :], 1.0, None, ALU.subtract))
                chain(dve.tensor_copy(cwb[:, :, 0:EXPERTS], rt[:, 7, :, :]))
                chain(dve.tensor_tensor(rt[:, 12, :, :], rt[:, 6, :, :], rt[:, 10, :, :], ALU.subtract))
                chain(dve.scalar_tensor_tensor(out=rt[:, 12, :, :], in0=rt[:, 8, :, :], scalar=float(P - 1),
                                               in1=rt[:, 12, :, :], op0=ALU.subtract, op1=ALU.mult))
                chain(dve.tensor_scalar(rt[:, 9, 1, :], rt[:, 9, 0, :], float(P), None, ALU.is_gt))
                chain(dve.memset(rt[:, 13, 0, :], 0.0))
                for e in range(1, EXPERTS):
                    chain(dve.tensor_tensor(rt[:, 13, 0, e:e + 1], rt[:, 13, 0, e - 1:e], rt[:, 9, 1, e - 1:e], ALU.add))
                chain(dve.tensor_reduce(ctl[:, 0:1], rt[:, 9, 1, :], AX, ALU.add))
                chain(dve.tensor_scalar(ctl[:, 0:1], ctl[:, 0:1], float(EXPERTS), None, ALU.add))
                for s in range(SLOTS):
                    chain(dve.scalar_tensor_tensor(out=rt[:, 13, 1, :], in0=rt[:, 13, 0, :], scalar=float(s),
                                                   in1=rt[:, 9, 1, :], op0=ALU.is_equal, op1=ALU.mult))
                    chain(dve.tensor_tensor(rt[:, 14, 0, :], rt[:, 13, 1, :], iota_e[:, :], ALU.mult))
                    chain(dve.tensor_reduce(ctl[:, 1 + s:2 + s], rt[:, 14, 0, :], AX, ALU.add))
                    for t in range(TT):
                        chain(dve.tensor_tensor(rt[:, 14, 0, :], rt[:, 13, 1, :], rt[:, 12, t, :], ALU.mult))
                        chain(dve.tensor_tensor(rt[:, 14, 1, :], rt[:, 13, 1, :], rt[:, 7, t, :], ALU.mult))
                        c = EXPERTS + s
                        chain(dve.tensor_reduce(posb[:, t, c:c + 1], rt[:, 14, 0, :], AX, ALU.add))
                        chain(dve.tensor_reduce(cwb[:, t, c:c + 1], rt[:, 14, 1, :], AX, ALU.add))
                        chain(dve.tensor_scalar(posb[:, t, c:c + 1], posb[:, t, c:c + 1], 1.0, None, ALU.subtract))
                dve.tensor_copy(ctl_i[:, :], ctl[:, :]).then_inc(route_ready, 1)

            def experts():
                dve.wait_ge(rtr_hi_ready, 1)
                dve.tensor_tensor(rtr_lo[:, :], rtr[:, :], rtr_hi[:, :], ALU.subtract).then_inc(rtr_lo_ready, 1)
                for t in range(TT):
                    dve.wait_ge(hr_hi_ready, t + 1)
                    dve.tensor_tensor(hr_lo[:, t, :], hrow[:, t, :], hr_hi[:, t, :], ALU.subtract).then_inc(hr_lo_ready, 1)
                route()
                dve.wait_ge(route_ready, 1)
                blocks = dve.value_load(ctl_i[0:1, 0:1], min_val=EXPERTS, max_val=EXPERTS + SLOTS)

                def make_pick(g):
                    dve.tensor_copy(pcol[:, :], posb[:, :, bass.ds(g, 1)].rearrange("p t o -> p (t o)")).then_inc(col_ready, 1)
                    dve.tensor_copy(gcol[:, :], cwb[:, :, bass.ds(g, 1)].rearrange("p t o -> p (t o)")).then_inc(col_ready, 1)
                    dve.wait_ge(col_ready, 2 * g + 2)
                    for t in range(TT):
                        dve.tensor_scalar(pick[:, t, :], iota_j[:, :], pcol[:, t:t + 1], None,
                                          ALU.is_equal).then_inc(pick_ready, 1)
                        dve.tensor_scalar(pick_r[:, t, :], iota_j[:, :], pcol[:, t:t + 1], None,
                                          ALU.is_equal).then_inc(pick_ready, 1)

                def gathered(g):
                    for i, b, dst in ((1, 7, xg_hi[:, CHUNK:D]), (3, 6, xg_lo[:, CHUNK:D])):
                        dve.wait_ge(gather_ps, 4 * g + i + 1)
                        dve.tensor_copy(dst, bank[b][:, :]).then_inc(xg_dve, 1)

                def take_y(b):
                    for hf in range(2):
                        dve.wait_ge(y_hi_ready, 2 * b + hf + 1)
                        dve.scalar_tensor_tensor(out=y_lo[:, CHUNK * hf:CHUNK * (hf + 1)], in0=bank[4 + hf][:, :],
                                                 scalar=gate[:, 0:1], in1=y_hi[:, CHUNK * hf:CHUNK * (hf + 1)],
                                                 op0=ALU.mult, op1=ALU.subtract).then_inc(y_lo_ready, 1)

                def add_scattered(b):
                    for i, bk in enumerate((6, 7, 3, 6)):
                        t, hf = i // 2, i % 2
                        dve.wait_ge(scatter_ps, 4 * b + i + 2)
                        dve.tensor_tensor(X[:, t, CHUNK * hf:CHUNK * (hf + 1)], X[:, t, CHUNK * hf:CHUNK * (hf + 1)],
                                          bank[bk][:, :], ALU.add).then_inc(x_add, 1)

                def gated(b, m):
                    dve.wait_ge(e_silu, MSTEPS * b + m + 1)
                    dve.wait_ge(e_lo, MSTEPS * b + m + 1)
                    dve.tensor_tensor(rows[:, 0:CHUNK], bank[1][:, :], part[:, 0:CHUNK], ALU.mult).then_inc(e_rows, 1)

                def turn_lo(b, m):
                    dve.wait_ge(e_hi, MSTEPS * b + m + 1)
                    dve.tensor_tensor(ffT_lo, bank[2][:, :], ffT_hi, ALU.subtract).then_inc(e_lo, 1)

                chain(dve.memset(gate[:, :], 0.0))
                chain(dve.memset(cT_hi[:, 1792:2048].bitcast(F32), 0.0))
                for hf in range(2):
                    chain(dve.memset(bank[4 + hf][:, :], 0.0))
                for s in (scatter_ps, spread_ready, e_rows, e_lo):
                    dve.sem_inc(s, 1)
                dve.sem_inc(moe_init, 1)
                make_pick(0)
                gathered(0)
                with dve.Fori(0, blocks) as b:
                    c = CYCLES * b
                    split_lo(dve, MOE0, c)
                    split_lo(dve, MOE0 + 1, c)
                    take_y(b)
                    for i in range(2, 6):
                        split_lo(dve, MOE0 + i, c)
                    gated(b, 0)
                    add_scattered(b)
                    dve.wait_ge(spread_ps, b + 1)
                    make_pick(b + 1)
                    with dve.Fori(1, MSTEPS) as m:
                        cm = c + m - 1
                        split_lo(dve, MOE0 + 6, cm)
                        turn_lo(b, m - 1)
                        for i in range(7, 11):
                            split_lo(dve, MOE0 + i, cm)
                        gated(b, m)
                        split_lo(dve, MOE0 + 11, cm)
                    turn_lo(b, MSTEPS - 1)
                    gathered(b + 1)
                take_y(blocks)
                add_scattered(blocks)

            chain(dve.memset(zero_r[:, :].bitcast(F32), 0.0))
            chain(dve.memset(relb[NBUCKETS:64, :], -BIG))
            dve.wait_ge(relb_in, 16)
            dve.wait_ge(pool_step, 3)
            for h in range(HEADS):
                if h:
                    dve.wait_ge(line_ps, h)
                dve.tensor_scalar(relb_bc[:, :], ones[0:64, :], relb[:, h:h + 1], None, ALU.mult).then_inc(relb_ready, 1)
            dve.wait_ge(lam_in, 16)
            for i in range(2):
                for l in range(DEPTH):
                    chain(dve.tensor_tensor(lamq[:, l, 2 * i, :], lamq[:, l, 2 * i, :], lamq[:, l, 2 * i + 1, :], ALU.mult))
                    chain(dve.tensor_reduce(lam4[:, i, l:l + 1], lamq[:, l, 2 * i, :], AX, ALU.add))
            dve.sem_inc(lam_sums, 1)
            dve.wait_ge(lam_exp, 1)
            chain(dve.tensor_tensor(neg_lam[:, :], lam4[:, 1, :], lam4[:, 0, :], ALU.subtract))
            dve.wait_ge(sub_in, 16)
            for l in range(DEPTH):
                chain(dve.tensor_scalar(neg_lam[:, l:l + 1], neg_lam[:, l:l + 1], lambda_init(l), None, ALU.subtract))
                chain(dve.tensor_scalar(gsub[:, l, :], gsub[:, l, :], 1.0 - lambda_init(l), None, ALU.mult))
            dve.wait_ge(conv_ps, 1)
            chain(dve.tensor_copy(convT[:, :, :, :].rearrange("p l w c -> p (l w c)"), bank[0][:, 0:DEPTH * 3 * KC]))

            norm_rows(0)
            split_lo(dve, 0)
            split_lo(dve, 1)
            norm_lo(0)
            mixer(0)
            norm_rows(1)
            norm_lo(1)
            dve.sem_inc(d_rows, 1)
            dve.sem_inc(d_lo, 1)
            dense()
            norm_rows(2)
            norm_lo(2)
            mixer(1)
            norm_rows(3)
            norm_lo(3)
            experts()
            norm_rows(4)

        @block.tensor
        def _(pe):
            pe.wait_ge(bucket_in, 16)
            for h in range(HEADS):
                pe.wait_ge(relb_ready, h + 1)
                if h >= 4:
                    pe.wait_ge(line_sb, h - 3)
                pe.matmul(bank[4 + h % 4][:, 0:LINE], relb_bc[0:NBUCKETS + 1, :],
                          w_raw[0:NBUCKETS + 1, RAW - 1, 0:LINE], start=True, stop=True).then_inc(line_ps, 1)

            def norm_turn(q):
                for t in range(TT):
                    pe.wait_ge(hrow_ready, 2 * q + t + 1)
                    for g in range(2):
                        for c in range(4):
                            k = 4 * g + c
                            ins = pe.transpose(bank[2 * t + g][:, P * c:P * c + P], hrow[:, t, P * k:P * k + P], ident[:, :])
                        ins.then_inc(norm_ps, 1)

            def mixer(layer):
                n0 = MIX0[layer]
                pe.wait_ge(hT_lo_ready, 4 * (2 * layer + 1))
                for s in range(MIX_HALVES):
                    u, hf = unit_of(s)
                    if hf == 0 and u >= 2:
                        unit_out(pe, layer, u - 2)
                    if s == 2 * U_OUT:
                        pe.wait_ge(aT_lo_ready, HEADS * (layer + 1))
                    if s == 2 * U_OUT + 2:
                        pe.wait_ge(cT_lo_ready, 2 * (layer + 1))
                    if s in (2 * U_WO, 2 * U_WO + 2):
                        pe.wait_ge(mT_lo_ready, 4 * layer + 2 * (hf + 1))
                    if u < U_OUT or u >= U_WO:
                        hi, lo = k_tok(hT_hi), k_tok(hT_lo)
                    elif u % 2 == 0:
                        hi, lo = k_tok(aT_hi), k_tok(aT_lo)
                    else:
                        hi, lo = k_tok(cT_hi), k_tok(cT_lo)
                    pe.wait_ge(lo_ready, n0 + s + 1)
                    for t in range(TT):
                        for c in range(4):
                            k = 4 * hf + c
                            whi, wlo = half_parts(n0 + s, 4, c)
                            ins = product(pe, bank[2 * (u % 2) + t][:, :], hi[:, k, P * t:P * t + P],
                                          lo[:, k, P * t:P * t + P], whi, wlo, k == 0, k == KC - 1)
                    ins.then_inc(half_used, 1)
                    for job in JOBS[s]:
                        kind, i = job
                        for b in JOB_BANKS[kind]:
                            if JOB_BEFORE[job, b]:
                                job_out(pe, layer, JOB_BEFORE[job, b])
                            elif layer:
                                job_out(pe, layer - 1, LAST_JOB[b])
                            else:
                                pe.wait_ge(line_sb, HEADS)
                        head = HEADS * layer + i
                        if kind in ("turn_qk", "turn_u", "turn_b"):
                            if kind == "turn_u":
                                pe.wait_ge(dve_rows, 2 * (2 * layer + i) + 2)
                            else:
                                u_src = i if kind == "turn_qk" else (8, 11)[i]
                                pe.wait_ge(act_rows, ACT_ROWS[layer, u_src])
                            for t in range(TT):
                                for c in range(4):
                                    ins = pe.transpose(bank[6 + t][:, P * c:P * c + P],
                                                       tok_c(rows)[:, t, P * c:P * c + P], ident[:, :])
                                ins.then_inc(bank_full[6 + t], 1)
                        if kind == "turn_m":
                            pe.wait_ge(merged_ready, 2 * (2 * layer + i) + 2)
                            for t in range(TT):
                                for c in range(4):
                                    k = 4 * i + c
                                    ins = pe.transpose(bank[6 + t][:, P * c:P * c + P],
                                                       merged[:, t, P * k:P * k + P], ident[:, :])
                                ins.then_inc(bank_full[6 + t], 1)
                        if kind == "scores":
                            pe.wait_ge(qk_ready, 8 * (layer + 1))
                            for m in range(2):
                                r = slice(HD * m, HD * m + HD)
                                pe.matmul(bank[4 + m][:, 0:P], qT[r, i, 0:P], kT[r, i, 0:P], start=True, stop=True)
                                pe.matmul(bank[4 + m][:, P:LINE], qT[r, i, P:SEQ], kT[r, i, 0:SEQ],
                                          start=True, stop=True).then_inc(bank_full[4 + m], 1)
                        if kind == "turn_w":
                            pe.wait_ge(wgt_ready, 2 * head + 2)
                            for c in range(3):
                                ins = pe.transpose(bank[6][:, P * c:P * c + P], wgt[:, P * c:P * c + P], ident[:, :])
                            ins.then_inc(bank_full[6], 1)
                        if kind == "values":
                            pe.wait_ge(wgtT_ready, head + 1)
                            pe.wait_ge(v_ready, 4 * (layer + 1))
                            e = slice(P * i, P * i + P)
                            pe.matmul(bank[7][:, 0:P], wgtT[:, 0:P], v_rows[:, 0, e], start=True, stop=True)
                            pe.matmul(bank[7][:, P:2 * P], wgtT[:, P:2 * P], v_rows[:, 0, e], start=True, stop=False)
                            pe.matmul(bank[7][:, P:2 * P], wgtT[:, 2 * P:LINE], v_rows[:, 1, e], start=False,
                                      stop=True).then_inc(bank_full[7], 1)
                        if kind == "turn_a":
                            pe.wait_ge(arow_ready, 2 * head + 2)
                            for t in range(TT):
                                ins = pe.transpose(bank[6][:, P * t:P * t + P], arow[:, t, :], ident[:, :])
                            ins.then_inc(bank_full[6], 1)

            def dense():
                n0 = DENSE0
                hi, lo = k_tok(hT_hi), k_tok(hT_lo)
                pe.wait_ge(hT_lo_ready, 8)

                def gate_up(n, cyc):
                    for hf in range(2):
                        pe.wait_ge(lo_ready, n + hf + 1 + RAW * cyc)
                        for t in range(TT):
                            for k in range(KC):
                                whi, wlo = half_parts(n + hf, KC, k)
                                ins = product(pe, bank[t][:, FFW * hf:FFW * (hf + 1)], hi[:, k, P * t:P * t + P], lo[:, k, P * t:P * t + P],
                                              whi, wlo, k == 0, k == KC - 1)
                        ins.then_inc(half_used, 1)

                def turn(m):
                    pe.wait_ge(d_rows, 2 * m + 3)
                    for t in range(TT):
                        for j in range(2):
                            ins = pe.transpose(bank[2][:, SEQ * j + P * t:SEQ * j + P * t + P],
                                               tok_c(rows)[:, t, P * j:P * j + P], ident[:, :])
                    ins.then_inc(d_turn, 1)

                def down(n, cyc, m):
                    pe.wait_ge(lo_ready, n + 1 + RAW * cyc)
                    pe.wait_ge(d_lo, m + 2)
                    for t in range(TT):
                        for j in range(2):
                            whi, wlo = half_parts(n, 2, j)
                            at = slice(SEQ * j + P * t, SEQ * j + P * t + P)
                            for hf in range(2):
                                cols = slice(CHUNK * hf, CHUNK * (hf + 1))
                                ins = product(pe, bank[4 + 2 * t + hf][:, :], ffT_hi[:, at], ffT_lo[:, at],
                                              whi[:, cols], wlo[:, cols], False, False)
                    ins.then_inc(half_used, 1)

                for b in range(4, 8):
                    pe.matmul(bank[b][:, :], zero_r[:, 0:P], zero_r[:, :], start=True, stop=False, skip_group_check=True)
                gate_up(n0, 0)
                turn(0)
                with pe.Fori(0, (FSTEPS - 1) // 2) as it:
                    for i in range(2):
                        m = 2 * it + 1 + i
                        gate_up(n0 + 2 + 3 * i, it)
                        down(n0 + 4 + 3 * i, it, m - 1)
                        turn(m)
                down(n0 + DENSE_HALVES - 1, 0, FSTEPS - 1)

            def experts():
                pe.wait_ge(hT_lo_ready, 16)
                pe.wait_ge(rtr_lo_ready, 1)
                hi, lo = k_tok(hT_hi), k_tok(hT_lo)
                for t in range(TT):
                    for k in range(KC):
                        e = slice(EXPERTS * k, EXPERTS * (k + 1))
                        ins = product(pe, bank[4][:, EXPERTS * t:EXPERTS * (t + 1)], hi[:, k, P * t:P * t + P],
                                      lo[:, k, P * t:P * t + P], rtr_hi[:, e], rtr_lo[:, e], k == 0, k == KC - 1)
                ins.then_inc(logits_ps, 1)
                pe.wait_ge(mask_ready, 1)
                pe.wait_ge(const_ready, 4)
                mask = rt[:, 6, :, :]
                for dst, terms in ((slice(0, 8), ((before, 0),)), (slice(8, 16), ((ones, 0), (before, 1))),
                                   (slice(16, 24), ((ones, 0), (ones, 1)))):
                    for i, (left, t) in enumerate(terms):
                        ins = pe.matmul(bank[5][:, dst], left[:, :], mask[:, t, :], start=i == 0, stop=i == len(terms) - 1)
                ins.then_inc(place_ps, 1)
                pe.wait_ge(route_ready, 1)
                blocks = pe.value_load(ctl_i[0:1, 0:1], min_val=EXPERTS, max_val=EXPERTS + SLOTS)

                def gather(g):
                    pe.wait_ge(pick_ready, 4 * g + 4)
                    for i, (src, k0, b) in enumerate(((hr_hi, 0, 6), (hr_hi, 4, 7), (hr_lo, 0, 3), (hr_lo, 4, 6))):
                        if i == 3:
                            pe.wait_ge(xg_act, 2 * g + 1)
                        for c in range(4):
                            for t in range(TT):
                                k = k0 + c
                                ins = pe.matmul(bank[b][:, P * c:P * c + P], src[:, t, P * k:P * k + P], pick_r[:, t, :],
                                                start=t == 0, stop=t == TT - 1)
                        ins.then_inc(gather_ps, 1)

                def up(n, cyc, b):
                    for hf in range(2):
                        pe.wait_ge(lo_ready, n + hf + 1 + RAW * cyc)
                        for c in range(4):
                            k = 4 * hf + c
                            whi, wlo = half_parts(n + hf, 4, c)
                            at = slice(P * k, P * k + P)
                            ins = product(pe, bank[b][:, :], xg_hi[:, at], xg_lo[:, at], whi, wlo, k == 0, k == KC - 1)
                        ins.then_inc(half_used, 1)

                def turn(b, m):
                    pe.wait_ge(e_rows, MSTEPS * b + m + 2)
                    for j in range(4):
                        ins = pe.transpose(bank[2][:, P * j:P * j + P], rows[:, P * j:P * j + P], ident[:, :])
                    ins.then_inc(e_turn, 1)

                def down(n, cyc, b, m):
                    pe.wait_ge(e_lo, MSTEPS * b + m + 2)
                    for i in range(2):
                        pe.wait_ge(lo_ready, n + i + 1 + RAW * cyc)
                        for j in range(2):
                            whi, wlo = half_parts(n + i, 2, j)
                            at = slice(P * (2 * i + j), P * (2 * i + j) + P)
                            for hf in range(2):
                                cols = slice(CHUNK * hf, CHUNK * (hf + 1))
                                ins = product(pe, bank[4 + hf][:, :], ffT_hi[:, at], ffT_lo[:, at],
                                              whi[:, cols], wlo[:, cols], False, False)
                        ins.then_inc(half_used, 1)

                def scatter(b, i):
                    t, hf = i // 2, i % 2
                    bk = (6, 7, 3, 6)[i]
                    if i == 3:
                        pe.wait_ge(x_add, 4 * b + 1)
                    cols = slice(CHUNK * hf, CHUNK * (hf + 1))
                    pe.matmul(bank[bk][:, :], spread_r[:, t, :], y_hi[:, cols], start=True, stop=False)
                    pe.matmul(bank[bk][:, :], spread_r[:, t, :], y_lo[:, cols], start=False,
                              stop=True).then_inc(scatter_ps, 1)

                def spread(b):
                    pe.wait_ge(x_add, 4 * b + 2)
                    for t in range(TT):
                        pe.transpose(bank[7][:, P * t:P * t + P], pick[:, t, :], ident[:, :])
                    for t in range(TT):
                        ins = pe.matmul(bank[7][:, SEQ:SEQ + 1], pick[:, t, :], gcol[:, t:t + 1],
                                        start=t == 0, stop=t == TT - 1)
                    ins.then_inc(spread_ps, 1)

                pe.wait_ge(hr_lo_ready, 2)
                pe.wait_ge(moe_init, 1)
                gather(0)
                with pe.Fori(0, blocks) as b:
                    c = CYCLES * b
                    pe.wait_ge(xg_act, 2 * b + 2)
                    pe.wait_ge(xg_dve, 2 * b + 2)
                    up(MOE0, c, 0)
                    up(MOE0 + 2, c, 1)
                    pe.wait_ge(y_lo_ready, 2 * b + 2)
                    for hf in range(2):
                        pe.matmul(bank[4 + hf][:, :], zero_r[:, 0:P], zero_r[:, :], start=True, stop=False,
                                  skip_group_check=True)
                    for i in range(3):
                        scatter(b, i)
                    turn(b, 0)
                    scatter(b, 3)
                    spread(b)
                    with pe.Fori(1, MSTEPS) as m:
                        cm = c + m - 1
                        up(MOE0 + 4, cm, 0)
                        up(MOE0 + 6, cm, 1)
                        down(MOE0 + 8, cm, b, m - 1)
                        turn(b, m)
                    pe.wait_ge(spread_ready, 2 * b + 3)
                    pe.wait_ge(x_add, 4 * b + 4)
                    gather(b + 1)
                    down(MOE0 + BLOCK_HALVES - 2, c, b, MSTEPS - 1)
                pe.wait_ge(y_lo_ready, 2 * blocks + 2)
                pe.wait_ge(xg_act, 2 * blocks + 2)
                pe.wait_ge(xg_dve, 2 * blocks + 2)
                for i in range(4):
                    scatter(blocks, i)

            pe.wait_ge(const_ready, 4)
            pe.wait_ge(conv_in, 16)
            n = DEPTH * 3 * KC
            pe.transpose(bank[0][:, 0:n], conv_rows[:, :], ident[0:n, 0:n]).then_inc(conv_ps, 1)
            norm_turn(0)
            mixer(0)
            norm_turn(1)
            dense()
            norm_turn(2)
            mixer(1)
            norm_turn(3)
            experts()


def bucket_lines():
    import numpy as np
    dist = SEQ - 1 - np.arange(LINE)
    exact = NBUCKETS // 2
    d = np.maximum(dist, 1).astype(np.float32)
    large = exact + (np.log(d / np.float32(exact)) / np.float32(math.log(128 / exact))
                     * np.float32(NBUCKETS - exact)).astype(np.int32)
    bucket = np.where(dist < exact, dist, np.minimum(large, NBUCKETS - 1))
    bucket = np.where(dist < 0, NBUCKETS, bucket)
    return (np.arange(NBUCKETS + 1)[:, None] == bucket[None, :]).astype(np.float32)


_INS = ["x", "rel_bias", "mix_norm_g", "w_in", "lam_qk", "subln_g", "conv_w", "w_o_attn", "w_o_conv", "w_o",
        "ffn_norm_g", "dense_w_gate_up", "dense_w_down", "router_w", "expert_w_gate_up", "expert_w_down",
        "final_norm_g"]


def kernel(**inputs):
    import numpy as np
    import concourse.bacc as bacc
    from concourse.bass_utils import run_bass_kernel_spmd as run

    nc = bacc.Bacc("TRN2", target_bir_lowering=False, num_devices=1, dynamic_dma_scratch_size=1024)
    arrays, args = {}, []
    for name in _INS:
        arrays[f"in_{name}"] = np.ascontiguousarray(inputs[name])
        args.append(nc.dram_tensor(f"in_{name}", arrays[f"in_{name}"].shape, F32, kind="ExternalInput").ap())
    arrays["bucket_of"] = bucket_lines()
    args.append(nc.dram_tensor("bucket_of", arrays["bucket_of"].shape, F32, kind="ExternalInput").ap())
    out = nc.dram_tensor("out", (1, SEQ, D), F32, kind="ExternalOutput").ap()
    build(nc, *args, out)
    return run(nc, [arrays], core_ids=[0]).results[0]["out"]
```

```python
import math
from contextlib import ExitStack

import concourse.bass as bass
from concourse import mybir

P = 128
F32 = mybir.dt.float32
F32R = mybir.dt.float32r
I32 = mybir.dt.int32
ALU = mybir.AluOpType
ACT = mybir.ActivationFunctionType
AX = mybir.AxisListType.X

D = 1024
SEQ = 256
TT = SEQ // P
KC = D // P
HEADS = 8
HD = 64
NBUCKETS = 32
EPS = 1e-6
DEPTH = 2
FF = 2816
FE = 3584
EXPERTS = 8
CHUNK = 512
HALF = 2048
RAW = 6
SPLIT = 3
FFW = 256
FSTEPS = FF // FFW
MSTEPS = FE // CHUNK
SLOTS = 3
COLS = EXPERTS + SLOTS + 1
LINE = 384
BIG = 1e30

MIX_HALVES = 44
DENSE_HALVES = 3 * FSTEPS
BLOCK_HALVES = 6 * MSTEPS
CYCLES = BLOCK_HALVES // RAW
MIX0 = (0, MIX_HALVES + DENSE_HALVES)
DENSE0 = MIX_HALVES
MOE0 = 2 * MIX_HALVES + DENSE_HALVES

UNIT = [("q", 0), ("k", 0), ("v", 0), ("q", 1), ("k", 1), ("v", 1), ("ch", 0), ("cc", 0), ("cb", 0),
        ("ch", 1), ("cc", 1), ("cb", 1), ("ga", 0), ("ga", 1), ("gc", 0), ("gc", 1),
        ("conv", 0), ("conv", 1), ("attn", 0), ("attn", 1), ("wo", 0), ("wo", 1)]
UNITS = len(UNIT)
W_IN_COL = {"q": 0, "k": D, "v": 2 * D, "ch": 3 * D, "cb": 4 * D, "cc": 5 * D, "ga": 6 * D, "gc": 7 * D}
S_CONV, S_ATTN, S_WO = (2 * UNIT.index((kind, 0)) for kind in ("conv", "attn", "wo"))


def unit_of(s):
    return (s // 2, s % 2) if s < S_WO else (UNITS - 2 + s % 2, (s - S_WO) // 2)


def last_half(u):
    return 2 * u + 1 if u < UNITS - 2 else MIX_HALVES - UNITS + u


def mixer_jobs():
    jobs = {s: [] for s in range(MIX_HALVES + 1)}
    for h in range(HEADS):
        a = 8 + 3 * h
        jobs[a].append(("scores", h))
        jobs[a + 1].append(("turn_w", h))
        jobs[a + 2].append(("values", h))
        jobs[a + 4].append(("turn_a", h))
    for s in jobs:
        jobs[s].sort(key=lambda j: ["scores", "turn_a", "values", "turn_w"].index(j[0]))
    for s, job in {2: ("turn_qk", 0), 4: ("turn_qk", 1), 8: ("turn_qk", 2), 11: ("turn_qk", 3),
                   17: ("turn_u", 0), 20: ("turn_b", 0), 23: ("turn_u", 1), 26: ("turn_b", 1),
                   38: ("turn_m", 0), 40: ("turn_m", 1)}.items():
        jobs[s].append(job)
    return jobs


JOBS = mixer_jobs()
JOB_BANKS = {"scores": (4, 5), "turn_w": (6,), "values": (7,), "turn_a": (7,),
             "turn_qk": (6, 7), "turn_u": (6, 7), "turn_b": (6, 7), "turn_m": (6, 7)}
TURNS_OF_ROWS = ("turn_qk", "turn_u", "turn_b")


def count_bank_uses():
    uses, last, at, before_it = {b: 0 for b in (4, 5, 6, 7)}, {}, {}, {}
    for s in range(MIX_HALVES):
        for job in JOBS[s]:
            for b in JOB_BANKS[job[0]]:
                uses[b] += 1
                at[job, b] = uses[b]
                before_it[job, b] = last.get(b)
                last[b] = job
    return at, before_it, uses, last


BANK_AT, JOB_BEFORE, BANK_USES, LAST_JOB = count_bank_uses()
ROW_UNITS = [("q", 0), ("k", 0), ("q", 1), ("k", 1), ("cb", 0), ("cb", 1)]
ACT_ROWS = {(layer, u): 2 * (6 * layer + i + 1) for layer in range(DEPTH) for i, u in enumerate(ROW_UNITS)}
X_ADDS = {1: 4, 2: 8, 3: 12}


def lambda_init(layer):
    return 0.8 - 0.6 * math.exp(-0.3 * layer)


def build(nc, x, rel_bias, mix_norm_g, w_in, lam_qk, subln_g, conv_w, w_o_attn, w_o_conv, w_o,
          ffn_norm_g, dense_gu, dense_down, router_w, expert_gu, expert_down, final_norm_g,
          bucket_of, out):
    lines = nc.dram_tensor("bias_lines", (HEADS, P, LINE), F32, kind="Internal").ap()
    with ExitStack() as ctx:
        def sb(name, shape, dt=F32):
            return ctx.enter_context(nc.sbuf_tensor(name, shape, dt))

        def sem(name):
            return ctx.enter_context(nc.semaphore(name))

        w_raw = sb("w_raw", [P, RAW, HALF])
        w_hi = sb("w_hi", [P, SPLIT, HALF], F32R)
        w_lo = sb("w_lo", [P, SPLIT, HALF], F32R)
        X = sb("X", [P, TT, D])
        hT_hi = sb("hT_hi", [P, KC * SEQ], F32R)
        hT_lo = sb("hT_lo", [P, KC * SEQ], F32R)
        q_buf = sb("q_buf", [P, KC * SEQ])
        k_buf = sb("k_buf", [P, KC * SEQ])
        v_buf = sb("v_buf", [P, KC * SEQ])
        aT_hi = sb("aT_hi", [P, KC * SEQ], F32R)
        aT_lo = sb("aT_lo", [P, KC * SEQ], F32R)
        cT_hi = sb("cT_hi", [P, KC * SEQ], F32R)
        cT_lo = sb("cT_lo", [P, KC * SEQ], F32R)
        rows = sb("rows", [P, TT * CHUNK])
        part = sb("part", [P, TT * CHUNK])
        uT = sb("uT", [P, 4, SEQ + 2])
        yT = sb("yT", [P, KC * P])
        prob = sb("prob", [P, 2, LINE])
        wgt = sb("wgt", [P, LINE])
        wgtT = sb("wgtT", [P, LINE])
        arow = sb("arow", [P, TT, P])
        squares = sb("squares", [P, TT, P])
        bias = sb("bias", [P, HEADS, LINE])
        ident = sb("ident", [P, P])
        before = sb("before", [P, P])
        ones = sb("ones", [P, P])
        iota_1 = sb("iota_1", [P, P])
        zero_r = sb("zero_r", [P, CHUNK], F32R)
        relb = sb("relb", [64, HEADS])
        relb_bc = sb("relb_bc", [64, P])
        gsub = sb("gsub", [P, DEPTH, P])
        conv_rows = sb("conv_rows", [DEPTH * 3 * KC, P])
        convT = sb("convT", [P, DEPTH, 3, KC])
        lam4 = sb("lam4", [P, 2, DEPTH])
        neg_lam = sb("neg_lam", [P, DEPTH])
        nmax = sb("nmax", [P, 4])
        psum_row = sb("psum_row", [P, 4])
        recip = sb("recip", [P, 4])
        ssq = sb("ssq", [P, 2])
        nw = [sb(f"nw{i}", [P, 2]) for i in range(2)]
        nwi = sb("nwi", [P, 2], I32)
        head_ss = sb("head_ss", [P, 2])
        head_nw = [sb(f"head_nw{i}", [P, 2]) for i in range(2)]
        head_nwi = sb("head_nwi", [P, 2], I32)
        rtr = sb("rtr", [P, KC * EXPERTS])
        rtr_hi = sb("rtr_hi", [P, KC * EXPERTS], F32R)
        rtr_lo = sb("rtr_lo", [P, KC * EXPERTS], F32R)
        beats = sb("beats", [P, TT, EXPERTS, EXPERTS])
        ties = sb("ties", [P, TT, EXPERTS, EXPERTS])
        earlier = sb("earlier", [P, EXPERTS, EXPERTS])
        rank = sb("rank", [P, TT, EXPERTS])
        chosen = sb("chosen", [P, 2, TT, EXPERTS])
        picked = sb("picked", [P, 2, TT, EXPERTS])
        mask = sb("mask", [P, TT, EXPERTS])
        first = sb("first", [P, TT, EXPERTS])
        beyond = sb("beyond", [P, TT, EXPERTS])
        top = sb("top", [P, 2, TT])
        gap = sb("gap", [P, TT])
        places = sb("places", [P, 3, EXPERTS])
        over = sb("over", [P, EXPERTS])
        count_a = sb("count_a", [P, EXPERTS])
        count_b = sb("count_b", [P, EXPERTS])
        slot_no = sb("slot_no", [P, SLOTS, EXPERTS])
        slot_of = sb("slot_of", [P, SLOTS, EXPERTS])
        src = sb("src", [P, 5, EXPERTS])
        terms = sb("terms", [P, 5, SLOTS, EXPERTS])
        found = sb("found", [P, 5, SLOTS])
        seats = sb("seats", [P, 2 * TT, COLS])
        seat = sb("seat", [P, 2 * TT])
        ctl = sb("ctl", [P, 4])
        ctl_i = sb("ctl_i", [P, 4], I32)
        gate = sb("gate", [P, 1])

        bank = [ctx.enter_context(nc.psum_tensor(f"bank{b}", [P, CHUNK], F32)) for b in range(8)]

        def k_tok(buf):
            return buf[:, :].rearrange("p (k t) -> p k t", t=SEQ)

        def tok_d(buf):
            return buf[:, :].rearrange("p (t d) -> p t d", t=TT)

        def tok_c(buf):
            return buf[:, :].rearrange("p (t c) -> p t c", t=TT)

        def quad(ap):
            return ap.rearrange("p (c n) -> p c n", n=P)

        hrow, merged = tok_d(q_buf), tok_d(k_buf)
        qT, kT = k_tok(q_buf), k_tok(k_buf)
        v_rows, sig_conv = tok_d(v_buf), tok_d(k_buf)
        sig_attn = (tok_c(part), tok_c(rows))
        gain = yT[:, :]
        yTv = yT[:, :].rearrange("p (c t) -> p c t", t=SEQ)
        lamq = rows[:, 0:DEPTH * 4 * HD].rearrange("p (l i d) -> p l i d", l=DEPTH, i=4)
        ffT_hi, ffT_lo = cT_hi[:, 0:CHUNK], cT_lo[:, 0:CHUNK]
        y_hi, y_lo = cT_hi[:, CHUNK:CHUNK + D], cT_lo[:, CHUNK:CHUNK + D]
        pick_r = cT_hi[:, 1536:1792].rearrange("p (t j) -> p t j", t=TT)
        spread_r = cT_hi[:, 1792:2048].rearrange("p (t j) -> p t j", t=TT)
        pick = prob[:, 0, 0:256].rearrange("p (t j) -> p t j", t=TT)
        xg_hi, xg_lo = hT_hi[:, 0:D], hT_lo[:, 0:D]
        hr_hi, hr_lo = tok_d(aT_hi), tok_d(aT_lo)

        x_in, relb_in, bucket_in, lam_in, sub_in, conv_in, rtr_in, gain_in = (
            sem(n) for n in ("x_in", "relb_in", "bucket_in", "lam_in", "sub_in", "conv_in", "rtr_in", "gain_in"))
        line_out, bias_in, out_sent = sem("line_out"), sem("bias_in"), sem("out_sent")
        landed = [sem(f"landed{i}") for i in range(RAW)]
        hi_ready, lo_ready, half_used = sem("hi_ready"), sem("lo_ready"), sem("half_used")
        bank_full = {b: sem(f"bank_full{b}") for b in (4, 5, 6, 7)}
        const_ready = sem("const_ready")
        conv_ps = sem("conv_ps")
        line_ps, line_sb, relb_ready = sem("line_ps"), sem("line_sb"), sem("relb_ready")
        gsub_ready, scaled = sem("gsub_ready"), sem("scaled")
        lam_sums, lam_exp = sem("lam_sums"), sem("lam_exp")
        dve_step = sem("dve_step")
        pool_step = sem("pool_step")
        x_new = sem("x_new")
        ss_ready, hrow_ready, norm_ps = sem("ss_ready"), sem("hrow_ready"), sem("norm_ps")
        hT_hi_ready, hT_lo_ready = sem("hT_hi_ready"), sem("hT_lo_ready")
        act_rows, dve_rows = sem("act_rows"), sem("dve_rows")
        qk_ready, v_ready, ch_ready = sem("qk_ready"), sem("v_ready"), sem("ch_ready")
        biased, exp_ready, wgt_ready, wgtT_ready = sem("biased"), sem("exp_ready"), sem("wgt_ready"), sem("wgtT_ready")
        o_ss, o_out, arow_ready, aT_hi_ready, aT_lo_ready = sem("o_ss"), sem("o_out"), sem("arow_ready"), sem("aT_hi_ready"), sem("aT_lo_ready")
        merged_attn, merged_conv, merged_ready = sem("merged_attn"), sem("merged_conv"), sem("merged_ready")
        uT_ready, tap_ready, yT_ready, c_ready = sem("uT_ready"), sem("tap_ready"), sem("yT_ready"), sem("c_ready")
        cT_hi_ready, cT_lo_ready = sem("cT_hi_ready"), sem("cT_lo_ready")
        sig_ready, mT_hi_ready, mT_lo_ready = sem("sig_ready"), sem("mT_hi_ready"), sem("mT_lo_ready")
        d_silu, d_rows, d_turn, d_hi, d_lo = sem("d_silu"), sem("d_rows"), sem("d_turn"), sem("d_hi"), sem("d_lo")
        rtr_hi_ready, rtr_lo_ready, hr_hi_ready, hr_lo_ready = (
            sem("rtr_hi_ready"), sem("rtr_lo_ready"), sem("hr_hi_ready"), sem("hr_lo_ready"))
        logits_ps, gap_ready, gap_exp, mask_ready, place_ps = (
            sem("logits_ps"), sem("gap_ready"), sem("gap_exp"), sem("mask_ready"), sem("place_ps"))
        rank_ready, places_out, first_ready, seats_ready, gates_ready = (
            sem("rank_ready"), sem("places_out"), sem("first_ready"), sem("seats_ready"), sem("gates_ready"))
        route_ready, moe_init = sem("route_ready"), sem("moe_init")
        e_silu, e_rows, e_turn, e_hi, e_lo = sem("e_silu"), sem("e_rows"), sem("e_turn"), sem("e_hi"), sem("e_lo")
        y_hi_ready, y_lo_ready, scatter_ps, x_add = sem("y_hi_ready"), sem("y_lo_ready"), sem("scatter_ps"), sem("x_add")
        pick_r_ready, pick_ready = sem("pick_r_ready"), sem("pick_ready")
        spread_ps, spread_ready = sem("spread_ps"), sem("spread_ready")
        gather_ps, xg_act, xg_dve = sem("gather_ps"), sem("xg_act"), sem("xg_dve")
        col_ready, moe_step = sem("col_ready"), sem("moe_step")

        def load_half(sp, n, src, cyc=0):
            if n >= RAW:
                sp.wait_ge(lo_ready, n - RAW + 1 + RAW * cyc)
            dst = w_raw[:, n % RAW, :]
            sp.dma_start(dst.rearrange("p (a b) -> p a b", a=src.shape[1]), src).then_inc(landed[n % RAW], 16)

        def split_hi(act, n, cyc=0):
            act.wait_ge(landed[n % RAW], 16 * (n // RAW + 1) + 16 * cyc)
            if n >= SPLIT:
                act.wait_ge(half_used, n - SPLIT + 1 + RAW * cyc)
            act.activation(w_hi[:, n % SPLIT, :], w_raw[:, n % RAW, :], ACT.Copy).then_inc(hi_ready, 1)

        def split_lo(dve, n, cyc=0):
            dve.wait_ge(hi_ready, n + 1 + RAW * cyc)
            dve.tensor_tensor(w_lo[:, n % SPLIT, :], w_raw[:, n % RAW, :], w_hi[:, n % SPLIT, :],
                              ALU.subtract).then_inc(lo_ready, 1)

        def product(pe, dst, hi, lo, whi, wlo, first, last):
            pe.matmul(dst, hi, whi, start=first, stop=False, skip_group_check=True)
            pe.matmul(dst, hi, wlo, start=False, stop=False, skip_group_check=True)
            return pe.matmul(dst, lo, whi, start=False, stop=last, skip_group_check=True)

        def half_parts(n, rows_, c):
            a = w_hi[:, n % SPLIT, :].rearrange("p (k c) -> p k c", k=rows_)[:, c]
            b = w_lo[:, n % SPLIT, :].rearrange("p (k c) -> p k c", k=rows_)[:, c]
            return a, b

        def unit_out(eng, layer, u):
            kind, i = UNIT[u]
            if kind in ("q", "k", "cb"):
                eng.wait_ge(act_rows, ACT_ROWS[layer, (kind, i)])
            else:
                ready, per_layer = {"v": (v_ready, 4), "ch": (ch_ready, 4), "cc": (dve_rows, 4),
                                    "ga": (sig_ready, 8), "gc": (sig_ready, 8), "conv": (merged_conv, 4),
                                    "attn": (merged_attn, 4), "wo": (x_new, 8)}[kind]
                eng.wait_ge(ready, per_layer * layer + 2 * i + (6 if kind == "gc" else 2))

        def job_out(eng, layer, job):
            kind, i = job
            head, both = HEADS * layer + i, 2 * layer + i
            if kind == "scores":
                eng.wait_ge(biased, head + 1)
            elif kind == "turn_w":
                eng.wait_ge(wgtT_ready, head + 1)
            elif kind == "values":
                eng.wait_ge(o_out, head + 1)
            elif kind == "turn_a":
                eng.wait_ge(aT_lo_ready, head + 1)
            elif kind == "turn_qk":
                eng.wait_ge(qk_ready, 2 * (4 * layer + i) + 2)
            elif kind == "turn_u":
                eng.wait_ge(uT_ready, 2 * both + 2)
            elif kind == "turn_b":
                eng.wait_ge(c_ready, 2 * both + 2)
            else:
                eng.wait_ge(mT_lo_ready, 2 * both + 2)

        def job_in_bank(eng, layer, job, b):
            eng.wait_ge(bank_full[b], BANK_USES[b] * layer + BANK_AT[job, b])

        def rows_turned(eng, layer, s):
            past = [j for t in range(s) for j in JOBS[t] if j[0] in TURNS_OF_ROWS]
            if past:
                job_in_bank(eng, layer, past[-1], 7)

        def cols_of(w, c0, hf):
            return w.rearrange("(k p) n -> p k n", p=P)[:, 4 * hf:4 * hf + 4, c0:c0 + CHUNK]

        def mixer_source(layer, s):
            u, hf = unit_of(s)
            kind, i = UNIT[u]
            if kind in W_IN_COL:
                return cols_of(w_in[layer], W_IN_COL[kind] + CHUNK * i, hf)
            return cols_of({"conv": w_o_conv, "attn": w_o_attn, "wo": w_o}[kind][layer], CHUNK * i, hf)

        gu_view = dense_gu[0].rearrange("(k p) (two n) -> p k two n", p=P, two=2)
        down_view = dense_down[0].rearrange("(j p) n -> p j n", p=P)

        def bank_quads(b):
            return bank[b][:, :].rearrange("p (c n) -> p c n", n=P)

        block = ctx.enter_context(nc.Block())

        @block.sync
        def _(sp):
            sp.dma_start(X[:, :, :],
                         x.rearrange("a (t p) d -> p (a t) d", p=P)).then_inc(x_in, 16)
            sp.dma_start(gain, mix_norm_g[0].partition_broadcast(P)).then_inc(gain_in, 16)
            load_half(sp, 0, mixer_source(0, 0))
            load_half(sp, 1, mixer_source(0, 1))
            sp.dma_start(relb[0:NBUCKETS, :], rel_bias).then_inc(relb_in, 16)
            sp.dma_start(w_raw[0:NBUCKETS + 1, RAW - 1, 0:LINE], bucket_of).then_inc(bucket_in, 16)
            sp.dma_start(rows[:, 0:DEPTH * 4 * HD],
                         lam_qk.rearrange("l i d -> (l i d)").partition_broadcast(P)).then_inc(lam_in, 16)
            sp.dma_start(gsub[:, :, :].rearrange("p l e -> p (l e)"),
                         subln_g.rearrange("l e -> (l e)").partition_broadcast(P)).then_inc(sub_in, 16)
            sp.dma_start(conv_rows[:, :], conv_w.rearrange("l w (c p) -> (l w c) p", p=P)).then_inc(conv_in, 16)
            for s in range(2, RAW - 1):
                load_half(sp, s, mixer_source(0, s))
            for h in range(HEADS):
                sp.wait_ge(line_sb, h + 1)
                sp.dma_start(lines[h], bias[:, h, :]).then_inc(line_out, 16)
            sp.wait_ge(line_out, 16 * HEADS)
            for h in range(HEADS):
                for c0, j0, n in ((0, 255, P), (P, 127, 2 * P)):
                    sp.dma_start(bias[:, h, c0:c0 + n],
                                 bass.AP(tensor=lines.tensor, offset=h * P * LINE + j0,
                                         ap=[[LINE - 1, P], [1, n]])).then_inc(bias_in, 16)
            sp.wait_ge(line_ps, HEADS)
            for s in range(RAW - 1, MIX_HALVES):
                load_half(sp, s, mixer_source(0, s))
            n = DENSE0
            for hf in range(2):
                load_half(sp, n + hf, gu_view[:, :, hf, 0:FFW])
            with sp.Fori(0, (FSTEPS - 1) // 2) as it:
                for i in range(2):
                    m = 2 * it + 1 + i
                    for hf in range(2):
                        load_half(sp, n + 2 + 3 * i + hf, gu_view[:, :, hf, bass.ds(FFW * m, FFW)], it)
                    load_half(sp, n + 4 + 3 * i, down_view[:, bass.ds(2 * (m - 1), 2), :], it)
            load_half(sp, n + DENSE_HALVES - 1, down_view[:, 2 * (FSTEPS - 1):2 * FSTEPS, :])
            for s in range(MIX_HALVES):
                load_half(sp, MIX0[1] + s, mixer_source(1, s))

            def stream_expert(e, b):
                gu = expert_gu[0, e].rearrange("(k p) (two n) -> p k two n", p=P, two=2)
                down = expert_down[0, e].rearrange("(j p) n -> p j n", p=P)
                for i in range(4):
                    load_half(sp, MOE0 + i, gu[:, 4 * (i % 2):4 * (i % 2) + 4, i // 2, 0:CHUNK], CYCLES * b)
                with sp.Fori(1, MSTEPS) as m:
                    cyc = CYCLES * b + m - 1
                    for i in range(4):
                        load_half(sp, MOE0 + 4 + i,
                                  gu[:, 4 * (i % 2):4 * (i % 2) + 4, i // 2, bass.ds(CHUNK * m, CHUNK)], cyc)
                    for i in range(2):
                        load_half(sp, MOE0 + 8 + i, down[:, bass.ds(4 * (m - 1) + 2 * i, 2), :], cyc)
                for i in range(2):
                    j = 4 * (MSTEPS - 1) + 2 * i
                    load_half(sp, MOE0 + BLOCK_HALVES - 2 + i, down[:, j:j + 2, :], CYCLES * b)

            with sp.Fori(0, EXPERTS) as b:
                stream_expert(b, b)
            sp.wait_ge(route_ready, 1)
            blocks = sp.value_load(ctl_i[0:1, 0:1], min_val=EXPERTS, max_val=EXPERTS + SLOTS)
            with sp.If(blocks > EXPERTS):
                with sp.Fori(EXPERTS, blocks) as b:
                    e = sp.value_load(ctl_i[0:1, bass.ds(b - (EXPERTS - 1), 1)], min_val=0, max_val=EXPERTS - 1)
                    stream_expert(e, b)
            sp.wait_ge(hrow_ready, 2 * 5)
            sp.dma_start(out.rearrange("a (t p) d -> p (a t) d", p=P), hrow).then_inc(out_sent, 16)
            sp.wait_ge(out_sent, 16)

        @block.gpsimd
        def _(pool):
            pool.memset(ident[:, :], 0.0).then_inc(pool_step, 1)
            pool.memset(ones[:, :], 1.0).then_inc(pool_step, 1)
            pool.memset(uT[:, :, :], 0.0).then_inc(pool_step, 1)
            pool.wait_ge(pool_step, 3)
            pool.affine_select(out=ident[:, :], in_=ident[:, :], compare_op=ALU.not_equal, fill=1.0, base=0,
                               pattern=[[-1, P]], channel_multiplier=1).then_inc(const_ready, 1)
            pool.affine_select(out=before[:, :], in_=ones[:, :], compare_op=ALU.is_gt, fill=0.0, base=0,
                               pattern=[[1, P]], channel_multiplier=-1).then_inc(const_ready, 1)
            pool.iota(iota_1[:, :], pattern=[[1, P]], base=1, channel_multiplier=0,
                      allow_small_or_imprecise_dtypes=True).then_inc(const_ready, 1)
            pool.affine_select(out=earlier[:, :, :], in_=ones[:, 0:EXPERTS * EXPERTS].rearrange("p (e j) -> p e j", e=EXPERTS),
                               compare_op=ALU.is_gt, fill=0.0, base=0,
                               pattern=[[1, EXPERTS], [-1, EXPERTS]], channel_multiplier=0).then_inc(const_ready, 1)

            count = [3]

            def chain(ins):
                count[0] += 1
                ins.then_inc(pool_step, 1)
                pool.wait_ge(pool_step, count[0])

            for i in range(SLOTS):
                chain(pool.memset(slot_no[:, i, :], float(i)))
            chain(pool.iota(src[:, 0, :], pattern=[[1, EXPERTS]], base=0, channel_multiplier=0,
                            allow_small_or_imprecise_dtypes=True))
            chain(pool.memset(seats[:, :, EXPERTS:COLS], 0.0))
            chain(pool.memset(ctl[:, :], 0.0))

            pool.wait_ge(gsub_ready, 1)
            v, t_, y = head_nw[0][:, :], head_nw[1][:, :], head_nwi[:, :].bitcast(F32)
            for head in range(DEPTH * HEADS):
                pool.wait_ge(o_ss, 2 * head + 2)
                chain(pool.tensor_scalar(v, head_ss[:, :], 1.0 / P, EPS, ALU.mult, ALU.add))
                chain(pool.tensor_scalar(head_nwi[:, :], v.bitcast(I32), -0.5, float(0x5F3759DF), ALU.mult, ALU.add))
                chain(pool.tensor_scalar(v, v, -0.5, None, ALU.mult))
                for _ in range(3):
                    chain(pool.tensor_tensor(t_, y, y, ALU.mult))
                    chain(pool.tensor_tensor(t_, t_, v, ALU.mult))
                    chain(pool.tensor_scalar(t_, t_, 1.5, None, ALU.add))
                    chain(pool.tensor_tensor(y, t_, y, ALU.mult))
                pool.wait_ge(o_out, head + 1)
                for t in range(TT):
                    pool.tensor_scalar(arow[:, t, :], arow[:, t, :], y[:, t:t + 1], None, ALU.mult).then_inc(scaled, 1)
                for t in range(TT):
                    pool.wait_ge(scaled, 2 * head + t + 1)
                    pool.tensor_tensor(arow[:, t, :], arow[:, t, :], gsub[:, head // HEADS, :],
                                       ALU.mult).then_inc(arow_ready, 1)

            for t in range(TT):
                pool.wait_ge(hr_hi_ready, t + 1)
                pool.tensor_tensor(hr_lo[:, t, :], hrow[:, t, :], hr_hi[:, t, :], ALU.subtract).then_inc(hr_lo_ready, 1)

            pool.wait_ge(places_out, 1)
            chain(pool.tensor_scalar(over[:, :], places[:, 2, :], float(P), None, ALU.is_gt))
            a, b = over, count_a
            for step in (1, 2, 4):
                chain(pool.tensor_copy(b[:, 0:step], a[:, 0:step]))
                chain(pool.tensor_tensor(b[:, step:EXPERTS], a[:, step:EXPERTS], a[:, 0:EXPERTS - step], ALU.add))
                a, b = b, (count_b if b is count_a else count_a)
            chain(pool.tensor_scalar(ctl[:, 0:1], a[:, EXPERTS - 1:EXPERTS], float(EXPERTS), None, ALU.add))
            chain(pool.tensor_tensor(b[:, :], a[:, :], over[:, :], ALU.subtract))
            chain(pool.tensor_tensor(slot_of[:, :, :], slot_no[:, :, :],
                                     b[:, :].unsqueeze(1).to_broadcast([P, SLOTS, EXPERTS]), ALU.subtract))
            chain(pool.tensor_scalar(slot_of[:, :, :], slot_of[:, :, :], 0.0, None, ALU.is_equal))
            chain(pool.tensor_tensor(slot_of[:, :, :], slot_of[:, :, :],
                                     over[:, :].unsqueeze(1).to_broadcast([P, SLOTS, EXPERTS]), ALU.mult))
            pool.wait_ge(first_ready, 1)
            chain(pool.tensor_tensor(beyond[:, :, :], mask[:, :, :], first[:, :, :], ALU.subtract))
            chain(pool.tensor_scalar(src[:, 1:3, :], places[:, 0:2, :], float(P - 1), None, ALU.subtract))
            chain(pool.tensor_tensor(src[:, 1:3, :], src[:, 1:3, :], beyond[:, :, :], ALU.mult))
            pool.wait_ge(gates_ready, 1)
            chain(pool.tensor_copy(src[:, 3:5, :], seats[:, TT:2 * TT, 0:EXPERTS]))
            for i in range(SLOTS):
                chain(pool.tensor_tensor(terms[:, :, i, :], src[:, :, :],
                                         slot_of[:, i:i + 1, :].to_broadcast([P, 5, EXPERTS]), ALU.mult))
            for n in (4, 2):
                chain(pool.tensor_tensor(terms[:, :, :, 0:n], terms[:, :, :, 0:n], terms[:, :, :, n:2 * n], ALU.add))
            chain(pool.tensor_tensor(found[:, :, :], terms[:, :, :, 0], terms[:, :, :, 1], ALU.add))
            chain(pool.tensor_copy(seats[:, :, EXPERTS:EXPERTS + SLOTS], found[:, 1:5, :]))
            chain(pool.tensor_copy(ctl[:, 1:1 + SLOTS], found[:, 0, :]))
            pool.tensor_copy(ctl_i[:, :], ctl[:, :]).then_inc(route_ready, 1)

        @block.scalar
        def _(act):
            for h in range(HEADS):
                act.wait_ge(line_ps, h + 1)
                act.activation(bias[:, h, :], bank[4 + h % 4][:, 0:LINE], ACT.Copy).then_inc(line_sb, 1)
            act.wait_ge(lam_sums, 1)
            act.activation(lam4[:, :, :], lam4[:, :, :], ACT.Exp).then_inc(lam_exp, 1)

            def norm_sums(q):
                if q == 0:
                    act.wait_ge(x_in, 16)
                else:
                    act.wait_ge(x_new, X_ADDS[q])
                    act.wait_ge(hrow_ready, 2 * q)
                for t in range(TT):
                    act.activation(part[:, :], X[:, t, :], ACT.Square,
                                   accum_out=ssq[:, t:t + 1]).then_inc(ss_ready, 1)
                    act.wait_ge(ss_ready, 2 * q + t + 1)

            def norm_hi(q):
                for t in range(TT):
                    for g in range(2):
                        act.wait_ge(norm_ps, 4 * q + 2 * t + g + 1)
                        act.activation(k_tok(hT_hi)[:, 4 * g:4 * g + 4, P * t:P * t + P],
                                       bank_quads(2 * t + g), ACT.Copy).then_inc(hT_hi_ready, 1)

            def next_gain(q, source):
                act.wait_ge(hrow_ready, 2 * q)
                act.wait_ge(cT_lo_ready, q + 1)
                act.dma_start(gain, source.partition_broadcast(P)).then_inc(gain_in, 16)

            def mixer(layer):
                n0 = MIX0[layer]
                for s in range(MIX_HALVES + 1):
                    if s < MIX_HALVES:
                        split_hi(act, n0 + s + 2)
                    if s == 38 and layer == 1:
                        act.wait_ge(rtr_in, 16)
                        act.activation(rtr_hi[:, :], rtr[:, :], ACT.Copy).then_inc(rtr_hi_ready, 1)
                    if s == 30 and layer == 0:
                        next_gain(1, ffn_norm_g[0])
                    if s == 30 and layer == 1:
                        next_gain(3, ffn_norm_g[1])
                        act.dma_start(rtr[:, :].rearrange("p (k e) -> p k e", e=EXPERTS),
                                      router_w[0].rearrange("(k p) e -> p k e", p=P)).then_inc(rtr_in, 16)
                    for u in range(UNITS):
                        if last_half(u) != s - 1:
                            continue
                        banks = [bank[2 * (u % 2) + t] for t in range(TT)]
                        kind, i = UNIT[u]
                        if kind in ("conv", "attn", "wo"):
                            continue
                        if kind != "cc":
                            act.wait_ge(half_used, n0 + s)
                        if kind in ("q", "k", "cb"):
                            rows_turned(act, layer, s)
                            for t in range(TT):
                                act.activation(tok_c(rows)[:, t], banks[t][:, :], ACT.Copy,
                                               scale=HD ** -0.5 if kind == "q" else 1.0).then_inc(act_rows, 1)
                        if kind == "v":
                            for t in range(TT):
                                act.activation(v_rows[:, t, CHUNK * i:CHUNK * (i + 1)], banks[t][:, :],
                                               ACT.Copy).then_inc(v_ready, 1)
                        if kind == "ch":
                            for t in range(TT):
                                act.activation(tok_c(part)[:, t], banks[t][:, :], ACT.Copy).then_inc(ch_ready, 1)
                        if kind == "ga":
                            if i:
                                rows_turned(act, layer, s)
                            for t in range(TT):
                                act.activation(sig_attn[i][:, t], banks[t][:, :], ACT.Sigmoid).then_inc(sig_ready, 1)
                        if kind == "gc":
                            if i == 0:
                                job_in_bank(act, layer, ("scores", HEADS - 1), 5)
                            for t in range(TT):
                                act.activation(sig_conv[:, t, CHUNK * i:CHUNK * (i + 1)], banks[t][:, :],
                                               ACT.Sigmoid).then_inc(sig_ready, 1)
                    for kind, i in JOBS[s - 1] if s else []:
                        def full(b):
                            job_in_bank(act, layer, (kind, i), b)
                        if kind == "scores":
                            act.wait_ge(biased, HEADS * layer + i + 1)
                            for t, c0, c1 in ((0, 0, P), (1, P, LINE)):
                                for m in range(2):
                                    act.activation(prob[:, m, c0:c1], prob[:, m, c0:c1], ACT.Exp,
                                                   bias=nmax[:, 2 * t + m:2 * t + m + 1],
                                                   accum_out=psum_row[:, 2 * t + m:2 * t + m + 1]).then_inc(exp_ready, 1)
                        if kind == "turn_w":
                            full(6)
                            if i or layer:
                                pl, ph = (layer, i - 1) if i else (layer - 1, HEADS - 1)
                                job_in_bank(act, pl, ("values", ph), 7)
                            act.activation(wgtT[:, :], bank[6][:, 0:LINE], ACT.Copy).then_inc(wgtT_ready, 1)
                        if kind == "values":
                            full(7)
                            if i or layer:
                                pl, ph = (layer, i - 1) if i else (layer - 1, HEADS - 1)
                                job_in_bank(act, pl, ("turn_a", ph), 7)
                            for t in range(TT):
                                act.activation(squares[:, t, :], bank[7][:, P * t:P * t + P], ACT.Square,
                                               accum_out=head_ss[:, t:t + 1]).then_inc(o_ss, 1)
                            act.activation(arow[:, :, :].rearrange("p t e -> p (t e)"), bank[7][:, 0:SEQ],
                                           ACT.Copy).then_inc(o_out, 1)
                        if kind == "turn_a":
                            full(7)
                            act.activation(k_tok(aT_hi)[:, i, :], bank[7][:, 0:SEQ], ACT.Copy).then_inc(aT_hi_ready, 1)
                        if kind == "turn_qk":
                            buf = kT if i % 2 else qT
                            for t in range(TT):
                                full(6 + t)
                                act.activation(buf[:, 4 * (i // 2):4 * (i // 2) + 4, P * t:P * t + P],
                                               bank_quads(6 + t), ACT.Copy).then_inc(qk_ready, 1)
                        if kind == "turn_u":
                            if i or layer:
                                act.wait_ge(yT_ready, 4 * (2 * layer + i))
                            for t in range(TT):
                                full(6 + t)
                                act.activation(uT[:, :, 2 + P * t:2 + P * t + P], bank_quads(6 + t),
                                               ACT.Copy).then_inc(uT_ready, 1)
                            if i:
                                act.wait_ge(cT_lo_ready, 2 * layer + i)
                            act.wait_ge(uT_ready, 2 * (2 * layer + i) + 2)
                            for c in range(4):
                                act.activation(yTv[:, c, :], uT[:, c, 2:2 + SEQ], ACT.Copy,
                                               scale=convT[:, layer, 2, 4 * i + c:4 * i + c + 1]).then_inc(tap_ready, 1)
                        if kind == "turn_b":
                            act.wait_ge(c_ready, 2 * (2 * layer + i) + 2)
                            act.activation(k_tok(cT_hi)[:, 4 * i:4 * i + 4, :], yTv, ACT.Copy).then_inc(cT_hi_ready, 1)
                        if kind == "turn_m":
                            for t in range(TT):
                                full(6 + t)
                                act.activation(k_tok(hT_hi)[:, 4 * i:4 * i + 4, P * t:P * t + P], bank_quads(6 + t),
                                               ACT.Copy).then_inc(mT_hi_ready, 1)

            def dense():
                def silu(m):
                    for t in range(TT):
                        act.wait_ge(d_rows, 2 * m + 1)
                        act.activation(tok_c(part)[:, t, 0:FFW], bank[t][:, 0:FFW], ACT.Silu).then_inc(d_silu, 1)

                def turn_hi(m):
                    act.wait_ge(d_turn, m + 1)
                    act.activation(ffT_hi, bank[2][:, :], ACT.Copy).then_inc(d_hi, 1)

                n0 = DENSE0
                split_hi(act, n0 + 2)
                split_hi(act, n0 + 3)
                act.wait_ge(half_used, n0 + 2)
                silu(0)
                with act.Fori(0, (FSTEPS - 1) // 2) as it:
                    for i in range(2):
                        m = 2 * it + 1 + i
                        n = n0 + 2 + 3 * i
                        split_hi(act, n + 2, it)
                        turn_hi(m - 1)
                        split_hi(act, n + 3, it)
                        split_hi(act, n + 4, it)
                        act.wait_ge(half_used, n + 2 + RAW * it)
                        silu(m)
                turn_hi(FSTEPS - 1)
                split_hi(act, n0 + DENSE_HALVES + 1)

            def experts():
                act.wait_ge(hrow_ready, 8)
                for t in range(TT):
                    act.activation(hr_hi[:, t, :], hrow[:, t, :], ACT.Copy).then_inc(hr_hi_ready, 1)
                split_hi(act, MOE0 + 2)
                act.wait_ge(gap_ready, 1)
                act.activation(gap[:, :], gap[:, :], ACT.Exp).then_inc(gap_exp, 1)
                act.wait_ge(seats_ready, 1)
                act.activation(places[:, :, :].rearrange("p a e -> p (a e)"), bank[5][:, 0:3 * EXPERTS],
                               ACT.Copy).then_inc(places_out, 1)

                def gathered(g):
                    for i, b, dst in ((0, 6, xg_hi[:, 0:CHUNK]), (2, 3, xg_lo[:, 0:CHUNK])):
                        act.wait_ge(gather_ps, 4 * g + i + 1)
                        act.activation(dst, bank[b][:, :], ACT.Copy).then_inc(xg_act, 1)

                def take_y(b):
                    act.wait_ge(half_used, MOE0 + BLOCK_HALVES * b)
                    act.wait_ge(spread_ready, 2 * b)
                    for hf in range(2):
                        act.activation(y_hi[:, CHUNK * hf:CHUNK * (hf + 1)], bank[4 + hf][:, :], ACT.Copy,
                                       scale=gate[:, 0:1]).then_inc(y_hi_ready, 1)

                def silu(b, m):
                    act.wait_ge(e_rows, MSTEPS * b + m + 1)
                    act.activation(part[:, 0:CHUNK], bank[0][:, :], ACT.Silu).then_inc(e_silu, 1)

                def turn_hi(b, m):
                    act.wait_ge(e_turn, MSTEPS * b + m + 1)
                    act.activation(ffT_hi, bank[2][:, :], ACT.Copy).then_inc(e_hi, 1)

                def block(b, opening=False):
                    c = CYCLES * b
                    if not opening:
                        split_hi(act, MOE0, c)
                        split_hi(act, MOE0 + 1, c)
                        take_y(b)
                        split_hi(act, MOE0 + 2, c)
                    for i in range(3, 6):
                        split_hi(act, MOE0 + i, c)
                    act.wait_ge(half_used, MOE0 + 4 + BLOCK_HALVES * b)
                    silu(b, 0)
                    act.wait_ge(spread_ps, b + 1)
                    act.activation(spread_r, bank[7][:, 0:SEQ].rearrange("p (t j) -> p t j", t=TT),
                                   ACT.Copy).then_inc(spread_ready, 1)
                    act.activation(gate[:, :], bank[7][:, SEQ:SEQ + 1], ACT.Copy).then_inc(spread_ready, 1)
                    with act.Fori(1, MSTEPS) as m:
                        cm = c + m - 1
                        split_hi(act, MOE0 + 6, cm)
                        turn_hi(b, m - 1)
                        for i in range(7, 11):
                            split_hi(act, MOE0 + i, cm)
                        act.wait_ge(half_used, MOE0 + 8 + RAW * cm)
                        silu(b, m)
                        split_hi(act, MOE0 + 11, cm)
                    turn_hi(b, MSTEPS - 1)
                    gathered(b + 1)

                act.wait_ge(moe_init, 1)
                gathered(0)
                block(0, opening=True)
                with act.Fori(1, EXPERTS) as b:
                    block(b)
                act.wait_ge(route_ready, 1)
                blocks = act.value_load(ctl_i[0:1, 0:1], min_val=EXPERTS, max_val=EXPERTS + SLOTS)
                with act.If(blocks > EXPERTS):
                    with act.Fori(EXPERTS, blocks) as b:
                        block(b)
                take_y(blocks)
                return blocks

            norm_sums(0)
            split_hi(act, 0)
            split_hi(act, 1)
            norm_hi(0)
            mixer(0)
            norm_sums(1)
            norm_hi(1)
            act.wait_ge(hrow_ready, 4)
            act.dma_start(gain, mix_norm_g[1].partition_broadcast(P)).then_inc(gain_in, 16)
            dense()
            norm_sums(2)
            norm_hi(2)
            mixer(1)
            norm_sums(3)
            norm_hi(3)
            act.wait_ge(hrow_ready, 8)
            act.dma_start(gain, final_norm_g.partition_broadcast(P)).then_inc(gain_in, 16)
            blocks = experts()
            act.wait_ge(x_add, 4 * blocks + 4)
            act.wait_ge(e_rows, MSTEPS * EXPERTS)
            for t in range(TT):
                act.activation(part[:, :], X[:, t, :], ACT.Square, accum_out=ssq[:, t:t + 1]).then_inc(ss_ready, 1)
                act.wait_ge(ss_ready, 8 + t + 1)

        @block.vector
        def _(dve):
            count = [0]

            def chain(ins):
                count[0] += 1
                ins.then_inc(dve_step, 1)
                dve.wait_ge(dve_step, count[0])

            def rsqrt_of(sums, scale, n):
                v, t, y = nw[0][:, 0:n], nw[1][:, 0:n], nwi[:, 0:n].bitcast(F32)
                chain(dve.tensor_scalar(v, sums, scale, EPS, ALU.mult, ALU.add))
                chain(dve.tensor_scalar(nwi[:, 0:n], v.bitcast(I32), -0.5, float(0x5F3759DF), ALU.mult, ALU.add))
                chain(dve.tensor_scalar(v, v, -0.5, None, ALU.mult))
                for _ in range(3):
                    chain(dve.tensor_tensor(t, y, y, ALU.mult))
                    chain(dve.tensor_tensor(t, t, v, ALU.mult))
                    chain(dve.scalar_tensor_tensor(out=y, in0=t, scalar=1.5, in1=y, op0=ALU.add, op1=ALU.mult))
                return y

            def norm_rows(q):
                dve.wait_ge(ss_ready, 2 * q + 2)
                y = rsqrt_of(ssq[:, 0:TT], 1.0 / D, TT)
                dve.wait_ge(gain_in, 16 * (q + 1))
                for t in range(TT):
                    dve.scalar_tensor_tensor(out=hrow[:, t, :], in0=X[:, t, :], scalar=y[:, t:t + 1], in1=gain,
                                             op0=ALU.mult, op1=ALU.mult).then_inc(hrow_ready, 1)

            def norm_lo(q):
                for t in range(TT):
                    for g in range(2):
                        dve.wait_ge(hT_hi_ready, 4 * q + 2 * t + g + 1)
                        dve.tensor_tensor(k_tok(hT_lo)[:, 4 * g:4 * g + 4, P * t:P * t + P], bank_quads(2 * t + g),
                                          k_tok(hT_hi)[:, 4 * g:4 * g + 4, P * t:P * t + P],
                                          ALU.subtract).then_inc(hT_lo_ready, 1)

            def mixer(layer):
                n0 = MIX0[layer]

                for s in range(MIX_HALVES + 1):
                    def full(b):
                        job_in_bank(dve, layer, (kind, i), b)
                    jobs = JOBS[s - 1] if s else []
                    for kind, i in jobs:
                        if kind == "scores":
                            for m in range(2):
                                full(4 + m)
                                if i == 0 and m == 0 and layer == 0:
                                    dve.wait_ge(bias_in, 16 * 2 * HEADS)
                                chain(dve.tensor_tensor(prob[:, m, :], bank[4 + m][:, 0:LINE], bias[:, i, :],
                                                        ALU.add))
                            chain(dve.tensor_reduce(nmax[:, 0:2], prob[:, :, 0:P], AX, ALU.max, negate=True))
                            dve.tensor_reduce(nmax[:, 2:4], prob[:, :, P:LINE], AX, ALU.max,
                                              negate=True).then_inc(biased, 1)
                    if s < MIX_HALVES:
                        split_lo(dve, n0 + s + 2)
                    if s == 38 and layer == 1:
                        dve.wait_ge(rtr_hi_ready, 1)
                        dve.tensor_tensor(rtr_lo[:, :], rtr[:, :], rtr_hi[:, :],
                                          ALU.subtract).then_inc(rtr_lo_ready, 1)
                    for u in range(UNITS):
                        if last_half(u) != s - 1:
                            continue
                        banks = [bank[2 * (u % 2) + t] for t in range(TT)]
                        kind, i = UNIT[u]
                        cols = slice(CHUNK * i, CHUNK * (i + 1))
                        if kind in ("cc", "conv", "attn", "wo"):
                            dve.wait_ge(half_used, n0 + s)
                        if kind == "cc":
                            dve.wait_ge(ch_ready, 4 * layer + 2 * i + 2)
                            rows_turned(dve, layer, s)
                            for t in range(TT):
                                dve.tensor_tensor(tok_c(rows)[:, t], banks[t][:, :], tok_c(part)[:, t],
                                                  ALU.mult).then_inc(dve_rows, 1)
                        if kind == "conv":
                            dve.wait_ge(sig_ready, 8 * (layer + 1))
                            for t in range(TT):
                                dve.tensor_tensor(sig_conv[:, t, cols], banks[t][:, :], sig_conv[:, t, cols],
                                                  ALU.mult).then_inc(merged_conv, 1)
                        if kind == "attn":
                            for t in range(TT):
                                dve.tensor_tensor(sig_attn[i][:, t], banks[t][:, :], sig_attn[i][:, t],
                                                  ALU.mult).then_inc(merged_attn, 1)
                            dve.wait_ge(merged_attn, 4 * layer + 2 * i + 2)
                            dve.wait_ge(merged_conv, 4 * layer + 2 * i + 2)
                            for t in range(TT):
                                dve.tensor_tensor(merged[:, t, cols], sig_attn[i][:, t], sig_conv[:, t, cols],
                                                  ALU.add).then_inc(merged_ready, 1)
                        if kind == "wo":
                            for t in range(TT):
                                dve.tensor_tensor(X[:, t, cols], X[:, t, cols], banks[t][:, :],
                                                  ALU.add).then_inc(x_new, 1)
                    for kind, i in jobs:
                        head = HEADS * layer + i
                        if kind == "scores":
                            dve.wait_ge(exp_ready, 4 * head + 4)
                            chain(dve.reciprocal(recip[:, :], psum_row[:, :]))
                            chain(dve.tensor_scalar(recip[:, 1:4:2], recip[:, 1:4:2], neg_lam[:, layer:layer + 1],
                                                    None, ALU.mult))
                            if head:
                                pl, ph = (layer, i - 1) if i else (layer - 1, HEADS - 1)
                                job_in_bank(dve, pl, ("turn_w", ph), 6)
                            for t, c0, c1 in ((0, 0, P), (1, P, LINE)):
                                dve.tensor_scalar(wgt[:, c0:c1], prob[:, 0, c0:c1], recip[:, 2 * t:2 * t + 1], None,
                                                  ALU.mult).then_inc(dve_step, 1)
                            count[0] += 2
                            dve.wait_ge(dve_step, count[0])
                            for t, c0, c1 in ((0, 0, P), (1, P, LINE)):
                                dve.scalar_tensor_tensor(out=wgt[:, c0:c1], in0=prob[:, 1, c0:c1],
                                                         scalar=recip[:, 2 * t + 1:2 * t + 2], in1=wgt[:, c0:c1],
                                                         op0=ALU.mult, op1=ALU.add).then_inc(wgt_ready, 1)
                            dve.wait_ge(wgt_ready, 2 * head + 2)
                        if kind == "turn_a":
                            dve.wait_ge(aT_hi_ready, head + 1)
                            dve.tensor_tensor(k_tok(aT_lo)[:, i, :], bank[7][:, 0:SEQ], k_tok(aT_hi)[:, i, :],
                                              ALU.subtract).then_inc(aT_lo_ready, 1)
                        if kind == "turn_u":
                            dve.wait_ge(uT_ready, 2 * (2 * layer + i) + 2)
                            dve.wait_ge(tap_ready, 4 * (2 * layer + i) + 4)
                            for tap in (1, 0):
                                for c in range(4):
                                    w = convT[:, layer, tap, 4 * i + c:4 * i + c + 1]
                                    src = uT[:, c, tap:tap + SEQ]
                                    ins = dve.scalar_tensor_tensor(out=yTv[:, c, :], in0=src, scalar=w,
                                                                   in1=yTv[:, c, :], op0=ALU.mult, op1=ALU.add)
                                    ins.then_inc(dve_step if tap else yT_ready, 1)
                                if tap:
                                    count[0] += 4
                                    dve.wait_ge(dve_step, count[0])
                        if kind == "turn_b":
                            for t in range(TT):
                                full(6 + t)
                                dve.wait_ge(yT_ready, 4 * (2 * layer + i) + 4)
                                dve.tensor_tensor(yTv[:, :, P * t:P * t + P], bank_quads(6 + t),
                                                  yTv[:, :, P * t:P * t + P], ALU.mult).then_inc(c_ready, 1)
                            dve.wait_ge(cT_hi_ready, 2 * layer + i + 1)
                            dve.tensor_tensor(k_tok(cT_lo)[:, 4 * i:4 * i + 4, :], yTv,
                                              k_tok(cT_hi)[:, 4 * i:4 * i + 4, :],
                                              ALU.subtract).then_inc(cT_lo_ready, 1)
                        if kind == "turn_m":
                            for t in range(TT):
                                dve.wait_ge(mT_hi_ready, 2 * (2 * layer + i) + t + 1)
                                dve.tensor_tensor(k_tok(hT_lo)[:, 4 * i:4 * i + 4, P * t:P * t + P], bank_quads(6 + t),
                                                  k_tok(hT_hi)[:, 4 * i:4 * i + 4, P * t:P * t + P],
                                                  ALU.subtract).then_inc(mT_lo_ready, 1)

            def dense():
                def gated(m):
                    for t in range(TT):
                        dve.wait_ge(d_silu, 2 * m + t + 1)
                        if t == 0:
                            dve.wait_ge(d_lo, m + 1)
                        dve.tensor_tensor(tok_c(rows)[:, t, 0:FFW], bank[t][:, FFW:2 * FFW], tok_c(part)[:, t, 0:FFW],
                                          ALU.mult).then_inc(d_rows, 1)

                def turn_lo(m):
                    dve.wait_ge(d_hi, m + 1)
                    dve.tensor_tensor(ffT_lo, bank[2][:, :], ffT_hi, ALU.subtract).then_inc(d_lo, 1)

                n0 = DENSE0
                split_lo(dve, n0 + 2)
                split_lo(dve, n0 + 3)
                gated(0)
                with dve.Fori(0, (FSTEPS - 1) // 2) as it:
                    for i in range(2):
                        m = 2 * it + 1 + i
                        n = n0 + 2 + 3 * i
                        split_lo(dve, n + 2, it)
                        turn_lo(m - 1)
                        split_lo(dve, n + 3, it)
                        split_lo(dve, n + 4, it)
                        gated(m)
                turn_lo(FSTEPS - 1)
                split_lo(dve, n0 + DENSE_HALVES + 1)
                dve.wait_ge(half_used, n0 + DENSE_HALVES)
                for t in range(TT):
                    for hf in range(2):
                        dve.tensor_tensor(X[:, t, CHUNK * hf:CHUNK * (hf + 1)], X[:, t, CHUNK * hf:CHUNK * (hf + 1)],
                                          bank[4 + 2 * t + hf][:, :], ALU.add).then_inc(x_new, 1)

            def route():
                logits = bank[4][:, 0:TT * EXPERTS].rearrange("p (t e) -> p t e", t=TT)
                square = [P, TT, EXPERTS, EXPERTS]
                dve.wait_ge(const_ready, 4)
                dve.wait_ge(logits_ps, 1)
                chain(dve.tensor_copy(rank[:, :, :], logits))
                row, col = rank[:, :, :].unsqueeze(2).to_broadcast(square), rank[:, :, :].unsqueeze(3).to_broadcast(square)
                dve.tensor_tensor(beats[:, :, :, :], row, col, ALU.is_gt).then_inc(rank_ready, 1)
                dve.tensor_tensor(ties[:, :, :, :], row, col, ALU.is_equal).then_inc(rank_ready, 1)
                dve.wait_ge(rank_ready, 2)
                chain(dve.tensor_tensor(ties[:, :, :, :], ties[:, :, :, :],
                                        earlier[:, :, :].unsqueeze(1).to_broadcast(square), ALU.mult))
                chain(dve.tensor_tensor(beats[:, :, :, :], beats[:, :, :, :], ties[:, :, :, :], ALU.add))
                chain(dve.tensor_reduce(rank[:, :, :], beats[:, :, :, :], AX, ALU.add))
                dve.tensor_scalar(mask[:, :, :], rank[:, :, :], 2.0, None, ALU.is_lt).then_inc(mask_ready, 1)
                for r in range(2):
                    ins = dve.tensor_scalar(chosen[:, r, :, :], rank[:, :, :], float(r), None, ALU.is_equal)
                    ins.then_inc(rank_ready, 1)
                dve.wait_ge(rank_ready, 4)
                both = [P, 2, TT, EXPERTS]
                for r in range(2):
                    ins = dve.tensor_tensor(picked[:, r, :, :], chosen[:, r, :, :], logits, ALU.mult)
                    ins.then_inc(rank_ready, 1)
                dve.wait_ge(rank_ready, 6)
                chain(dve.tensor_reduce(top[:, :, :], picked[:, :, :, :], AX, ALU.add))
                dve.tensor_tensor(gap[:, :], top[:, 1, :], top[:, 0, :], ALU.subtract).then_inc(gap_ready, 1)
                dve.wait_ge(place_ps, 1)
                place = bank[5][:, 0:TT * EXPERTS].rearrange("p (t e) -> p t e", t=TT)
                dve.wait_ge(mask_ready, 1)
                dve.scalar_tensor_tensor(out=first[:, :, :], in0=place, scalar=float(P), in1=mask[:, :, :],
                                         op0=ALU.is_lt, op1=ALU.mult).then_inc(first_ready, 1)
                dve.wait_ge(first_ready, 1)
                dve.scalar_tensor_tensor(out=seats[:, 0:TT, 0:EXPERTS], in0=place, scalar=1.0, in1=first[:, :, :],
                                         op0=ALU.add, op1=ALU.mult).then_inc(seats_ready, 1)
                dve.wait_ge(seats_ready, 1)
                for t in range(TT):
                    dve.tensor_scalar(pick_r[:, t, :], iota_1[:, :], seats[:, t, 0:1], None,
                                      ALU.is_equal).then_inc(pick_r_ready, 1)
                dve.wait_ge(gap_exp, 1)
                chain(dve.tensor_scalar(top[:, 1, :], gap[:, :], 1.0, None, ALU.add))
                chain(dve.reciprocal(top[:, 0, :], top[:, 1, :]))
                chain(dve.tensor_tensor(top[:, 1, :], gap[:, :], top[:, 0, :], ALU.mult))
                chain(dve.tensor_tensor(picked[:, :, :, :], chosen[:, :, :, :],
                                        top[:, :, :].unsqueeze(3).to_broadcast(both), ALU.mult))
                dve.tensor_tensor(seats[:, TT:2 * TT, 0:EXPERTS], picked[:, 0, :, :], picked[:, 1, :, :],
                                  ALU.add).then_inc(gates_ready, 1)
                dve.wait_ge(gates_ready, 1)

            def experts():
                for sm, n in ((e_rows, 1), (e_lo, 1), (y_hi_ready, 2), (scatter_ps, 4), (x_add, 4)):
                    dve.sem_inc(sm, n)
                dve.sem_inc(moe_init, 1)
                split_lo(dve, MOE0 + 2)
                route()

                def make_pick(g, rest_only=False):
                    dve.tensor_copy(seat[:, :], seats[:, :, bass.ds(g, 1)].rearrange("p c o -> p (c o)")).then_inc(col_ready, 1)
                    dve.wait_ge(col_ready, g + 1)
                    for t in range(TT):
                        dve.tensor_scalar(pick[:, t, :], iota_1[:, :], seat[:, t:t + 1], None,
                                          ALU.is_equal).then_inc(pick_ready, 1)
                        if not rest_only:
                            dve.tensor_scalar(pick_r[:, t, :], iota_1[:, :], seat[:, t:t + 1], None,
                                              ALU.is_equal).then_inc(pick_r_ready, 1)

                def gathered(g):
                    for i, b, dst in ((1, 7, xg_hi[:, CHUNK:D]), (3, 6, xg_lo[:, CHUNK:D])):
                        dve.wait_ge(gather_ps, 4 * g + i + 1)
                        dve.tensor_copy(dst, bank[b][:, :]).then_inc(xg_dve, 1)

                def take_y(b):
                    for hf in range(2):
                        dve.wait_ge(y_hi_ready, 2 * b + hf + 1)
                        dve.scalar_tensor_tensor(out=y_lo[:, CHUNK * hf:CHUNK * (hf + 1)], in0=bank[4 + hf][:, :],
                                                 scalar=gate[:, 0:1], in1=y_hi[:, CHUNK * hf:CHUNK * (hf + 1)],
                                                 op0=ALU.mult, op1=ALU.subtract).then_inc(y_lo_ready, 1)

                def add_scattered(b):
                    for i, bk in enumerate((6, 7, 3, 6)):
                        t, hf = i // 2, i % 2
                        dve.wait_ge(scatter_ps, 4 * b + i + 1)
                        dve.tensor_tensor(X[:, t, CHUNK * hf:CHUNK * (hf + 1)], X[:, t, CHUNK * hf:CHUNK * (hf + 1)],
                                          bank[bk][:, :], ALU.add).then_inc(x_add, 1)

                def gated(b, m):
                    dve.wait_ge(e_silu, MSTEPS * b + m + 1)
                    dve.wait_ge(e_lo, MSTEPS * b + m + 1)
                    dve.tensor_tensor(rows[:, 0:CHUNK], bank[1][:, :], part[:, 0:CHUNK], ALU.mult).then_inc(e_rows, 1)

                def turn_lo(b, m):
                    dve.wait_ge(e_hi, MSTEPS * b + m + 1)
                    dve.tensor_tensor(ffT_lo, bank[2][:, :], ffT_hi, ALU.subtract).then_inc(e_lo, 1)

                def block(b, opening=False):
                    c = CYCLES * b
                    if not opening:
                        split_lo(dve, MOE0, c)
                        split_lo(dve, MOE0 + 1, c)
                        take_y(b)
                        split_lo(dve, MOE0 + 2, c)
                    for i in range(3, 6):
                        split_lo(dve, MOE0 + i, c)
                    gated(b, 0)
                    if not opening:
                        add_scattered(b)
                    dve.wait_ge(route_ready, 1)
                    dve.wait_ge(spread_ps, b + 1)
                    make_pick(b + 1)
                    with dve.Fori(1, MSTEPS) as m:
                        cm = c + m - 1
                        split_lo(dve, MOE0 + 6, cm)
                        turn_lo(b, m - 1)
                        for i in range(7, 11):
                            split_lo(dve, MOE0 + i, cm)
                        gated(b, m)
                        split_lo(dve, MOE0 + 11, cm)
                    turn_lo(b, MSTEPS - 1)
                    gathered(b + 1)

                make_pick(0, rest_only=True)
                gathered(0)
                block(0, opening=True)
                with dve.Fori(1, EXPERTS) as b:
                    block(b)
                blocks = dve.value_load(ctl_i[0:1, 0:1], min_val=EXPERTS, max_val=EXPERTS + SLOTS)
                with dve.If(blocks > EXPERTS):
                    with dve.Fori(EXPERTS, blocks) as b:
                        block(b)
                take_y(blocks)
                add_scattered(blocks)

            chain(dve.memset(zero_r[:, :].bitcast(F32), 0.0))
            chain(dve.memset(relb[NBUCKETS:64, :], -BIG))
            dve.wait_ge(relb_in, 16)
            dve.wait_ge(pool_step, 3)
            for h in range(HEADS):
                if h:
                    dve.wait_ge(line_ps, h)
                dve.tensor_scalar(relb_bc[:, :], ones[0:64, :], relb[:, h:h + 1], None, ALU.mult).then_inc(relb_ready, 1)
            dve.wait_ge(lam_in, 16)
            for i in range(2):
                for l in range(DEPTH):
                    chain(dve.tensor_tensor(lamq[:, l, 2 * i, :], lamq[:, l, 2 * i, :], lamq[:, l, 2 * i + 1, :], ALU.mult))
                    chain(dve.tensor_reduce(lam4[:, i, l:l + 1], lamq[:, l, 2 * i, :], AX, ALU.add))
            dve.sem_inc(lam_sums, 1)
            dve.wait_ge(lam_exp, 1)
            chain(dve.tensor_tensor(neg_lam[:, :], lam4[:, 1, :], lam4[:, 0, :], ALU.subtract))
            dve.wait_ge(sub_in, 16)
            for l in range(DEPTH):
                chain(dve.tensor_scalar(neg_lam[:, l:l + 1], neg_lam[:, l:l + 1], lambda_init(l), None, ALU.subtract))
                chain(dve.tensor_scalar(gsub[:, l, :], gsub[:, l, :], 1.0 - lambda_init(l), None, ALU.mult))
            dve.sem_inc(gsub_ready, 1)
            dve.wait_ge(conv_ps, 1)
            chain(dve.tensor_copy(convT[:, :, :, :].rearrange("p l w c -> p (l w c)"), bank[0][:, 0:DEPTH * 3 * KC]))

            norm_rows(0)
            split_lo(dve, 0)
            split_lo(dve, 1)
            norm_lo(0)
            mixer(0)
            norm_rows(1)
            norm_lo(1)
            dve.sem_inc(d_rows, 1)
            dve.sem_inc(d_lo, 1)
            dense()
            norm_rows(2)
            norm_lo(2)
            mixer(1)
            norm_rows(3)
            norm_lo(3)
            experts()
            norm_rows(4)

        @block.tensor
        def _(pe):
            pe.wait_ge(bucket_in, 16)
            for h in range(HEADS):
                pe.wait_ge(relb_ready, h + 1)
                if h >= 4:
                    pe.wait_ge(line_sb, h - 3)
                pe.matmul(bank[4 + h % 4][:, 0:LINE], relb_bc[0:NBUCKETS + 1, :],
                          w_raw[0:NBUCKETS + 1, RAW - 1, 0:LINE], start=True, stop=True).then_inc(line_ps, 1)

            def norm_turn(q):
                for t in range(TT):
                    pe.wait_ge(hrow_ready, 2 * q + t + 1)
                    for g in range(2):
                        for c in range(4):
                            k = 4 * g + c
                            ins = pe.transpose(bank[2 * t + g][:, P * c:P * c + P], hrow[:, t, P * k:P * k + P], ident[:, :])
                        ins.then_inc(norm_ps, 1)

            def mixer(layer):
                n0 = MIX0[layer]
                pe.wait_ge(hT_lo_ready, 4 * (2 * layer + 1))
                for s in range(MIX_HALVES):
                    u, hf = unit_of(s)
                    if hf == 0 and u >= 2:
                        unit_out(pe, layer, u - 2)
                    if s == S_CONV:
                        pe.wait_ge(cT_lo_ready, 2 * (layer + 1))
                    if s == S_ATTN:
                        pe.wait_ge(aT_lo_ready, HEADS * (layer + 1))
                    if s in (S_WO, S_WO + 2):
                        pe.wait_ge(mT_lo_ready, 4 * layer + 2 * (hf + 1))
                    hi, lo = {"conv": (k_tok(cT_hi), k_tok(cT_lo)),
                              "attn": (k_tok(aT_hi), k_tok(aT_lo))}.get(UNIT[u][0], (k_tok(hT_hi), k_tok(hT_lo)))
                    pe.wait_ge(lo_ready, n0 + s + 1)
                    for t in range(TT):
                        for c in range(4):
                            k = 4 * hf + c
                            whi, wlo = half_parts(n0 + s, 4, c)
                            ins = product(pe, bank[2 * (u % 2) + t][:, :], hi[:, k, P * t:P * t + P],
                                          lo[:, k, P * t:P * t + P], whi, wlo, k == 0, k == KC - 1)
                    ins.then_inc(half_used, 1)
                    for job in JOBS[s]:
                        kind, i = job
                        for b in JOB_BANKS[kind]:
                            if JOB_BEFORE[job, b]:
                                job_out(pe, layer, JOB_BEFORE[job, b])
                            elif layer:
                                job_out(pe, layer - 1, LAST_JOB[b])
                            else:
                                pe.wait_ge(line_sb, HEADS)
                        head = HEADS * layer + i
                        if kind in ("turn_qk", "turn_u", "turn_b"):
                            if kind == "turn_u":
                                pe.wait_ge(dve_rows, 2 * (2 * layer + i) + 2)
                            else:
                                source = ROW_UNITS[i if kind == "turn_qk" else 4 + i]
                                pe.wait_ge(act_rows, ACT_ROWS[layer, source])
                            for t in range(TT):
                                for c in range(4):
                                    ins = pe.transpose(bank[6 + t][:, P * c:P * c + P],
                                                       tok_c(rows)[:, t, P * c:P * c + P], ident[:, :])
                                ins.then_inc(bank_full[6 + t], 1)
                        if kind == "turn_m":
                            pe.wait_ge(merged_ready, 2 * (2 * layer + i) + 2)
                            for t in range(TT):
                                for c in range(4):
                                    k = 4 * i + c
                                    ins = pe.transpose(bank[6 + t][:, P * c:P * c + P],
                                                       merged[:, t, P * k:P * k + P], ident[:, :])
                                ins.then_inc(bank_full[6 + t], 1)
                        if kind == "scores":
                            pe.wait_ge(qk_ready, 8 * layer + (4 if i < 4 else 8))
                            for m in range(2):
                                r = slice(HD * m, HD * m + HD)
                                pe.matmul(bank[4 + m][:, 0:P], qT[r, i, 0:P], kT[r, i, 0:P], start=True, stop=True)
                                pe.matmul(bank[4 + m][:, P:LINE], qT[r, i, P:SEQ], kT[r, i, 0:SEQ],
                                          start=True, stop=True).then_inc(bank_full[4 + m], 1)
                        if kind == "turn_w":
                            pe.wait_ge(wgt_ready, 2 * head + 2)
                            for c in range(3):
                                ins = pe.transpose(bank[6][:, P * c:P * c + P], wgt[:, P * c:P * c + P], ident[:, :])
                            ins.then_inc(bank_full[6], 1)
                        if kind == "values":
                            pe.wait_ge(wgtT_ready, head + 1)
                            pe.wait_ge(v_ready, 4 * layer + (2 if i < 4 else 4))
                            e = slice(P * i, P * i + P)
                            pe.matmul(bank[7][:, 0:P], wgtT[:, 0:P], v_rows[:, 0, e], start=True, stop=True)
                            pe.matmul(bank[7][:, P:2 * P], wgtT[:, P:2 * P], v_rows[:, 0, e], start=True, stop=False)
                            pe.matmul(bank[7][:, P:2 * P], wgtT[:, 2 * P:LINE], v_rows[:, 1, e], start=False,
                                      stop=True).then_inc(bank_full[7], 1)
                        if kind == "turn_a":
                            pe.wait_ge(arow_ready, 2 * head + 2)
                            for t in range(TT):
                                ins = pe.transpose(bank[7][:, P * t:P * t + P], arow[:, t, :], ident[:, :])
                            ins.then_inc(bank_full[7], 1)

            def dense():
                n0 = DENSE0
                hi, lo = k_tok(hT_hi), k_tok(hT_lo)
                pe.wait_ge(hT_lo_ready, 8)

                def gate_up(n, cyc):
                    for hf in range(2):
                        pe.wait_ge(lo_ready, n + hf + 1 + RAW * cyc)
                        for t in range(TT):
                            for k in range(KC):
                                whi, wlo = half_parts(n + hf, KC, k)
                                ins = product(pe, bank[t][:, FFW * hf:FFW * (hf + 1)], hi[:, k, P * t:P * t + P], lo[:, k, P * t:P * t + P],
                                              whi, wlo, k == 0, k == KC - 1)
                        ins.then_inc(half_used, 1)

                def turn(m):
                    pe.wait_ge(d_rows, 2 * m + 3)
                    for t in range(TT):
                        for j in range(2):
                            ins = pe.transpose(bank[2][:, SEQ * j + P * t:SEQ * j + P * t + P],
                                               tok_c(rows)[:, t, P * j:P * j + P], ident[:, :])
                    ins.then_inc(d_turn, 1)

                def down(n, cyc, m):
                    pe.wait_ge(lo_ready, n + 1 + RAW * cyc)
                    pe.wait_ge(d_lo, m + 2)
                    for t in range(TT):
                        for j in range(2):
                            whi, wlo = half_parts(n, 2, j)
                            at = slice(SEQ * j + P * t, SEQ * j + P * t + P)
                            for hf in range(2):
                                cols = slice(CHUNK * hf, CHUNK * (hf + 1))
                                ins = product(pe, bank[4 + 2 * t + hf][:, :], ffT_hi[:, at], ffT_lo[:, at],
                                              whi[:, cols], wlo[:, cols], False, False)
                    ins.then_inc(half_used, 1)

                for b in range(4, 8):
                    pe.matmul(bank[b][:, :], zero_r[:, 0:P], zero_r[:, :], start=True, stop=False, skip_group_check=True)
                gate_up(n0, 0)
                turn(0)
                with pe.Fori(0, (FSTEPS - 1) // 2) as it:
                    for i in range(2):
                        m = 2 * it + 1 + i
                        gate_up(n0 + 2 + 3 * i, it)
                        down(n0 + 4 + 3 * i, it, m - 1)
                        turn(m)
                down(n0 + DENSE_HALVES - 1, 0, FSTEPS - 1)

            def experts():
                pe.wait_ge(rtr_lo_ready, 1)
                hi, lo = k_tok(hT_hi), k_tok(hT_lo)
                for t in range(TT):
                    pe.wait_ge(hT_lo_ready, 12 + 2 * (t + 1))
                    for k in range(KC):
                        e = slice(EXPERTS * k, EXPERTS * (k + 1))
                        ins = product(pe, bank[4][:, EXPERTS * t:EXPERTS * (t + 1)], hi[:, k, P * t:P * t + P],
                                      lo[:, k, P * t:P * t + P], rtr_hi[:, e], rtr_lo[:, e], k == 0, k == KC - 1)
                ins.then_inc(logits_ps, 1)
                pe.wait_ge(mask_ready, 1)
                pe.wait_ge(const_ready, 4)
                for dst, terms in ((slice(0, 8), ((before, 0),)), (slice(8, 16), ((ones, 0), (before, 1))),
                                   (slice(16, 24), ((ones, 0), (ones, 1)))):
                    for i, (left, t) in enumerate(terms):
                        ins = pe.matmul(bank[5][:, dst], left[:, :], mask[:, t, :], start=i == 0, stop=i == len(terms) - 1)
                ins.then_inc(place_ps, 1)

                def gather(g):
                    pe.wait_ge(pick_r_ready, 2 * g + 2)
                    for i, (src, k0, b) in enumerate(((hr_hi, 0, 6), (hr_hi, 4, 7), (hr_lo, 0, 3), (hr_lo, 4, 6))):
                        if i == 3:
                            pe.wait_ge(xg_act, 2 * g + 1)
                        for c in range(4):
                            for t in range(TT):
                                k = k0 + c
                                ins = pe.matmul(bank[b][:, P * c:P * c + P], src[:, t, P * k:P * k + P], pick_r[:, t, :],
                                                start=t == 0, stop=t == TT - 1)
                        ins.then_inc(gather_ps, 1)

                def up(n, cyc, b):
                    for hf in range(2):
                        pe.wait_ge(lo_ready, n + hf + 1 + RAW * cyc)
                        for c in range(4):
                            k = 4 * hf + c
                            whi, wlo = half_parts(n + hf, 4, c)
                            at = slice(P * k, P * k + P)
                            ins = product(pe, bank[b][:, :], xg_hi[:, at], xg_lo[:, at], whi, wlo, k == 0, k == KC - 1)
                        ins.then_inc(half_used, 1)

                def turn(b, m):
                    pe.wait_ge(e_rows, MSTEPS * b + m + 2)
                    for j in range(4):
                        ins = pe.transpose(bank[2][:, P * j:P * j + P], rows[:, P * j:P * j + P], ident[:, :])
                    ins.then_inc(e_turn, 1)

                def down(n, cyc, b, m):
                    pe.wait_ge(e_lo, MSTEPS * b + m + 2)
                    for i in range(2):
                        pe.wait_ge(lo_ready, n + i + 1 + RAW * cyc)
                        for j in range(2):
                            whi, wlo = half_parts(n + i, 2, j)
                            at = slice(P * (2 * i + j), P * (2 * i + j) + P)
                            for hf in range(2):
                                cols = slice(CHUNK * hf, CHUNK * (hf + 1))
                                ins = product(pe, bank[4 + hf][:, :], ffT_hi[:, at], ffT_lo[:, at],
                                              whi[:, cols], wlo[:, cols], False, False)
                        ins.then_inc(half_used, 1)

                def scatter(b, i):
                    t, hf = i // 2, i % 2
                    bk = (6, 7, 3, 6)[i]
                    if i == 3:
                        pe.wait_ge(x_add, 4 * b + 1)
                    cols = slice(CHUNK * hf, CHUNK * (hf + 1))
                    pe.matmul(bank[bk][:, :], spread_r[:, t, :], y_hi[:, cols], start=True, stop=False)
                    pe.matmul(bank[bk][:, :], spread_r[:, t, :], y_lo[:, cols], start=False,
                              stop=True).then_inc(scatter_ps, 1)

                def spread(b, opening):
                    if not opening:
                        pe.wait_ge(x_add, 4 * b + 2)
                    pe.wait_ge(pick_ready, 2 * b + 2)
                    for t in range(TT):
                        pe.transpose(bank[7][:, P * t:P * t + P], pick[:, t, :], ident[:, :])
                    for t in range(TT):
                        ins = pe.matmul(bank[7][:, SEQ:SEQ + 1], pick[:, t, :], seat[:, TT + t:TT + t + 1],
                                        start=t == 0, stop=t == TT - 1)
                    ins.then_inc(spread_ps, 1)

                pe.wait_ge(hr_lo_ready, 2)
                pe.wait_ge(moe_init, 1)
                def block(b, opening=False):
                    c = CYCLES * b
                    pe.wait_ge(xg_act, 2 * b + 2)
                    pe.wait_ge(xg_dve, 2 * b + 2)
                    up(MOE0, c, 0)
                    up(MOE0 + 2, c, 1)
                    if opening:
                        pe.wait_ge(places_out, 1)
                    else:
                        pe.wait_ge(y_lo_ready, 2 * b)
                    for hf in range(2):
                        pe.matmul(bank[4 + hf][:, :], zero_r[:, 0:P], zero_r[:, :], start=True, stop=False,
                                  skip_group_check=True)
                    if not opening:
                        for i in range(3):
                            scatter(b, i)
                    turn(b, 0)
                    if not opening:
                        scatter(b, 3)
                    spread(b, opening)
                    with pe.Fori(1, MSTEPS) as m:
                        cm = c + m - 1
                        up(MOE0 + 4, cm, 0)
                        up(MOE0 + 6, cm, 1)
                        down(MOE0 + 8, cm, b, m - 1)
                        turn(b, m)
                    pe.wait_ge(spread_ready, 2 * b + 2)
                    if not opening:
                        pe.wait_ge(x_add, 4 * b + 4)
                    gather(b + 1)
                    down(MOE0 + BLOCK_HALVES - 2, c, b, MSTEPS - 1)

                gather(0)
                block(0, opening=True)
                with pe.Fori(1, EXPERTS) as b:
                    block(b)
                pe.wait_ge(route_ready, 1)
                blocks = pe.value_load(ctl_i[0:1, 0:1], min_val=EXPERTS, max_val=EXPERTS + SLOTS)
                with pe.If(blocks > EXPERTS):
                    with pe.Fori(EXPERTS, blocks) as b:
                        block(b)
                pe.wait_ge(y_lo_ready, 2 * blocks)
                pe.wait_ge(xg_act, 2 * blocks + 2)
                pe.wait_ge(xg_dve, 2 * blocks + 2)
                for i in range(4):
                    scatter(blocks, i)

            pe.wait_ge(const_ready, 4)
            pe.wait_ge(conv_in, 16)
            n = DEPTH * 3 * KC
            pe.transpose(bank[0][:, 0:n], conv_rows[:, :], ident[0:n, 0:n]).then_inc(conv_ps, 1)
            norm_turn(0)
            mixer(0)
            norm_turn(1)
            dense()
            norm_turn(2)
            mixer(1)
            norm_turn(3)
            experts()


def bucket_lines():
    import numpy as np
    dist = SEQ - 1 - np.arange(LINE)
    exact = NBUCKETS // 2
    d = np.maximum(dist, 1).astype(np.float32)
    large = exact + (np.log(d / np.float32(exact)) / np.float32(math.log(128 / exact))
                     * np.float32(NBUCKETS - exact)).astype(np.int32)
    bucket = np.where(dist < exact, dist, np.minimum(large, NBUCKETS - 1))
    bucket = np.where(dist < 0, NBUCKETS, bucket)
    return (np.arange(NBUCKETS + 1)[:, None] == bucket[None, :]).astype(np.float32)


_INS = ["x", "rel_bias", "mix_norm_g", "w_in", "lam_qk", "subln_g", "conv_w", "w_o_attn", "w_o_conv", "w_o",
        "ffn_norm_g", "dense_w_gate_up", "dense_w_down", "router_w", "expert_w_gate_up", "expert_w_down",
        "final_norm_g"]


def kernel(**inputs):
    import numpy as np
    import concourse.bacc as bacc
    from concourse.bass_utils import run_bass_kernel_spmd as run

    nc = bacc.Bacc("TRN2", target_bir_lowering=False, num_devices=1, dynamic_dma_scratch_size=1024)
    arrays, args = {}, []
    for name in _INS:
        arrays[f"in_{name}"] = np.ascontiguousarray(inputs[name])
        args.append(nc.dram_tensor(f"in_{name}", arrays[f"in_{name}"].shape, F32, kind="ExternalInput").ap())
    arrays["bucket_of"] = bucket_lines()
    args.append(nc.dram_tensor("bucket_of", arrays["bucket_of"].shape, F32, kind="ExternalInput").ap())
    out = nc.dram_tensor("out", (1, SEQ, D), F32, kind="ExternalOutput").ap()
    build(nc, *args, out)
    return run(nc, [arrays], core_ids=[0]).results[0]["out"]
```

```python
import math
from contextlib import ExitStack

import concourse.bass as bass
from concourse import mybir

P = 128
F32 = mybir.dt.float32
F32R = mybir.dt.float32r
I32 = mybir.dt.int32
ALU = mybir.AluOpType
ACT = mybir.ActivationFunctionType
AX = mybir.AxisListType.X

D = 1024
SEQ = 256
TT = SEQ // P
KC = D // P
HEADS = 8
HD = 64
NBUCKETS = 32
EPS = 1e-6
DEPTH = 2
FF = 2816
FE = 3584
EXPERTS = 8
CHUNK = 512
HALF = 2048
RAW = 6
SPLIT = 3
FFW = 256
FSTEPS = FF // FFW
MSTEPS = FE // CHUNK
SLOTS = 3
COLS = EXPERTS + SLOTS + 1
LINE = 384
BIG = 1e30

MIX_HALVES = 44
DENSE_HALVES = 3 * FSTEPS
BLOCK_HALVES = 6 * MSTEPS
CYCLES = BLOCK_HALVES // RAW
MIX0 = (0, MIX_HALVES + DENSE_HALVES)
DENSE0 = MIX_HALVES
MOE0 = 2 * MIX_HALVES + DENSE_HALVES

UNIT = [("q", 0), ("k", 0), ("v", 0), ("q", 1), ("k", 1), ("v", 1), ("ch", 0), ("cc", 0), ("cb", 0),
        ("ch", 1), ("cc", 1), ("cb", 1), ("ga", 0), ("ga", 1), ("gc", 0), ("gc", 1),
        ("conv", 0), ("conv", 1), ("attn", 0), ("attn", 1), ("wo", 0), ("wo", 1)]
UNITS = len(UNIT)
W_IN_COL = {"q": 0, "k": D, "v": 2 * D, "ch": 3 * D, "cb": 4 * D, "cc": 5 * D, "ga": 6 * D, "gc": 7 * D}
S_CONV, S_ATTN, S_WO = (2 * UNIT.index((kind, 0)) for kind in ("conv", "attn", "wo"))


def unit_of(s):
    return (s // 2, s % 2) if s < S_WO else (UNITS - 2 + s % 2, (s - S_WO) // 2)


def last_half(u):
    return 2 * u + 1 if u < UNITS - 2 else MIX_HALVES - UNITS + u


def mixer_jobs():
    jobs = {s: [] for s in range(MIX_HALVES + 1)}
    for h in range(HEADS):
        a = 8 + 3 * h
        jobs[a].append(("scores", h))
        jobs[a + 2].append(("turn_w", h))
        jobs[a + 3].append(("values", h))
        jobs[a + 6].append(("turn_a", h))
    for s in jobs:
        jobs[s].sort(key=lambda j: ["scores", "turn_a", "values", "turn_w"].index(j[0]))
    for s, job in {2: ("turn_qk", 0), 4: ("turn_qk", 1), 9: ("turn_qk", 2), 10: ("turn_qk", 3),
                   16: ("turn_u", 0), 19: ("turn_b", 0), 22: ("turn_u", 1), 25: ("turn_b", 1),
                   38: ("turn_m", 0), 40: ("turn_m", 1)}.items():
        jobs[s].append(job)
    return jobs


JOBS = mixer_jobs()
JOB_BANKS = {"scores": (4, 5), "turn_w": (6,), "values": (7,), "turn_a": (6,),
             "turn_qk": (4, 5), "turn_u": (4, 5), "turn_b": (4, 5), "turn_m": (6, 7)}
TURNS_OF_ROWS = ("turn_qk", "turn_u", "turn_b")


def count_bank_uses():
    uses, last, at, before_it = {b: 0 for b in (4, 5, 6, 7)}, {}, {}, {}
    for s in range(MIX_HALVES):
        for job in JOBS[s]:
            for b in JOB_BANKS[job[0]]:
                uses[b] += 1
                at[job, b] = uses[b]
                before_it[job, b] = last.get(b)
                last[b] = job
    return at, before_it, uses, last


BANK_AT, JOB_BEFORE, BANK_USES, LAST_JOB = count_bank_uses()
ROW_UNITS = [("q", 0), ("k", 0), ("q", 1), ("k", 1), ("cb", 0), ("cb", 1)]
ACT_ROWS = {(layer, u): 2 * (6 * layer + i + 1) for layer in range(DEPTH) for i, u in enumerate(ROW_UNITS)}
NORM_AT = {0: 0, 1: MIX_HALVES, 2: MIX0[1], 3: MOE0}
NORM_BANK = {0: 0, 1: 4, 2: 0, 3: 4}
X_ADDS = {1: 4, 2: 8, 3: 12}


def lambda_init(layer):
    return 0.8 - 0.6 * math.exp(-0.3 * layer)


def build(nc, x, rel_bias, mix_norm_g, w_in, lam_qk, subln_g, conv_w, w_o_attn, w_o_conv, w_o,
          ffn_norm_g, dense_gu, dense_down, router_w, expert_gu, expert_down, final_norm_g,
          bucket_of, out):
    lines = nc.dram_tensor("bias_lines", (HEADS, P, LINE), F32, kind="Internal").ap()
    with ExitStack() as ctx:
        def sb(name, shape, dt=F32):
            return ctx.enter_context(nc.sbuf_tensor(name, shape, dt))

        def sem(name):
            return ctx.enter_context(nc.semaphore(name))

        w_raw = sb("w_raw", [P, RAW, HALF])
        w_hi = sb("w_hi", [P, SPLIT, HALF], F32R)
        w_lo = sb("w_lo", [P, SPLIT, HALF], F32R)
        X = sb("X", [P, TT, D])
        hT_hi = sb("hT_hi", [P, KC * SEQ], F32R)
        hT_lo = sb("hT_lo", [P, KC * SEQ], F32R)
        q_buf = sb("q_buf", [P, KC * SEQ])
        k_buf = sb("k_buf", [P, KC * SEQ])
        v_buf = sb("v_buf", [P, KC * SEQ])
        aT_hi = sb("aT_hi", [P, KC * SEQ], F32R)
        aT_lo = sb("aT_lo", [P, KC * SEQ], F32R)
        cT_hi = sb("cT_hi", [P, KC * SEQ], F32R)
        cT_lo = sb("cT_lo", [P, KC * SEQ], F32R)
        rows = sb("rows", [P, TT * CHUNK])
        part = sb("part", [P, TT * CHUNK])
        uT = sb("uT", [P, 4, SEQ + 2])
        yT = sb("yT", [P, KC * P])
        prob = sb("prob", [P, 2, LINE])
        wgt = sb("wgt", [P, LINE])
        wgtT = sb("wgtT", [P, LINE])
        arow = sb("arow", [P, TT, P])
        squares = sb("squares", [P, TT, P])
        bias = sb("bias", [P, HEADS, LINE])
        ident = sb("ident", [P, P])
        before = sb("before", [P, P])
        ones = sb("ones", [P, P])
        iota_1 = sb("iota_1", [P, P])
        zero_r = sb("zero_r", [P, CHUNK], F32R)
        relb = sb("relb", [64, HEADS])
        gsub = sb("gsub", [P, DEPTH, P])
        conv_rows = sb("conv_rows", [DEPTH * 3 * KC, P])
        convT = sb("convT", [P, DEPTH, 3, KC])
        lam4 = sb("lam4", [P, 2, DEPTH])
        neg_lam = sb("neg_lam", [P, DEPTH])
        nmax = sb("nmax", [P, 4])
        psum_row = sb("psum_row", [P, 4])
        recip = sb("recip", [P, 4])
        ssq = sb("ssq", [P, 2])
        nw = [sb(f"nw{i}", [P, 2]) for i in range(2)]
        nwi = sb("nwi", [P, 2], I32)
        head_ss = sb("head_ss", [P, 2])
        head_nw = [sb(f"head_nw{i}", [P, 2]) for i in range(2)]
        head_nwi = sb("head_nwi", [P, 2], I32)
        rtr = sb("rtr", [P, KC * EXPERTS])
        rtr_parts = sb("rtr_parts", [P, KC, 2, EXPERTS], F32R)
        logits = sb("logits", [P, TT, EXPERTS])
        beats = sb("beats", [P, TT, EXPERTS, EXPERTS])
        ties = sb("ties", [P, TT, EXPERTS, EXPERTS])
        earlier = sb("earlier", [P, EXPERTS, EXPERTS])
        rank = sb("rank", [P, TT, EXPERTS])
        chosen = sb("chosen", [P, 2, TT, EXPERTS])
        picked = sb("picked", [P, 2, TT, EXPERTS])
        mask = sb("mask", [P, TT, EXPERTS])
        first = sb("first", [P, TT, EXPERTS])
        beyond = sb("beyond", [P, TT, EXPERTS])
        top = sb("top", [P, 2, TT])
        gap = sb("gap", [P, TT])
        places = sb("places", [P, 3, EXPERTS])
        over = sb("over", [P, EXPERTS])
        count_a = sb("count_a", [P, EXPERTS])
        count_b = sb("count_b", [P, EXPERTS])
        slot_no = sb("slot_no", [P, SLOTS, EXPERTS])
        slot_of = sb("slot_of", [P, SLOTS, EXPERTS])
        src = sb("src", [P, 5, EXPERTS])
        terms = sb("terms", [P, 5, SLOTS, EXPERTS])
        found = sb("found", [P, 5, SLOTS])
        seats = sb("seats", [P, 2 * TT, COLS])
        seat = sb("seat", [P, 2 * TT])
        ctl = sb("ctl", [P, 4])
        ctl_i = sb("ctl_i", [P, 4], I32)
        gate = sb("gate", [P, 1])

        bank = [ctx.enter_context(nc.psum_tensor(f"bank{b}", [P, CHUNK], F32)) for b in range(8)]

        def k_tok(buf):
            return buf[:, :].rearrange("p (k t) -> p k t", t=SEQ)

        def tok_d(buf):
            return buf[:, :].rearrange("p (t d) -> p t d", t=TT)

        def tok_c(buf):
            return buf[:, :].rearrange("p (t c) -> p t c", t=TT)

        def quad(ap):
            return ap.rearrange("p (c n) -> p c n", n=P)

        hrow, merged = tok_d(q_buf), tok_d(k_buf)
        qT, kT = k_tok(q_buf), k_tok(k_buf)
        v_rows, sig_conv = tok_d(v_buf), tok_d(k_buf)
        sig_attn = (tok_c(part), tok_c(rows))
        gain = yT[:, :]
        yTv = yT[:, :].rearrange("p (c t) -> p c t", t=SEQ)
        relb_bc = v_buf[0:64, 0:HEADS * P].rearrange("b (h p) -> b h p", p=P)
        bucket = prob[0:NBUCKETS + 1, 0, :]
        lam_flat = k_buf[:, 0:DEPTH * 4 * HD]
        lamq = lam_flat.rearrange("p (l i d) -> p l i d", l=DEPTH, i=4)
        ffT_hi, ffT_lo = cT_hi[:, 0:CHUNK], cT_lo[:, 0:CHUNK]
        y_hi, y_lo = cT_hi[:, CHUNK:CHUNK + D], cT_lo[:, CHUNK:CHUNK + D]
        pick_r = cT_hi[:, 1536:1792].rearrange("p (t j) -> p t j", t=TT)
        spread_r = cT_hi[:, 1792:2048].rearrange("p (t j) -> p t j", t=TT)
        pick = prob[:, 0, 0:256].rearrange("p (t j) -> p t j", t=TT)
        xg_hi, xg_lo = hT_hi[:, 0:D], hT_lo[:, 0:D]
        hr_hi, hr_lo = tok_d(aT_hi), tok_d(aT_lo)

        x_in = [sem(f"x_in{t}") for t in range(TT)]
        relb_in, bucket_in, lam_in, sub_in, conv_in, rtr_in, gain_in = (
            sem(n) for n in ("relb_in", "bucket_in", "lam_in", "sub_in", "conv_in", "rtr_in", "gain_in"))
        line_out, bias_in, out_sent = sem("line_out"), sem("bias_in"), sem("out_sent")
        landed = [sem(f"landed{i}") for i in range(RAW)]
        early_in = {MOE0 + i: sem(f"early_in{i}") for i in range(RAW // 2, RAW)}
        hi_ready, lo_ready, half_used = sem("hi_ready"), sem("lo_ready"), sem("half_used")
        bank_full = {b: sem(f"bank_full{b}") for b in (4, 5, 6, 7)}
        const_ready = sem("const_ready")
        conv_ps, conv_sb = sem("conv_ps"), sem("conv_sb")
        sum_ps = sem("sum_ps")
        line_ps, line_sb, relb_ready = sem("line_ps"), sem("line_sb"), sem("relb_ready")
        gsub_ready, scaled = sem("gsub_ready"), sem("scaled")
        lam_sums, lam_exp = sem("lam_sums"), sem("lam_exp")
        dve_step = sem("dve_step")
        pool_step = sem("pool_step")
        x_new = sem("x_new")
        ss_ready, hrow_ready, norm_ps = sem("ss_ready"), sem("hrow_ready"), sem("norm_ps")
        hT_hi_ready, hT_lo_ready = sem("hT_hi_ready"), sem("hT_lo_ready")
        act_rows, dve_rows = sem("act_rows"), sem("dve_rows")
        qk_ready, v_ready, ch_ready = sem("qk_ready"), sem("v_ready"), sem("ch_ready")
        biased, exp_ready, wgt_ready, wgtT_ready = sem("biased"), sem("exp_ready"), sem("wgt_ready"), sem("wgtT_ready")
        o_ss, o_out, arow_ready, aT_hi_ready, aT_lo_ready = sem("o_ss"), sem("o_out"), sem("arow_ready"), sem("aT_hi_ready"), sem("aT_lo_ready")
        merged_attn, merged_conv, merged_ready = sem("merged_attn"), sem("merged_conv"), sem("merged_ready")
        uT_ready, tap_ready, yT_ready, c_ready = sem("uT_ready"), sem("tap_ready"), sem("yT_ready"), sem("c_ready")
        cT_hi_ready, cT_lo_ready = sem("cT_hi_ready"), sem("cT_lo_ready")
        sig_ready, mT_hi_ready, mT_lo_ready = sem("sig_ready"), sem("mT_hi_ready"), sem("mT_lo_ready")
        d_silu, d_rows, d_turn, d_hi, d_lo = sem("d_silu"), sem("d_rows"), sem("d_turn"), sem("d_hi"), sem("d_lo")
        rtr_hi_ready, rtr_lo_ready, hr_hi_ready, hr_lo_ready = (
            sem("rtr_hi_ready"), sem("rtr_lo_ready"), sem("hr_hi_ready"), sem("hr_lo_ready"))
        logits_ps, gap_ready, gap_exp, mask_ready, place_ps = (
            sem("logits_ps"), sem("gap_ready"), sem("gap_exp"), sem("mask_ready"), sem("place_ps"))
        rank_ready, places_out, first_ready, seats_ready, gates_ready = (
            sem("rank_ready"), sem("places_out"), sem("first_ready"), sem("seats_ready"), sem("gates_ready"))
        route_ready, moe_init = sem("route_ready"), sem("moe_init")
        e_silu, e_rows, e_turn, e_hi, e_lo = sem("e_silu"), sem("e_rows"), sem("e_turn"), sem("e_hi"), sem("e_lo")
        y_hi_ready, y_lo_ready, scatter_ps, x_add = sem("y_hi_ready"), sem("y_lo_ready"), sem("scatter_ps"), sem("x_add")
        pick_r_ready, pick_ready = sem("pick_r_ready"), sem("pick_ready")
        spread_ps, spread_ready = sem("spread_ps"), sem("spread_ready")
        gather_ps, xg_act, xg_dve = sem("gather_ps"), sem("xg_act"), sem("xg_dve")
        col_ready, moe_step = sem("col_ready"), sem("moe_step")

        early_raw = {MOE0 + RAW // 2: v_buf[:, :],
                     MOE0 + RAW // 2 + 1: bias[:, :, :].rearrange("p h j -> p (h j)")[:, 0:HALF],
                     MOE0 + RAW // 2 + 2: k_buf[:, :]}

        def load_half(sp, n, src, cyc=0, slot_free=False):
            if n >= RAW and not slot_free:
                sp.wait_ge(lo_ready, n - RAW + 1 + RAW * cyc)
            dst = w_raw[:, n % RAW, :]
            sp.dma_start(dst.rearrange("p (a b) -> p a b", a=src.shape[1]), src).then_inc(landed[n % RAW], 16)

        def load_early(sp, n, src):
            sp.wait_ge(lo_ready, n - RAW + 1)
            sp.sem_inc(landed[n % RAW], 16)
            dst = early_raw[n]
            sp.dma_start(dst.rearrange("p (a b) -> p a b", a=src.shape[1]), src).then_inc(early_in[n], 16)

        def split_hi(act, n, cyc=0, early=False):
            act.wait_ge(landed[n % RAW], 16 * (n // RAW + 1) + 16 * cyc)
            if early:
                act.wait_ge(early_in[n], 16)
            if n >= SPLIT:
                act.wait_ge(half_used, n - SPLIT + 1 + RAW * cyc)
            act.activation(w_hi[:, n % SPLIT, :], early_raw[n] if early else w_raw[:, n % RAW, :],
                           ACT.Copy).then_inc(hi_ready, 1)

        def split_lo(eng, n, cyc=0, early=False):
            eng.wait_ge(hi_ready, n + 1 + RAW * cyc)
            eng.tensor_tensor(w_lo[:, n % SPLIT, :], early_raw[n] if early else w_raw[:, n % RAW, :], w_hi[:, n % SPLIT, :],
                              ALU.subtract).then_inc(lo_ready, 1)

        def product(pe, dst, hi, lo, whi, wlo, first, last):
            pe.matmul(dst, hi, whi, start=first, stop=False, skip_group_check=True)
            pe.matmul(dst, hi, wlo, start=False, stop=False, skip_group_check=True)
            return pe.matmul(dst, lo, whi, start=False, stop=last, skip_group_check=True)

        def half_parts(n, rows_, c):
            a = w_hi[:, n % SPLIT, :].rearrange("p (k c) -> p k c", k=rows_)[:, c]
            b = w_lo[:, n % SPLIT, :].rearrange("p (k c) -> p k c", k=rows_)[:, c]
            return a, b

        def unit_out(eng, layer, u):
            kind, i = UNIT[u]
            if kind in ("q", "k", "cb"):
                eng.wait_ge(act_rows, ACT_ROWS[layer, (kind, i)])
            else:
                ready, per_layer = {"v": (v_ready, 4), "ch": (ch_ready, 4), "cc": (dve_rows, 4),
                                    "ga": (sig_ready, 8), "gc": (sig_ready, 8), "conv": (merged_conv, 4),
                                    "attn": (merged_attn, 4), "wo": (x_new, 8)}[kind]
                eng.wait_ge(ready, per_layer * layer + 2 * i + (6 if kind == "gc" else 2))

        def job_out(eng, layer, job):
            kind, i = job
            head, both = HEADS * layer + i, 2 * layer + i
            if kind == "scores":
                eng.wait_ge(biased, head + 1)
            elif kind == "turn_w":
                eng.wait_ge(wgtT_ready, head + 1)
            elif kind == "values":
                eng.wait_ge(o_out, head + 1)
            elif kind == "turn_a":
                eng.wait_ge(aT_lo_ready, head + 1)
            elif kind == "turn_qk":
                eng.wait_ge(qk_ready, 2 * (4 * layer + i) + 2)
            elif kind == "turn_u":
                eng.wait_ge(uT_ready, 2 * both + 2)
            elif kind == "turn_b":
                eng.wait_ge(c_ready, 2 * both + 2)
            else:
                eng.wait_ge(mT_lo_ready, 2 * both + 2)

        def job_in_bank(eng, layer, job, b):
            eng.wait_ge(bank_full[b], BANK_USES[b] * layer + BANK_AT[job, b])

        def rows_turned(eng, layer, s):
            past = [j for t in range(s) for j in JOBS[t] if j[0] in TURNS_OF_ROWS]
            if past:
                job_in_bank(eng, layer, past[-1], 5)

        def cols_of(w, c0, hf):
            return w.rearrange("(k p) n -> p k n", p=P)[:, 4 * hf:4 * hf + 4, c0:c0 + CHUNK]

        def mixer_source(layer, s):
            u, hf = unit_of(s)
            kind, i = UNIT[u]
            if kind in W_IN_COL:
                return cols_of(w_in[layer], W_IN_COL[kind] + CHUNK * i, hf)
            return cols_of({"conv": w_o_conv, "attn": w_o_attn, "wo": w_o}[kind][layer], CHUNK * i, hf)

        gu_view = dense_gu[0].rearrange("(k p) (two n) -> p k two n", p=P, two=2)
        down_view = dense_down[0].rearrange("(j p) n -> p j n", p=P)

        def bank_quads(b):
            return bank[b][:, :].rearrange("p (c n) -> p c n", n=P)

        block = ctx.enter_context(nc.Block())

        @block.sync
        def _(sp):
            for t in range(TT):
                sp.dma_start(X[:, t, :], x[0, P * t:P * t + P, :]).then_inc(x_in[t], 16)
            sp.dma_start(gain, mix_norm_g[0].partition_broadcast(P)).then_inc(gain_in, 16)
            load_half(sp, 0, mixer_source(0, 0))
            load_half(sp, 1, mixer_source(0, 1))
            sp.dma_start(relb[0:NBUCKETS, :], rel_bias).then_inc(relb_in, 16)
            sp.dma_start(bucket, bucket_of).then_inc(bucket_in, 16)
            sp.dma_start(conv_rows[:, :], conv_w.rearrange("l w (c p) -> (l w c) p", p=P)).then_inc(conv_in, 16)
            load_half(sp, 2, mixer_source(0, 2))
            sp.dma_start(lam_flat, lam_qk.rearrange("l i d -> (l i d)").partition_broadcast(P)).then_inc(lam_in, 16)
            sp.dma_start(gsub[:, :, :].rearrange("p l e -> p (l e)"),
                         subln_g.rearrange("l e -> (l e)").partition_broadcast(P)).then_inc(sub_in, 16)
            for s in range(3, RAW + 2):
                load_half(sp, s, mixer_source(0, s))
            sp.wait_ge(line_out, 16 * 2)
            for c0, j0, n in ((0, SEQ - 1, P), (P, SEQ - 1 - P, 2 * P)):
                sp.dma_start(bias[:, :, c0:c0 + n],
                             bass.AP(tensor=lines.tensor, offset=j0,
                                     ap=[[LINE - 1, P], [P * LINE, HEADS], [1, n]])).then_inc(bias_in, 16)
            for s in range(RAW + 2, MIX_HALVES):
                load_half(sp, s, mixer_source(0, s))
            n = DENSE0
            for hf in range(2):
                load_half(sp, n + hf, gu_view[:, :, hf, 0:FFW])
            with sp.Fori(0, (FSTEPS - 1) // 2) as it:
                for i in range(2):
                    m = 2 * it + 1 + i
                    for hf in range(2):
                        load_half(sp, n + 2 + 3 * i + hf, gu_view[:, :, hf, bass.ds(FFW * m, FFW)], it)
                    load_half(sp, n + 4 + 3 * i, down_view[:, bass.ds(2 * (m - 1), 2), :], it)
            load_half(sp, n + DENSE_HALVES - 1, down_view[:, 2 * (FSTEPS - 1):2 * FSTEPS, :])
            for s in range(MIX_HALVES):
                load_half(sp, MIX0[1] + s, mixer_source(1, s))

            def stream_expert(e, b, opening=False):
                gu = expert_gu[0, e].rearrange("(k p) (two n) -> p k two n", p=P, two=2)
                down = expert_down[0, e].rearrange("(j p) n -> p j n", p=P)

                def gate_up(i, m):
                    return gu[:, 4 * (i % 2):4 * (i % 2) + 4, i // 2, bass.ds(CHUNK * m, CHUNK)]

                def down_rows(i, m):
                    return down[:, bass.ds(4 * m + 2 * i, 2), :]

                def load_step(m, cyc):
                    for i in range(4):
                        load_half(sp, MOE0 + 4 + i, gate_up(i, m), cyc)
                    for i in range(2):
                        load_half(sp, MOE0 + 8 + i, down_rows(i, m - 1), cyc)

                for i in range(3):
                    load_half(sp, MOE0 + i, gate_up(i, 0), CYCLES * b)
                if opening:
                    job_in_bank(sp, 1, ("values", HEADS - 1), 7)
                    load_early(sp, MOE0 + 3, gate_up(3, 0))
                    sp.wait_ge(biased, DEPTH * HEADS)
                    load_early(sp, MOE0 + 4, gate_up(0, 1))
                    job_in_bank(sp, 1, ("turn_m", 1), 7)
                    load_early(sp, MOE0 + 5, gate_up(1, 1))
                    for i in range(2, 4):
                        load_half(sp, MOE0 + 4 + i, gate_up(i, 1))
                    load_half(sp, MOE0 + 8, down_rows(0, 0))
                    load_half(sp, MOE0 + 9, down_rows(1, 0), slot_free=True)
                    for i in range(2):
                        load_half(sp, MOE0 + 10 + i, gate_up(i, 2), slot_free=True)
                    for i in range(2, 4):
                        load_half(sp, MOE0 + 10 + i, gate_up(i, 2))
                    for i in range(2):
                        load_half(sp, MOE0 + 14 + i, down_rows(i, 1))
                    with sp.Fori(3, MSTEPS) as m:
                        load_step(m, m - 1)
                else:
                    load_half(sp, MOE0 + 3, gate_up(3, 0), CYCLES * b)
                    with sp.Fori(1, MSTEPS) as m:
                        load_step(m, CYCLES * b + m - 1)
                for i in range(2):
                    load_half(sp, MOE0 + BLOCK_HALVES - 2 + i, down_rows(i, MSTEPS - 1), CYCLES * b)

            stream_expert(0, 0, opening=True)
            with sp.Fori(1, EXPERTS) as b:
                stream_expert(b, b)
            sp.wait_ge(route_ready, 1)
            last = sp.value_load(ctl_i[0:1, 0:1], min_val=EXPERTS - 1, max_val=EXPERTS - 1 + SLOTS)
            with sp.If(last >= EXPERTS):
                with sp.Fori(EXPERTS, last + 1) as b:
                    e = sp.value_load(ctl_i[0:1, bass.ds(b - (EXPERTS - 1), 1)], min_val=0, max_val=EXPERTS - 1)
                    stream_expert(e, b)
            for t in range(TT):
                sp.wait_ge(hrow_ready, 2 * 4 + t + 1)
                sp.dma_start(out[0, P * t:P * t + P, :], hrow[:, t, :]).then_inc(out_sent, 16)
            sp.wait_ge(out_sent, 16 * TT)

        @block.gpsimd
        def _(pool):
            pool.memset(ident[:, :], 0.0).then_inc(pool_step, 1)
            pool.memset(ones[:, :], 1.0).then_inc(pool_step, 1)
            pool.memset(uT[:, :, :], 0.0).then_inc(pool_step, 1)
            pool.wait_ge(pool_step, 3)
            pool.affine_select(out=ident[:, :], in_=ident[:, :], compare_op=ALU.not_equal, fill=1.0, base=0,
                               pattern=[[-1, P]], channel_multiplier=1).then_inc(const_ready, 1)
            pool.affine_select(out=before[:, :], in_=ones[:, :], compare_op=ALU.is_gt, fill=0.0, base=0,
                               pattern=[[1, P]], channel_multiplier=-1).then_inc(const_ready, 1)
            pool.iota(iota_1[:, :], pattern=[[1, P]], base=1, channel_multiplier=0,
                      allow_small_or_imprecise_dtypes=True).then_inc(const_ready, 1)
            pool.affine_select(out=earlier[:, :, :], in_=ones[:, 0:EXPERTS * EXPERTS].rearrange("p (e j) -> p e j", e=EXPERTS),
                               compare_op=ALU.is_gt, fill=0.0, base=0,
                               pattern=[[1, EXPERTS], [-1, EXPERTS]], channel_multiplier=0).then_inc(const_ready, 1)

            count = [3]

            def chain(ins):
                count[0] += 1
                ins.then_inc(pool_step, 1)
                pool.wait_ge(pool_step, count[0])

            def norm_split(q):
                pool.wait_ge(lo_ready, NORM_AT[q] + 1)
                split_lo(pool, NORM_AT[q] + 1)

            norm_split(0)
            for i in range(SLOTS):
                chain(pool.memset(slot_no[:, i, :], float(i)))
            chain(pool.iota(src[:, 0, :], pattern=[[1, EXPERTS]], base=0, channel_multiplier=0,
                            allow_small_or_imprecise_dtypes=True))
            chain(pool.memset(seats[:, :, EXPERTS:COLS], 0.0))
            chain(pool.memset(ctl[:, :], 0.0))

            v, t_, y = head_nw[0][:, :], head_nw[1][:, :], head_nwi[:, :].bitcast(F32)
            def head_norm(head):
                pool.wait_ge(o_ss, 2 * head + 2)
                chain(pool.tensor_scalar(v, head_ss[:, :], 1.0 / P, EPS, ALU.mult, ALU.add))
                chain(pool.tensor_scalar(head_nwi[:, :], v.bitcast(I32), -0.5, float(0x5F3759DF), ALU.mult, ALU.add))
                chain(pool.tensor_scalar(v, v, -0.5, None, ALU.mult))
                for _ in range(3):
                    chain(pool.tensor_tensor(t_, y, y, ALU.mult))
                    chain(pool.tensor_tensor(t_, t_, v, ALU.mult))
                    chain(pool.tensor_scalar(t_, t_, 1.5, None, ALU.add))
                    chain(pool.tensor_tensor(y, t_, y, ALU.mult))
                pool.wait_ge(o_out, head + 1)
                for t in range(TT):
                    pool.tensor_scalar(arow[:, t, :], arow[:, t, :], y[:, t:t + 1], None, ALU.mult).then_inc(scaled, 1)
                for t in range(TT):
                    pool.wait_ge(scaled, 2 * head + t + 1)
                    pool.tensor_tensor(arow[:, t, :], arow[:, t, :], gsub[:, head // HEADS, :],
                                       ALU.mult).then_inc(arow_ready, 1)

            for layer in range(DEPTH):
                if layer:
                    norm_split(2)
                else:
                    pool.wait_ge(gsub_ready, 1)
                for h in range(HEADS):
                    head_norm(HEADS * layer + h)
                norm_split(2 * layer + 1)

            for t in range(TT):
                pool.wait_ge(hr_hi_ready, t + 1)
                pool.tensor_tensor(hr_lo[:, t, :], hrow[:, t, :], hr_hi[:, t, :], ALU.subtract).then_inc(hr_lo_ready, 1)

            pool.wait_ge(places_out, 1)
            chain(pool.tensor_scalar(over[:, :], places[:, 2, :], float(P), None, ALU.is_gt))
            a, b = over, count_a
            for step in (1, 2, 4):
                chain(pool.tensor_copy(b[:, 0:step], a[:, 0:step]))
                chain(pool.tensor_tensor(b[:, step:EXPERTS], a[:, step:EXPERTS], a[:, 0:EXPERTS - step], ALU.add))
                a, b = b, (count_b if b is count_a else count_a)
            chain(pool.tensor_scalar(ctl[:, 0:1], a[:, EXPERTS - 1:EXPERTS], float(EXPERTS - 1), None, ALU.add))
            chain(pool.tensor_tensor(b[:, :], a[:, :], over[:, :], ALU.subtract))
            chain(pool.tensor_tensor(slot_of[:, :, :], slot_no[:, :, :],
                                     b[:, :].unsqueeze(1).to_broadcast([P, SLOTS, EXPERTS]), ALU.subtract))
            chain(pool.tensor_scalar(slot_of[:, :, :], slot_of[:, :, :], 0.0, None, ALU.is_equal))
            chain(pool.tensor_tensor(slot_of[:, :, :], slot_of[:, :, :],
                                     over[:, :].unsqueeze(1).to_broadcast([P, SLOTS, EXPERTS]), ALU.mult))
            pool.wait_ge(first_ready, 1)
            chain(pool.tensor_tensor(beyond[:, :, :], mask[:, :, :], first[:, :, :], ALU.subtract))
            chain(pool.tensor_scalar(src[:, 1:3, :], places[:, 0:2, :], float(P - 1), None, ALU.subtract))
            chain(pool.tensor_tensor(src[:, 1:3, :], src[:, 1:3, :], beyond[:, :, :], ALU.mult))
            pool.wait_ge(gates_ready, 1)
            chain(pool.tensor_copy(src[:, 3:5, :], seats[:, TT:2 * TT, 0:EXPERTS]))
            for i in range(SLOTS):
                chain(pool.tensor_tensor(terms[:, :, i, :], src[:, :, :],
                                         slot_of[:, i:i + 1, :].to_broadcast([P, 5, EXPERTS]), ALU.mult))
            for n in (4, 2):
                chain(pool.tensor_tensor(terms[:, :, :, 0:n], terms[:, :, :, 0:n], terms[:, :, :, n:2 * n], ALU.add))
            chain(pool.tensor_tensor(found[:, :, :], terms[:, :, :, 0], terms[:, :, :, 1], ALU.add))
            chain(pool.tensor_copy(seats[:, :, EXPERTS:EXPERTS + SLOTS], found[:, 1:5, :]))
            chain(pool.tensor_copy(ctl[:, 1:1 + SLOTS], found[:, 0, :]))
            pool.tensor_copy(ctl_i[:, :], ctl[:, :]).then_inc(route_ready, 1)

        @block.scalar
        def _(act):
            def bias_lines():
                for h in range(HEADS):
                    act.wait_ge(line_ps, h + 1)
                    act.activation(bias[:, h, :], bank[4 + h % 4][:, 0:LINE], ACT.Copy).then_inc(line_sb, 1)
                    if h == 0:
                        act.wait_ge(conv_ps, 1)
                        act.activation(convT[:, :, :, :].rearrange("p l w c -> p (l w c)"),
                                       bank[4][:, LINE:LINE + DEPTH * 3 * KC], ACT.Copy).then_inc(conv_sb, 1)
                    if h % 4 == 3:
                        act.wait_ge(line_sb, h + 1)
                        act.dma_start(lines[h - 3:h + 1].rearrange("h p j -> p h j"),
                                      bias[:, h - 3:h + 1, :]).then_inc(line_out, 16)
                act.wait_ge(lam_sums, 1)
                act.activation(lam4[:, :, :], lam4[:, :, :], ACT.Exp).then_inc(lam_exp, 1)

            def norm_sums(q, t):
                if q == 0:
                    act.wait_ge(x_in[t], 16)
                elif t == 0:
                    act.wait_ge(hrow_ready, 2 * q)
                if q:
                    act.wait_ge(x_new, X_ADDS[q] - 2 * (TT - 1 - t))
                if q or t:
                    act.wait_ge(ss_ready, 2 * q + t)
                act.activation(part[:, :], X[:, t, :], ACT.Square,
                               accum_out=ssq[:, t:t + 1]).then_inc(ss_ready, 1)

            def norm_hi(q, t):
                for g in range(2):
                    act.wait_ge(norm_ps, 4 * q + 2 * t + g + 1)
                    act.activation(k_tok(hT_hi)[:, 4 * g:4 * g + 4, P * t:P * t + P],
                                   bank_quads(NORM_BANK[q] + 2 * t + g), ACT.Copy).then_inc(hT_hi_ready, 1)

            def norm(q):
                norm_sums(q, 0)
                if q == 0:
                    norm_sums(q, 1)
                    split_hi(act, 0)
                    norm_hi(q, 0)
                    split_hi(act, 1)
                else:
                    split_hi(act, NORM_AT[q] + 1)
                    norm_hi(q, 0)
                    norm_sums(q, 1)
                norm_hi(q, 1)

            def next_gain(q, source):
                act.wait_ge(hrow_ready, 2 * q)
                act.wait_ge(cT_lo_ready, q + 1)
                act.dma_start(gain, source.partition_broadcast(P)).then_inc(gain_in, 16)

            def mixer(layer):
                n0 = MIX0[layer]
                for s in range(MIX_HALVES + 1):
                    if s < MIX_HALVES - 1:
                        split_hi(act, n0 + s + 2)
                    if s == 38 and layer == 1:
                        act.wait_ge(rtr_in, 16)
                        act.activation(rtr_parts[:, :, 0, :], rtr[:, :].rearrange("p (k e) -> p k e", e=EXPERTS),
                                       ACT.Copy).then_inc(rtr_hi_ready, 1)
                    if s == 2 and layer == 0:
                        bias_lines()
                    if s == 30 and layer == 0:
                        next_gain(1, ffn_norm_g[0])
                    if s == 30 and layer == 1:
                        next_gain(3, ffn_norm_g[1])
                        act.dma_start(rtr[:, :].rearrange("p (k e) -> p k e", e=EXPERTS),
                                      router_w[0].rearrange("(k p) e -> p k e", p=P)).then_inc(rtr_in, 16)
                    for kind, i in JOBS[s - 1] if s else []:
                        if kind == "scores":
                            act.wait_ge(biased, HEADS * layer + i + 1)
                            for t, c0, c1 in ((0, 0, P), (1, P, LINE)):
                                for m in range(2):
                                    act.activation(prob[:, m, c0:c1], prob[:, m, c0:c1], ACT.Exp,
                                                   bias=nmax[:, 2 * t + m:2 * t + m + 1],
                                                   accum_out=psum_row[:, 2 * t + m:2 * t + m + 1]).then_inc(exp_ready, 1)
                    for u in range(UNITS):
                        if last_half(u) != s - 1:
                            continue
                        banks = [bank[2 * (u % 2) + t] for t in range(TT)]
                        kind, i = UNIT[u]
                        if kind in ("conv", "attn", "wo"):
                            continue
                        if kind != "cc":
                            act.wait_ge(half_used, n0 + s)
                        if kind in ("q", "k", "cb"):
                            rows_turned(act, layer, s)
                            for t in range(TT):
                                act.activation(tok_c(rows)[:, t], banks[t][:, :], ACT.Copy,
                                               scale=HD ** -0.5 if kind == "q" else 1.0).then_inc(act_rows, 1)
                        if kind == "v":
                            for t in range(TT):
                                act.activation(v_rows[:, t, CHUNK * i:CHUNK * (i + 1)], banks[t][:, :],
                                               ACT.Copy).then_inc(v_ready, 1)
                        if kind == "ch":
                            for t in range(TT):
                                act.activation(tok_c(part)[:, t], banks[t][:, :], ACT.Copy).then_inc(ch_ready, 1)
                        if kind == "ga":
                            if i:
                                rows_turned(act, layer, s)
                            for t in range(TT):
                                act.activation(sig_attn[i][:, t], banks[t][:, :], ACT.Sigmoid).then_inc(sig_ready, 1)
                        if kind == "gc":
                            if i == 0:
                                job_in_bank(act, layer, ("scores", HEADS - 1), 5)
                            for t in range(TT):
                                act.activation(sig_conv[:, t, CHUNK * i:CHUNK * (i + 1)], banks[t][:, :],
                                               ACT.Sigmoid).then_inc(sig_ready, 1)
                    for kind, i in JOBS[s - 1] if s else []:
                        def full(b):
                            job_in_bank(act, layer, (kind, i), b)
                        if kind == "turn_w":
                            full(6)
                            if i or layer:
                                pl, ph = (layer, i - 1) if i else (layer - 1, HEADS - 1)
                                job_in_bank(act, pl, ("values", ph), 7)
                            act.activation(wgtT[:, :], bank[6][:, 0:LINE], ACT.Copy).then_inc(wgtT_ready, 1)
                        if kind == "values":
                            full(7)
                            if i or layer:
                                pl, ph = (layer, i - 1) if i else (layer - 1, HEADS - 1)
                                job_in_bank(act, pl, ("turn_a", ph), 6)
                            for t in range(TT):
                                act.activation(squares[:, t, :], bank[7][:, P * t:P * t + P], ACT.Square,
                                               accum_out=head_ss[:, t:t + 1]).then_inc(o_ss, 1)
                            act.activation(arow[:, :, :].rearrange("p t e -> p (t e)"), bank[7][:, 0:SEQ],
                                           ACT.Copy).then_inc(o_out, 1)
                        if kind == "turn_a":
                            full(6)
                            act.activation(k_tok(aT_hi)[:, i, :], bank[6][:, 0:SEQ], ACT.Copy).then_inc(aT_hi_ready, 1)
                        if kind == "turn_qk":
                            buf = kT if i % 2 else qT
                            for t in range(TT):
                                full(4 + t)
                                act.activation(buf[:, 4 * (i // 2):4 * (i // 2) + 4, P * t:P * t + P],
                                               bank_quads(4 + t), ACT.Copy).then_inc(qk_ready, 1)
                        if kind == "turn_u":
                            if i or layer:
                                act.wait_ge(yT_ready, 4 * (2 * layer + i))
                            for t in range(TT):
                                full(4 + t)
                                act.activation(uT[:, :, 2 + P * t:2 + P * t + P], bank_quads(4 + t),
                                               ACT.Copy).then_inc(uT_ready, 1)
                            if i:
                                act.wait_ge(cT_lo_ready, 2 * layer + i)
                            act.wait_ge(uT_ready, 2 * (2 * layer + i) + 2)
                            for c in range(4):
                                act.activation(yTv[:, c, :], uT[:, c, 2:2 + SEQ], ACT.Copy,
                                               scale=convT[:, layer, 2, 4 * i + c:4 * i + c + 1]).then_inc(tap_ready, 1)
                        if kind == "turn_b":
                            act.wait_ge(c_ready, 2 * (2 * layer + i) + 2)
                            act.activation(k_tok(cT_hi)[:, 4 * i:4 * i + 4, :], yTv, ACT.Copy).then_inc(cT_hi_ready, 1)
                        if kind == "turn_m":
                            for t in range(TT):
                                full(6 + t)
                                act.activation(k_tok(hT_hi)[:, 4 * i:4 * i + 4, P * t:P * t + P], bank_quads(6 + t),
                                               ACT.Copy).then_inc(mT_hi_ready, 1)

            def dense():
                def silu(m):
                    for t in range(TT):
                        act.wait_ge(d_rows, 2 * m + 1)
                        act.activation(tok_c(part)[:, t, 0:FFW], bank[t][:, 0:FFW], ACT.Silu).then_inc(d_silu, 1)

                def turn_hi(m):
                    act.wait_ge(d_turn, m + 1)
                    act.activation(ffT_hi, bank[2][:, :], ACT.Copy).then_inc(d_hi, 1)

                n0 = DENSE0
                split_hi(act, n0 + 2)
                act.wait_ge(half_used, n0 + 2)
                silu(0)
                split_hi(act, n0 + 3)
                with act.Fori(0, (FSTEPS - 1) // 2) as it:
                    for i in range(2):
                        m = 2 * it + 1 + i
                        n = n0 + 2 + 3 * i
                        split_hi(act, n + 2, it)
                        turn_hi(m - 1)
                        split_hi(act, n + 3, it)
                        split_hi(act, n + 4, it)
                        act.wait_ge(half_used, n + 2 + RAW * it)
                        silu(m)
                turn_hi(FSTEPS - 1)

            def experts():
                act.wait_ge(hrow_ready, 8)
                for t in range(TT):
                    act.activation(hr_hi[:, t, :], hrow[:, t, :], ACT.Copy).then_inc(hr_hi_ready, 1)
                split_hi(act, MOE0 + 2)
                act.wait_ge(gap_ready, 1)
                act.activation(gap[:, :], gap[:, :], ACT.Exp).then_inc(gap_exp, 1)
                act.wait_ge(seats_ready, 1)
                act.activation(places[:, :, :].rearrange("p a e -> p (a e)"), bank[5][:, 0:3 * EXPERTS],
                               ACT.Copy).then_inc(places_out, 1)

                def gathered(g):
                    for i, b, dst in ((0, 6, xg_hi[:, 0:CHUNK]), (2, 3, xg_lo[:, 0:CHUNK])):
                        act.wait_ge(gather_ps, 4 * g + i + 1)
                        act.activation(dst, bank[b][:, :], ACT.Copy).then_inc(xg_act, 1)

                def take_y(b):
                    act.wait_ge(half_used, MOE0 + BLOCK_HALVES * b)
                    act.wait_ge(spread_ready, 2 * b)
                    for hf in range(2):
                        act.activation(y_hi[:, CHUNK * hf:CHUNK * (hf + 1)], bank[4 + hf][:, :], ACT.Copy,
                                       scale=gate[:, 0:1]).then_inc(y_hi_ready, 1)

                def silu(b, m):
                    act.wait_ge(e_rows, MSTEPS * b + m + 1)
                    act.activation(part[:, 0:CHUNK], bank[0][:, :], ACT.Silu).then_inc(e_silu, 1)

                def turn_hi(b, m):
                    act.wait_ge(e_turn, MSTEPS * b + m + 1)
                    act.activation(ffT_hi, bank[2][:, :], ACT.Copy).then_inc(e_hi, 1)

                def block(b, opening=False, closing=False):
                    c = CYCLES * b
                    if not opening:
                        split_hi(act, MOE0, c)
                        split_hi(act, MOE0 + 1, c)
                        take_y(b)
                        split_hi(act, MOE0 + 2, c)
                    for i in range(3, 6):
                        split_hi(act, MOE0 + i, c, early=opening)
                    act.wait_ge(half_used, MOE0 + 4 + BLOCK_HALVES * b)
                    silu(b, 0)
                    act.wait_ge(spread_ps, b + 1)
                    act.activation(spread_r, bank[7][:, 0:SEQ].rearrange("p (t j) -> p t j", t=TT),
                                   ACT.Copy).then_inc(spread_ready, 1)
                    act.activation(gate[:, :], bank[7][:, SEQ:SEQ + 1], ACT.Copy).then_inc(spread_ready, 1)
                    with act.Fori(1, MSTEPS) as m:
                        cm = c + m - 1
                        split_hi(act, MOE0 + 6, cm)
                        turn_hi(b, m - 1)
                        for i in range(7, 11):
                            split_hi(act, MOE0 + i, cm)
                        act.wait_ge(half_used, MOE0 + 8 + RAW * cm)
                        silu(b, m)
                        split_hi(act, MOE0 + 11, cm)
                    turn_hi(b, MSTEPS - 1)
                    if not closing:
                        gathered(b + 1)

                act.wait_ge(moe_init, 1)
                gathered(0)
                block(0, opening=True)
                act.wait_ge(route_ready, 1)
                last = act.value_load(ctl_i[0:1, 0:1], min_val=EXPERTS - 1, max_val=EXPERTS - 1 + SLOTS)
                with act.Fori(1, last) as b:
                    block(b)
                block(last, closing=True)
                blocks = last + 1
                take_y(blocks)
                return blocks

            norm(0)
            mixer(0)
            norm(1)
            act.wait_ge(hrow_ready, 4)
            act.dma_start(gain, mix_norm_g[1].partition_broadcast(P)).then_inc(gain_in, 16)
            dense()
            norm(2)
            mixer(1)
            norm(3)
            act.wait_ge(hrow_ready, 8)
            act.dma_start(gain, final_norm_g.partition_broadcast(P)).then_inc(gain_in, 16)
            blocks = experts()
            act.wait_ge(e_rows, MSTEPS * EXPERTS)
            for t in range(TT):
                act.wait_ge(x_add, 4 * blocks + 2 * (t + 1))
                act.activation(part[:, :], X[:, t, :], ACT.Square, accum_out=ssq[:, t:t + 1]).then_inc(ss_ready, 1)
                act.wait_ge(ss_ready, 8 + t + 1)

        @block.vector
        def _(dve):
            count = [0]

            def chain(ins):
                count[0] += 1
                ins.then_inc(dve_step, 1)
                dve.wait_ge(dve_step, count[0])

            def rsqrt_of(sums, scale, t_):
                v, t, y = nw[0][:, t_], nw[1][:, t_], nwi[:, t_].bitcast(F32)
                chain(dve.tensor_scalar(v, sums, scale, EPS, ALU.mult, ALU.add))
                chain(dve.tensor_scalar(nwi[:, t_], v.bitcast(I32), -0.5, float(0x5F3759DF), ALU.mult, ALU.add))
                chain(dve.tensor_scalar(v, v, -0.5, None, ALU.mult))
                for _ in range(3):
                    chain(dve.tensor_tensor(t, y, y, ALU.mult))
                    chain(dve.tensor_tensor(t, t, v, ALU.mult))
                    chain(dve.scalar_tensor_tensor(out=y, in0=t, scalar=1.5, in1=y, op0=ALU.add, op1=ALU.mult))
                return y

            def norm_rows(q, t):
                dve.wait_ge(ss_ready, 2 * q + t + 1)
                y = rsqrt_of(ssq[:, t:t + 1], 1.0 / D, slice(t, t + 1))
                dve.wait_ge(gain_in, 16 * (q + 1))
                dve.scalar_tensor_tensor(out=hrow[:, t, :], in0=X[:, t, :], scalar=y, in1=gain,
                                         op0=ALU.mult, op1=ALU.mult).then_inc(hrow_ready, 1)

            def add_sums(q, t):
                if t == 0:
                    dve.wait_ge(sum_ps, q)
                else:
                    dve.wait_ge(half_used, NORM_AT[q])
                for hf in range(2):
                    b = 4 + 2 * t + hf if q == 2 else 2 * hf + t
                    cols = slice(CHUNK * hf, CHUNK * (hf + 1))
                    dve.tensor_tensor(X[:, t, cols], X[:, t, cols], bank[b][:, :], ALU.add).then_inc(x_new, 1)

            def norm_lo(q, t):
                for g in range(2):
                    dve.wait_ge(hT_hi_ready, 4 * q + 2 * t + g + 1)
                    dve.tensor_tensor(k_tok(hT_lo)[:, 4 * g:4 * g + 4, P * t:P * t + P],
                                      bank_quads(NORM_BANK[q] + 2 * t + g),
                                      k_tok(hT_hi)[:, 4 * g:4 * g + 4, P * t:P * t + P],
                                      ALU.subtract).then_inc(hT_lo_ready, 1)

            def norm(q):
                if q:
                    add_sums(q, 0)
                norm_rows(q, 0)
                if q:
                    add_sums(q, 1)
                    norm_lo(q, 0)
                norm_rows(q, 1)
                if q == 0:
                    split_lo(dve, 0)
                    norm_lo(q, 0)
                norm_lo(q, 1)
                dve.wait_ge(lo_ready, NORM_AT[q] + 2)

            def mixer(layer):
                n0 = MIX0[layer]

                for s in range(MIX_HALVES + 1):
                    if s == 1 and layer == 0:
                        constants()
                    if s == 8 and layer == 0:
                        lambdas()

                    def full(b):
                        job_in_bank(dve, layer, (kind, i), b)
                    jobs = JOBS[s - 1] if s else []
                    for kind, i in jobs:
                        if kind == "scores":
                            for m in range(2):
                                full(4 + m)
                                if i == 0 and m == 0 and layer == 0:
                                    dve.wait_ge(bias_in, 16 * 2)
                                chain(dve.tensor_tensor(prob[:, m, :], bank[4 + m][:, 0:LINE], bias[:, i, :],
                                                        ALU.add))
                            chain(dve.tensor_reduce(nmax[:, 0:2], prob[:, :, 0:P], AX, ALU.max, negate=True))
                            dve.tensor_reduce(nmax[:, 2:4], prob[:, :, P:LINE], AX, ALU.max,
                                              negate=True).then_inc(biased, 1)
                    if s == 38 and layer == 1:
                        dve.wait_ge(rtr_hi_ready, 1)
                        dve.tensor_tensor(rtr_parts[:, :, 1, :], rtr[:, :].rearrange("p (k e) -> p k e", e=EXPERTS),
                                          rtr_parts[:, :, 0, :], ALU.subtract).then_inc(rtr_lo_ready, 1)
                    for u in range(UNITS):
                        if last_half(u) != s - 1:
                            continue
                        banks = [bank[2 * (u % 2) + t] for t in range(TT)]
                        kind, i = UNIT[u]
                        if kind == "wo":
                            continue
                        cols = slice(CHUNK * i, CHUNK * (i + 1))
                        if kind in ("cc", "conv", "attn"):
                            dve.wait_ge(half_used, n0 + s)
                        if kind == "cc":
                            dve.wait_ge(ch_ready, 4 * layer + 2 * i + 2)
                            rows_turned(dve, layer, s)
                            for t in range(TT):
                                dve.tensor_tensor(tok_c(rows)[:, t], banks[t][:, :], tok_c(part)[:, t],
                                                  ALU.mult).then_inc(dve_rows, 1)
                        if kind == "conv":
                            dve.wait_ge(sig_ready, 8 * (layer + 1))
                            for t in range(TT):
                                dve.tensor_tensor(sig_conv[:, t, cols], banks[t][:, :], sig_conv[:, t, cols],
                                                  ALU.mult).then_inc(merged_conv, 1)
                        if kind == "attn":
                            for t in range(TT):
                                dve.tensor_tensor(sig_attn[i][:, t], banks[t][:, :], sig_attn[i][:, t],
                                                  ALU.mult).then_inc(merged_attn, 1)
                            dve.wait_ge(merged_attn, 4 * layer + 2 * i + 2)
                            dve.wait_ge(merged_conv, 4 * layer + 2 * i + 2)
                            for t in range(TT):
                                dve.tensor_tensor(merged[:, t, cols], sig_attn[i][:, t], sig_conv[:, t, cols],
                                                  ALU.add).then_inc(merged_ready, 1)
                    if s < MIX_HALVES - 1:
                        split_lo(dve, n0 + s + 2)
                    for kind, i in jobs:
                        head = HEADS * layer + i
                        if kind == "scores":
                            dve.wait_ge(exp_ready, 4 * head + 4)
                            chain(dve.reciprocal(recip[:, :], psum_row[:, :]))
                            chain(dve.tensor_scalar(recip[:, 1:4:2], recip[:, 1:4:2], neg_lam[:, layer:layer + 1],
                                                    None, ALU.mult))
                            if head:
                                pl, ph = (layer, i - 1) if i else (layer - 1, HEADS - 1)
                                job_in_bank(dve, pl, ("turn_w", ph), 6)
                            for t, c0, c1 in ((0, 0, P), (1, P, LINE)):
                                dve.tensor_scalar(wgt[:, c0:c1], prob[:, 0, c0:c1], recip[:, 2 * t:2 * t + 1], None,
                                                  ALU.mult).then_inc(dve_step, 1)
                            count[0] += 2
                            dve.wait_ge(dve_step, count[0])
                            for t, c0, c1 in ((0, 0, P), (1, P, LINE)):
                                dve.scalar_tensor_tensor(out=wgt[:, c0:c1], in0=prob[:, 1, c0:c1],
                                                         scalar=recip[:, 2 * t + 1:2 * t + 2], in1=wgt[:, c0:c1],
                                                         op0=ALU.mult, op1=ALU.add).then_inc(wgt_ready, 1)
                            dve.wait_ge(wgt_ready, 2 * head + 2)
                        if kind == "turn_a":
                            dve.wait_ge(aT_hi_ready, head + 1)
                            dve.tensor_tensor(k_tok(aT_lo)[:, i, :], bank[6][:, 0:SEQ], k_tok(aT_hi)[:, i, :],
                                              ALU.subtract).then_inc(aT_lo_ready, 1)
                        if kind == "turn_u":
                            dve.wait_ge(uT_ready, 2 * (2 * layer + i) + 2)
                            dve.wait_ge(conv_sb, 1)
                            dve.wait_ge(tap_ready, 4 * (2 * layer + i) + 4)
                            for tap in (1, 0):
                                for c in range(4):
                                    w = convT[:, layer, tap, 4 * i + c:4 * i + c + 1]
                                    src = uT[:, c, tap:tap + SEQ]
                                    ins = dve.scalar_tensor_tensor(out=yTv[:, c, :], in0=src, scalar=w,
                                                                   in1=yTv[:, c, :], op0=ALU.mult, op1=ALU.add)
                                    ins.then_inc(dve_step if tap else yT_ready, 1)
                                if tap:
                                    count[0] += 4
                                    dve.wait_ge(dve_step, count[0])
                        if kind == "turn_b":
                            for t in range(TT):
                                full(4 + t)
                                dve.wait_ge(yT_ready, 4 * (2 * layer + i) + 4)
                                dve.tensor_tensor(yTv[:, :, P * t:P * t + P], bank_quads(4 + t),
                                                  yTv[:, :, P * t:P * t + P], ALU.mult).then_inc(c_ready, 1)
                            dve.wait_ge(cT_hi_ready, 2 * layer + i + 1)
                            dve.tensor_tensor(k_tok(cT_lo)[:, 4 * i:4 * i + 4, :], yTv,
                                              k_tok(cT_hi)[:, 4 * i:4 * i + 4, :],
                                              ALU.subtract).then_inc(cT_lo_ready, 1)
                        if kind == "turn_m":
                            for t in range(TT):
                                dve.wait_ge(mT_hi_ready, 2 * (2 * layer + i) + t + 1)
                                dve.tensor_tensor(k_tok(hT_lo)[:, 4 * i:4 * i + 4, P * t:P * t + P], bank_quads(6 + t),
                                                  k_tok(hT_hi)[:, 4 * i:4 * i + 4, P * t:P * t + P],
                                                  ALU.subtract).then_inc(mT_lo_ready, 1)

            def dense():
                def gated(m):
                    for t in range(TT):
                        dve.wait_ge(d_silu, 2 * m + t + 1)
                        if t == 0:
                            dve.wait_ge(d_lo, m + 1)
                        dve.tensor_tensor(tok_c(rows)[:, t, 0:FFW], bank[t][:, FFW:2 * FFW], tok_c(part)[:, t, 0:FFW],
                                          ALU.mult).then_inc(d_rows, 1)

                def turn_lo(m):
                    dve.wait_ge(d_hi, m + 1)
                    dve.tensor_tensor(ffT_lo, bank[2][:, :], ffT_hi, ALU.subtract).then_inc(d_lo, 1)

                n0 = DENSE0
                split_lo(dve, n0 + 2)
                gated(0)
                split_lo(dve, n0 + 3)
                with dve.Fori(0, (FSTEPS - 1) // 2) as it:
                    for i in range(2):
                        m = 2 * it + 1 + i
                        n = n0 + 2 + 3 * i
                        split_lo(dve, n + 2, it)
                        turn_lo(m - 1)
                        split_lo(dve, n + 3, it)
                        split_lo(dve, n + 4, it)
                        gated(m)
                turn_lo(FSTEPS - 1)

            def route():
                square = [P, TT, EXPERTS, EXPERTS]
                dve.wait_ge(const_ready, 4)
                for t in range(TT):
                    dve.wait_ge(logits_ps, t + 1)
                    chain(dve.tensor_copy(logits[:, t, :], bank[t][:, EXPERTS:2 * EXPERTS]))
                    chain(dve.tensor_tensor(logits[:, t, :], bank[t][:, 0:EXPERTS], logits[:, t, :], ALU.add))
                row, col = logits[:, :, :].unsqueeze(2).to_broadcast(square), logits[:, :, :].unsqueeze(3).to_broadcast(square)
                dve.tensor_tensor(beats[:, :, :, :], row, col, ALU.is_gt).then_inc(rank_ready, 1)
                dve.tensor_tensor(ties[:, :, :, :], row, col, ALU.is_equal).then_inc(rank_ready, 1)
                dve.wait_ge(rank_ready, 2)
                chain(dve.tensor_tensor(ties[:, :, :, :], ties[:, :, :, :],
                                        earlier[:, :, :].unsqueeze(1).to_broadcast(square), ALU.mult))
                chain(dve.tensor_tensor(beats[:, :, :, :], beats[:, :, :, :], ties[:, :, :, :], ALU.add))
                chain(dve.tensor_reduce(rank[:, :, :], beats[:, :, :, :], AX, ALU.add))
                dve.tensor_scalar(mask[:, :, :], rank[:, :, :], 2.0, None, ALU.is_lt).then_inc(mask_ready, 1)
                for r in range(2):
                    ins = dve.tensor_scalar(chosen[:, r, :, :], rank[:, :, :], float(r), None, ALU.is_equal)
                    ins.then_inc(rank_ready, 1)
                dve.wait_ge(rank_ready, 4)
                both = [P, 2, TT, EXPERTS]
                for r in range(2):
                    ins = dve.tensor_tensor(picked[:, r, :, :], chosen[:, r, :, :], logits[:, :, :], ALU.mult)
                    ins.then_inc(rank_ready, 1)
                dve.wait_ge(rank_ready, 6)
                chain(dve.tensor_reduce(top[:, :, :], picked[:, :, :, :], AX, ALU.add))
                dve.tensor_tensor(gap[:, :], top[:, 1, :], top[:, 0, :], ALU.subtract).then_inc(gap_ready, 1)
                dve.wait_ge(place_ps, 1)
                place = bank[5][:, 0:TT * EXPERTS].rearrange("p (t e) -> p t e", t=TT)
                dve.wait_ge(mask_ready, 1)
                dve.scalar_tensor_tensor(out=first[:, :, :], in0=place, scalar=float(P), in1=mask[:, :, :],
                                         op0=ALU.is_lt, op1=ALU.mult).then_inc(first_ready, 1)
                dve.wait_ge(first_ready, 1)
                dve.scalar_tensor_tensor(out=seats[:, 0:TT, 0:EXPERTS], in0=place, scalar=1.0, in1=first[:, :, :],
                                         op0=ALU.add, op1=ALU.mult).then_inc(seats_ready, 1)
                dve.wait_ge(seats_ready, 1)
                for t in range(TT):
                    dve.tensor_scalar(pick_r[:, t, :], iota_1[:, :], seats[:, t, 0:1], None,
                                      ALU.is_equal).then_inc(pick_r_ready, 1)
                dve.wait_ge(gap_exp, 1)
                chain(dve.tensor_scalar(top[:, 1, :], gap[:, :], 1.0, None, ALU.add))
                chain(dve.reciprocal(top[:, 0, :], top[:, 1, :]))
                chain(dve.tensor_tensor(top[:, 1, :], gap[:, :], top[:, 0, :], ALU.mult))
                chain(dve.tensor_tensor(picked[:, :, :, :], chosen[:, :, :, :],
                                        top[:, :, :].unsqueeze(3).to_broadcast(both), ALU.mult))
                dve.tensor_tensor(seats[:, TT:2 * TT, 0:EXPERTS], picked[:, 0, :, :], picked[:, 1, :, :],
                                  ALU.add).then_inc(gates_ready, 1)
                dve.wait_ge(gates_ready, 1)

            def experts():
                for sm, n in ((e_rows, 1), (e_lo, 1), (y_hi_ready, 2), (scatter_ps, 4), (x_add, 4)):
                    dve.sem_inc(sm, n)
                dve.sem_inc(moe_init, 1)
                split_lo(dve, MOE0 + 2)
                route()

                def make_pick(g, rest_only=False):
                    dve.tensor_copy(seat[:, :], seats[:, :, bass.ds(g, 1)].rearrange("p c o -> p (c o)")).then_inc(col_ready, 1)
                    dve.wait_ge(col_ready, g + 1)
                    for t in range(TT):
                        dve.tensor_scalar(pick[:, t, :], iota_1[:, :], seat[:, t:t + 1], None,
                                          ALU.is_equal).then_inc(pick_ready, 1)
                        if not rest_only:
                            dve.tensor_scalar(pick_r[:, t, :], iota_1[:, :], seat[:, t:t + 1], None,
                                              ALU.is_equal).then_inc(pick_r_ready, 1)

                def gathered(g):
                    for i, b, dst in ((1, 7, xg_hi[:, CHUNK:D]), (3, 6, xg_lo[:, CHUNK:D])):
                        dve.wait_ge(gather_ps, 4 * g + i + 1)
                        dve.tensor_copy(dst, bank[b][:, :]).then_inc(xg_dve, 1)

                def take_y(b):
                    for hf in range(2):
                        dve.wait_ge(y_hi_ready, 2 * b + hf + 1)
                        dve.scalar_tensor_tensor(out=y_lo[:, CHUNK * hf:CHUNK * (hf + 1)], in0=bank[4 + hf][:, :],
                                                 scalar=gate[:, 0:1], in1=y_hi[:, CHUNK * hf:CHUNK * (hf + 1)],
                                                 op0=ALU.mult, op1=ALU.subtract).then_inc(y_lo_ready, 1)

                def add_scattered(b):
                    for i, bk in enumerate((6, 7, 3, 6)):
                        t, hf = i // 2, i % 2
                        dve.wait_ge(scatter_ps, 4 * b + i + 1)
                        dve.tensor_tensor(X[:, t, CHUNK * hf:CHUNK * (hf + 1)], X[:, t, CHUNK * hf:CHUNK * (hf + 1)],
                                          bank[bk][:, :], ALU.add).then_inc(x_add, 1)

                def gated(b, m):
                    dve.wait_ge(e_silu, MSTEPS * b + m + 1)
                    dve.wait_ge(e_lo, MSTEPS * b + m + 1)
                    dve.tensor_tensor(rows[:, 0:CHUNK], bank[1][:, :], part[:, 0:CHUNK], ALU.mult).then_inc(e_rows, 1)

                def turn_lo(b, m):
                    dve.wait_ge(e_hi, MSTEPS * b + m + 1)
                    dve.tensor_tensor(ffT_lo, bank[2][:, :], ffT_hi, ALU.subtract).then_inc(e_lo, 1)

                def block(b, opening=False, closing=False):
                    c = CYCLES * b
                    if not opening:
                        split_lo(dve, MOE0, c)
                        split_lo(dve, MOE0 + 1, c)
                        take_y(b)
                        split_lo(dve, MOE0 + 2, c)
                    for i in range(3, 6):
                        split_lo(dve, MOE0 + i, c, early=opening)
                    gated(b, 0)
                    if not opening:
                        add_scattered(b)
                    if not closing:
                        dve.wait_ge(route_ready, 1)
                        dve.wait_ge(spread_ps, b + 1)
                        make_pick(b + 1)
                    with dve.Fori(1, MSTEPS) as m:
                        cm = c + m - 1
                        split_lo(dve, MOE0 + 6, cm)
                        turn_lo(b, m - 1)
                        for i in range(7, 11):
                            split_lo(dve, MOE0 + i, cm)
                        gated(b, m)
                        split_lo(dve, MOE0 + 11, cm)
                    turn_lo(b, MSTEPS - 1)
                    if not closing:
                        gathered(b + 1)

                make_pick(0, rest_only=True)
                gathered(0)
                block(0, opening=True)
                dve.wait_ge(route_ready, 1)
                last = dve.value_load(ctl_i[0:1, 0:1], min_val=EXPERTS - 1, max_val=EXPERTS - 1 + SLOTS)
                with dve.Fori(1, last) as b:
                    block(b)
                block(last, closing=True)
                blocks = last + 1
                take_y(blocks)
                add_scattered(blocks)

            def constants():
                dve.wait_ge(lam_in, 16)
                for i in range(2):
                    chain(dve.tensor_tensor(lamq[:, :, 2 * i, :], lamq[:, :, 2 * i, :], lamq[:, :, 2 * i + 1, :], ALU.mult))
                    chain(dve.tensor_reduce(lam4[:, i, :], lamq[:, :, 2 * i, :], AX, ALU.add))
                dve.sem_inc(lam_sums, 1)
                dve.wait_ge(sub_in, 16)
                for l in range(DEPTH):
                    chain(dve.tensor_scalar(gsub[:, l, :], gsub[:, l, :], 1.0 - lambda_init(l), None, ALU.mult))
                dve.sem_inc(gsub_ready, 1)

            def lambdas():
                dve.wait_ge(lam_exp, 1)
                chain(dve.tensor_tensor(neg_lam[:, :], lam4[:, 1, :], lam4[:, 0, :], ALU.subtract))
                for l in range(DEPTH):
                    chain(dve.tensor_scalar(neg_lam[:, l:l + 1], neg_lam[:, l:l + 1], lambda_init(l), None, ALU.subtract))

            chain(dve.memset(zero_r[:, :].bitcast(F32), 0.0))
            chain(dve.memset(relb[NBUCKETS:64, :], -BIG))
            norm(0)
            dve.wait_ge(relb_in, 16)
            dve.tensor_copy(relb_bc, relb[:, :].unsqueeze(2).to_broadcast([64, HEADS, P])).then_inc(relb_ready, 1)
            mixer(0)
            norm(1)
            dve.sem_inc(d_rows, 1)
            dve.sem_inc(d_lo, 1)
            dense()
            norm(2)
            mixer(1)
            norm(3)
            experts()
            dve.wait_ge(ss_ready, 2 * 4 + TT)
            y = rsqrt_of(ssq[:, 0:TT], 1.0 / D, slice(0, TT))
            dve.wait_ge(gain_in, 16 * 5)
            for t in range(TT):
                dve.scalar_tensor_tensor(out=hrow[:, t, :], in0=X[:, t, :], scalar=y[:, t:t + 1], in1=gain,
                                         op0=ALU.mult, op1=ALU.mult).then_inc(hrow_ready, 1)

        @block.tensor
        def _(pe):
            def bias_lines():
                n = DEPTH * 3 * KC
                pe.wait_ge(conv_in, 16)
                pe.transpose(bank[4][:, LINE:LINE + n], conv_rows[:, :], ident[0:n, 0:n]).then_inc(conv_ps, 1)
                pe.wait_ge(bucket_in, 16)
                pe.wait_ge(relb_ready, 1)
                for h in range(HEADS):
                    if h >= 4:
                        pe.wait_ge(line_sb, h - 3)
                    if h == 4:
                        pe.wait_ge(conv_sb, 1)
                    pe.matmul(bank[4 + h % 4][:, 0:LINE], relb_bc[0:NBUCKETS + 1, h, :], bucket,
                              start=True, stop=True).then_inc(line_ps, 1)

            def norm_turn(q, t):
                pe.wait_ge(hrow_ready, 2 * q + t + 1)
                for g in range(2):
                    for c in range(4):
                        k = 4 * g + c
                        ins = pe.transpose(bank[NORM_BANK[q] + 2 * t + g][:, P * c:P * c + P], hrow[:, t, P * k:P * k + P], ident[:, :])
                    ins.then_inc(norm_ps, 1)

            def mixer(layer):
                n0 = MIX0[layer]
                def half(s, tiles, chunks=range(4)):
                    u, hf = unit_of(s)
                    hi, lo = {"conv": (k_tok(cT_hi), k_tok(cT_lo)),
                              "attn": (k_tok(aT_hi), k_tok(aT_lo))}.get(UNIT[u][0], (k_tok(hT_hi), k_tok(hT_lo)))
                    pe.wait_ge(lo_ready, n0 + s + 1)
                    for t in tiles:
                        for c in chunks:
                            k = 4 * hf + c
                            whi, wlo = half_parts(n0 + s, 4, c)
                            ins = product(pe, bank[2 * (u % 2) + t][:, :], hi[:, k, P * t:P * t + P],
                                          lo[:, k, P * t:P * t + P], whi, wlo, k == 0, k == KC - 1)
                    return ins

                norm_turn(2 * layer, 0)
                for s in range(MIX_HALVES):
                    u, hf = unit_of(s)
                    if hf == 0 and u >= 2:
                        unit_out(pe, layer, u - 2)
                    if s == S_CONV:
                        pe.wait_ge(cT_lo_ready, 2 * (layer + 1))
                    if s in (S_ATTN, S_ATTN + 1):
                        pe.wait_ge(aT_lo_ready, HEADS * layer + HEADS // 2 * (hf + 1))
                    if s in (S_WO, S_WO + 2):
                        pe.wait_ge(mT_lo_ready, 4 * layer + 2 * (hf + 1))
                    if s in (0, MIX_HALVES - 2):
                        continue
                    if s in (1, MIX_HALVES - 1):
                        for t in range(TT):
                            if s == 1:
                                pe.wait_ge(hT_lo_ready, 4 * 2 * layer + 2 * (t + 1))
                            half(s - 1, (t,))
                            if s == 1 and t == 0:
                                half(s, (t,), (0, 1))
                                norm_turn(2 * layer, 1)
                                ins = half(s, (t,), (2, 3))
                            else:
                                ins = half(s, (t,))
                            if s > 1 and t == 0:
                                ins.then_inc(sum_ps, 1)
                        ins.then_inc(half_used, 2)
                    else:
                        half(s, range(TT)).then_inc(half_used, 1)
                    if s == 1 and layer == 0:
                        bias_lines()
                    for job in JOBS[s]:
                        kind, i = job
                        for b in JOB_BANKS[kind]:
                            if JOB_BEFORE[job, b]:
                                job_out(pe, layer, JOB_BEFORE[job, b])
                            elif layer:
                                job_out(pe, layer - 1, LAST_JOB[b])
                            else:
                                pe.wait_ge(line_sb, HEADS)
                        head = HEADS * layer + i
                        if kind in ("turn_qk", "turn_u", "turn_b"):
                            if kind == "turn_u":
                                pe.wait_ge(dve_rows, 2 * (2 * layer + i) + 2)
                            else:
                                source = ROW_UNITS[i if kind == "turn_qk" else 4 + i]
                                pe.wait_ge(act_rows, ACT_ROWS[layer, source])
                            for t in range(TT):
                                for c in range(4):
                                    ins = pe.transpose(bank[4 + t][:, P * c:P * c + P],
                                                       tok_c(rows)[:, t, P * c:P * c + P], ident[:, :])
                                ins.then_inc(bank_full[4 + t], 1)
                        if kind == "turn_m":
                            pe.wait_ge(merged_ready, 2 * (2 * layer + i) + 2)
                            for t in range(TT):
                                for c in range(4):
                                    k = 4 * i + c
                                    ins = pe.transpose(bank[6 + t][:, P * c:P * c + P],
                                                       merged[:, t, P * k:P * k + P], ident[:, :])
                                ins.then_inc(bank_full[6 + t], 1)
                        if kind == "scores":
                            pe.wait_ge(qk_ready, 8 * layer + (4 if i < 4 else 8))
                            for m in range(2):
                                r = slice(HD * m, HD * m + HD)
                                pe.matmul(bank[4 + m][:, 0:P], qT[r, i, 0:P], kT[r, i, 0:P], start=True, stop=True)
                                pe.matmul(bank[4 + m][:, P:LINE], qT[r, i, P:SEQ], kT[r, i, 0:SEQ],
                                          start=True, stop=True).then_inc(bank_full[4 + m], 1)
                        if kind == "turn_w":
                            pe.wait_ge(wgt_ready, 2 * head + 2)
                            for c in range(3):
                                ins = pe.transpose(bank[6][:, P * c:P * c + P], wgt[:, P * c:P * c + P], ident[:, :])
                            ins.then_inc(bank_full[6], 1)
                        if kind == "values":
                            pe.wait_ge(wgtT_ready, head + 1)
                            pe.wait_ge(v_ready, 4 * layer + (2 if i < 4 else 4))
                            e = slice(P * i, P * i + P)
                            pe.matmul(bank[7][:, 0:P], wgtT[:, 0:P], v_rows[:, 0, e], start=True, stop=True)
                            pe.matmul(bank[7][:, P:2 * P], wgtT[:, P:2 * P], v_rows[:, 0, e], start=True, stop=False)
                            pe.matmul(bank[7][:, P:2 * P], wgtT[:, 2 * P:LINE], v_rows[:, 1, e], start=False,
                                      stop=True).then_inc(bank_full[7], 1)
                        if kind == "turn_a":
                            pe.wait_ge(arow_ready, 2 * head + 2)
                            for t in range(TT):
                                ins = pe.transpose(bank[6][:, P * t:P * t + P], arow[:, t, :], ident[:, :])
                            ins.then_inc(bank_full[6], 1)

            def dense():
                n0 = DENSE0
                hi, lo = k_tok(hT_hi), k_tok(hT_lo)

                def tile_half(n, hf, t, chunks=range(KC)):
                    for k in chunks:
                        whi, wlo = half_parts(n + hf, KC, k)
                        ins = product(pe, bank[t][:, FFW * hf:FFW * (hf + 1)], hi[:, k, P * t:P * t + P],
                                      lo[:, k, P * t:P * t + P], whi, wlo, k == 0, k == KC - 1)
                    return ins

                def first_gate_up(n):
                    norm_turn(1, 0)
                    for t in range(TT):
                        pe.wait_ge(hT_lo_ready, 4 + 2 * (t + 1))
                        pe.wait_ge(lo_ready, n + 1)
                        tile_half(n, 0, t)
                        pe.wait_ge(lo_ready, n + 2)
                        if t == 0:
                            tile_half(n, 1, t, range(0, KC // 2))
                            norm_turn(1, 1)
                            tile_half(n, 1, t, range(KC // 2, KC))
                        else:
                            ins = tile_half(n, 1, t)
                    ins.then_inc(half_used, 2)

                def gate_up(n, cyc):
                    for hf in range(2):
                        pe.wait_ge(lo_ready, n + hf + 1 + RAW * cyc)
                        for t in range(TT):
                            ins = tile_half(n, hf, t)
                        ins.then_inc(half_used, 1)

                def turn(m):
                    pe.wait_ge(d_rows, 2 * m + 3)
                    for t in range(TT):
                        for j in range(2):
                            ins = pe.transpose(bank[2][:, SEQ * j + P * t:SEQ * j + P * t + P],
                                               tok_c(rows)[:, t, P * j:P * j + P], ident[:, :])
                    ins.then_inc(d_turn, 1)

                def down(n, cyc, m, closing=False):
                    pe.wait_ge(lo_ready, n + 1 + RAW * cyc)
                    pe.wait_ge(d_lo, m + 2)
                    for t in range(TT):
                        for j in range(2):
                            whi, wlo = half_parts(n, 2, j)
                            at = slice(SEQ * j + P * t, SEQ * j + P * t + P)
                            for hf in range(2):
                                cols = slice(CHUNK * hf, CHUNK * (hf + 1))
                                ins = product(pe, bank[4 + 2 * t + hf][:, :], ffT_hi[:, at], ffT_lo[:, at],
                                              whi[:, cols], wlo[:, cols], False, False)
                        if closing and t == 0:
                            ins.then_inc(sum_ps, 1)
                    ins.then_inc(half_used, 1)

                first_gate_up(n0)
                for b in range(4, 8):
                    pe.matmul(bank[b][:, :], zero_r[:, 0:P], zero_r[:, :], start=True, stop=False, skip_group_check=True)
                turn(0)
                with pe.Fori(0, (FSTEPS - 1) // 2) as it:
                    for i in range(2):
                        m = 2 * it + 1 + i
                        gate_up(n0 + 2 + 3 * i, it)
                        down(n0 + 4 + 3 * i, it, m - 1)
                        turn(m)
                down(n0 + DENSE_HALVES - 1, 0, FSTEPS - 1, closing=True)

            def experts():
                pe.wait_ge(rtr_lo_ready, 1)
                hi, lo = k_tok(hT_hi), k_tok(hT_lo)
                for t in range(TT):
                    norm_turn(3, t)
                    pe.wait_ge(hT_lo_ready, 12 + 2 * (t + 1))
                    for k in range(KC):
                        at = slice(P * t, P * t + P)
                        pe.matmul(bank[t][:, 0:2 * EXPERTS], hi[:, k, at],
                                  rtr_parts[:, k, :, :].rearrange("p a e -> p (a e)"),
                                  start=k == 0, stop=False, skip_group_check=True)
                        ins = pe.matmul(bank[t][:, 0:EXPERTS], lo[:, k, at], rtr_parts[:, k, 0, :],
                                        start=False, stop=k == KC - 1, skip_group_check=True)
                    ins.then_inc(logits_ps, 1)
                pe.wait_ge(mask_ready, 1)
                pe.wait_ge(const_ready, 4)
                for dst, terms in ((slice(0, 8), ((before, 0),)), (slice(8, 16), ((ones, 0), (before, 1))),
                                   (slice(16, 24), ((ones, 0), (ones, 1)))):
                    for i, (left, t) in enumerate(terms):
                        ins = pe.matmul(bank[5][:, dst], left[:, :], mask[:, t, :], start=i == 0, stop=i == len(terms) - 1)
                ins.then_inc(place_ps, 1)

                def gather(g):
                    pe.wait_ge(pick_r_ready, 2 * g + 2)
                    for i, (src, k0, b) in enumerate(((hr_hi, 0, 6), (hr_hi, 4, 7), (hr_lo, 0, 3), (hr_lo, 4, 6))):
                        if i == 3:
                            pe.wait_ge(xg_act, 2 * g + 1)
                        for c in range(4):
                            for t in range(TT):
                                k = k0 + c
                                ins = pe.matmul(bank[b][:, P * c:P * c + P], src[:, t, P * k:P * k + P], pick_r[:, t, :],
                                                start=t == 0, stop=t == TT - 1)
                        ins.then_inc(gather_ps, 1)

                def up(n, cyc, b):
                    for hf in range(2):
                        pe.wait_ge(lo_ready, n + hf + 1 + RAW * cyc)
                        for c in range(4):
                            k = 4 * hf + c
                            whi, wlo = half_parts(n + hf, 4, c)
                            at = slice(P * k, P * k + P)
                            ins = product(pe, bank[b][:, :], xg_hi[:, at], xg_lo[:, at], whi, wlo, k == 0, k == KC - 1)
                        ins.then_inc(half_used, 1)

                def turn(b, m):
                    pe.wait_ge(e_rows, MSTEPS * b + m + 2)
                    for j in range(4):
                        ins = pe.transpose(bank[2][:, P * j:P * j + P], rows[:, P * j:P * j + P], ident[:, :])
                    ins.then_inc(e_turn, 1)

                def down(n, cyc, b, m):
                    pe.wait_ge(e_lo, MSTEPS * b + m + 2)
                    for i in range(2):
                        pe.wait_ge(lo_ready, n + i + 1 + RAW * cyc)
                        for j in range(2):
                            whi, wlo = half_parts(n + i, 2, j)
                            at = slice(P * (2 * i + j), P * (2 * i + j) + P)
                            for hf in range(2):
                                cols = slice(CHUNK * hf, CHUNK * (hf + 1))
                                ins = product(pe, bank[4 + hf][:, :], ffT_hi[:, at], ffT_lo[:, at],
                                              whi[:, cols], wlo[:, cols], False, False)
                        ins.then_inc(half_used, 1)

                def scatter(b, i):
                    t, hf = i // 2, i % 2
                    bk = (6, 7, 3, 6)[i]
                    if i == 3:
                        pe.wait_ge(x_add, 4 * b + 1)
                    cols = slice(CHUNK * hf, CHUNK * (hf + 1))
                    pe.matmul(bank[bk][:, :], spread_r[:, t, :], y_hi[:, cols], start=True, stop=False)
                    pe.matmul(bank[bk][:, :], spread_r[:, t, :], y_lo[:, cols], start=False,
                              stop=True).then_inc(scatter_ps, 1)

                def spread(b, opening):
                    if not opening:
                        pe.wait_ge(x_add, 4 * b + 2)
                    pe.wait_ge(pick_ready, 2 * b + 2)
                    for t in range(TT):
                        pe.transpose(bank[7][:, P * t:P * t + P], pick[:, t, :], ident[:, :])
                    for t in range(TT):
                        ins = pe.matmul(bank[7][:, SEQ:SEQ + 1], pick[:, t, :], seat[:, TT + t:TT + t + 1],
                                        start=t == 0, stop=t == TT - 1)
                    ins.then_inc(spread_ps, 1)

                pe.wait_ge(hr_lo_ready, 2)
                pe.wait_ge(moe_init, 1)
                def block(b, opening=False, closing=False):
                    c = CYCLES * b
                    pe.wait_ge(xg_act, 2 * b + 2)
                    pe.wait_ge(xg_dve, 2 * b + 2)
                    up(MOE0, c, 0)
                    up(MOE0 + 2, c, 1)
                    if opening:
                        pe.wait_ge(places_out, 1)
                    else:
                        pe.wait_ge(y_lo_ready, 2 * b)
                    for hf in range(2):
                        pe.matmul(bank[4 + hf][:, :], zero_r[:, 0:P], zero_r[:, :], start=True, stop=False,
                                  skip_group_check=True)
                    if not opening:
                        for i in range(3):
                            scatter(b, i)
                    turn(b, 0)
                    if not opening:
                        scatter(b, 3)
                    spread(b, opening)
                    with pe.Fori(1, MSTEPS) as m:
                        cm = c + m - 1
                        up(MOE0 + 4, cm, 0)
                        up(MOE0 + 6, cm, 1)
                        down(MOE0 + 8, cm, b, m - 1)
                        turn(b, m)
                    if not closing:
                        pe.wait_ge(spread_ready, 2 * b + 2)
                        if not opening:
                            pe.wait_ge(x_add, 4 * b + 4)
                        gather(b + 1)
                    down(MOE0 + BLOCK_HALVES - 2, c, b, MSTEPS - 1)

                gather(0)
                block(0, opening=True)
                pe.wait_ge(route_ready, 1)
                last = pe.value_load(ctl_i[0:1, 0:1], min_val=EXPERTS - 1, max_val=EXPERTS - 1 + SLOTS)
                with pe.Fori(1, last) as b:
                    block(b)
                block(last, closing=True)
                blocks = last + 1
                pe.wait_ge(y_lo_ready, 2 * blocks)
                pe.wait_ge(spread_ready, 2 * blocks)
                pe.wait_ge(x_add, 4 * blocks)
                for i in range(4):
                    scatter(blocks, i)

            pe.wait_ge(const_ready, 4)
            mixer(0)
            dense()
            mixer(1)
            experts()


def bucket_lines():
    import numpy as np
    dist = SEQ - 1 - np.arange(LINE)
    exact = NBUCKETS // 2
    d = np.maximum(dist, 1).astype(np.float32)
    large = exact + (np.log(d / np.float32(exact)) / np.float32(math.log(128 / exact))
                     * np.float32(NBUCKETS - exact)).astype(np.int32)
    bucket = np.where(dist < exact, dist, np.minimum(large, NBUCKETS - 1))
    bucket = np.where(dist < 0, NBUCKETS, bucket)
    return (np.arange(NBUCKETS + 1)[:, None] == bucket[None, :]).astype(np.float32)


_INS = ["x", "rel_bias", "mix_norm_g", "w_in", "lam_qk", "subln_g", "conv_w", "w_o_attn", "w_o_conv", "w_o",
        "ffn_norm_g", "dense_w_gate_up", "dense_w_down", "router_w", "expert_w_gate_up", "expert_w_down",
        "final_norm_g"]


def kernel(**inputs):
    import numpy as np
    import concourse.bacc as bacc
    from concourse.bass_utils import run_bass_kernel_spmd as run

    nc = bacc.Bacc("TRN2", target_bir_lowering=False, num_devices=1, dynamic_dma_scratch_size=1024)
    arrays, args = {}, []
    for name in _INS:
        arrays[f"in_{name}"] = np.ascontiguousarray(inputs[name])
        args.append(nc.dram_tensor(f"in_{name}", arrays[f"in_{name}"].shape, F32, kind="ExternalInput").ap())
    arrays["bucket_of"] = bucket_lines()
    args.append(nc.dram_tensor("bucket_of", arrays["bucket_of"].shape, F32, kind="ExternalInput").ap())
    out = nc.dram_tensor("out", (1, SEQ, D), F32, kind="ExternalOutput").ap()
    build(nc, *args, out)
    return run(nc, [arrays], core_ids=[0]).results[0]["out"]
```
